# Optimizing a Trainium2 kernel written in Bass

```python
import math
import jax, jax.numpy as jnp
from jax import lax
import numpy as np

D_MODEL = 1024
BATCH = 1
SEQ = 256
DEPTH = 2

N_MIXERS = 2
N_GDN_LAYERS = (DEPTH + 1) // 2
N_SB_LAYERS = DEPTH // 2

GDN_HEAD_DIM = 128
GDN_QK_HEADS = D_MODEL // 128
GDN_V_HEADS = 2 * GDN_QK_HEADS
GDN_KEY_DIM = GDN_QK_HEADS * GDN_HEAD_DIM
GDN_VAL_DIM = GDN_V_HEADS * GDN_HEAD_DIM
GDN_CONV_K = 4
GDN_CONV_DIM = 2 * GDN_KEY_DIM + GDN_VAL_DIM
GDN_IN_DIM = GDN_CONV_DIM + GDN_VAL_DIM + 2 * GDN_V_HEADS
GDN_CHUNK = 64

SB_HEAD_DIM = 128
SB_HEADS = D_MODEL // SB_HEAD_DIM
SB_DIM = SB_HEADS * SB_HEAD_DIM
SB_BLOCK = 128

FF_DIM = 7 * D_MODEL // 2
N_EXPERTS = 8
TOP_K = 2

DEEPNORM_ALPHA = (2.0 * DEPTH) ** 0.25
DEEPNORM_BETA = (8.0 * DEPTH) ** -0.25
LN_EPS = 1e-5
RMS_EPS = 1e-6

kernel_name = 'hybrid_gdn_stickbreak_moe_deepnorm'

def layer_norm(x, g, b):
    xf = x.astype(jnp.float32)
    mu = xf.mean(-1, keepdims=True)
    var = jnp.square(xf - mu).mean(-1, keepdims=True)
    y = (xf - mu) * lax.rsqrt(var + LN_EPS) * g.astype(jnp.float32) + b.astype(jnp.float32)
    return y.astype(x.dtype)

def l2norm(x):
    xf = x.astype(jnp.float32)
    return xf * lax.rsqrt(jnp.sum(xf * xf, -1, keepdims=True) + RMS_EPS)

def causal_short_conv(x, w):
    K = w.shape[0]
    S = x.shape[1]
    xp = jnp.pad(x, ((0, 0), (K - 1, 0), (0, 0)))
    y = w[0] * xp[:, 0:S]
    for j in range(1, K):
        y = y + w[j] * xp[:, j:j + S]
    return jax.nn.silu(y)

def chunk_gated_delta_rule(q, k, v, g, beta):
    B, H, S, dk = q.shape
    dv = v.shape[-1]
    C = GDN_CHUNK
    N = S // C
    q = q * (dk ** -0.5)
    qc = q.reshape(B, H, N, C, dk)
    kc = k.reshape(B, H, N, C, dk)
    vc = v.reshape(B, H, N, C, dv)
    bc = beta.reshape(B, H, N, C)
    gcum = jnp.cumsum(g.reshape(B, H, N, C), axis=-1)
    tri = jnp.tril(jnp.ones((C, C), dtype=bool))
    strict = jnp.tril(jnp.ones((C, C), dtype=bool), -1)
    diff = gcum[..., :, None] - gcum[..., None, :]
    decay = jnp.where(tri, jnp.exp(jnp.where(tri, diff, 0.0)), 0.0)
    kb = kc * bc[..., None]
    L = jnp.where(strict, jnp.einsum('bhnid,bhnjd->bhnij', kb, kc) * decay, 0.0)
    eye = jnp.eye(C, dtype=jnp.float32)
    T = lax.linalg.triangular_solve(eye + L, jnp.broadcast_to(eye, L.shape),
                                    left_side=True, lower=True, unit_diagonal=True)
    u = jnp.einsum('bhnij,bhnjd->bhnid', T, vc * bc[..., None])
    w = jnp.einsum('bhnij,bhnjd->bhnid', T, kb * jnp.exp(gcum)[..., None])
    intra = jnp.where(tri, jnp.einsum('bhnid,bhnjd->bhnij', qc, kc) * decay, 0.0)

    def step(state, inp):
        q_i, k_i, u_i, w_i, g_i, a_i = inp
        v_new = u_i - jnp.einsum('bhcd,bhde->bhce', w_i, state)
        o = (jnp.einsum('bhcd,bhde->bhce', q_i * jnp.exp(g_i)[..., None], state)
             + jnp.einsum('bhij,bhje->bhie', a_i, v_new))
        g_last = g_i[..., -1]
        k_dec = k_i * jnp.exp(g_last[..., None] - g_i)[..., None]
        state = state * jnp.exp(g_last)[..., None, None] + jnp.einsum('bhcd,bhce->bhde', k_dec, v_new)
        return state, o

    xs = (qc, kc, u, w, gcum, intra)
    xs = tuple(jnp.moveaxis(a, 2, 0) for a in xs)
    state0 = jnp.zeros((B, H, dk, dv), jnp.float32)
    _, o = lax.scan(step, state0, xs)
    return jnp.moveaxis(o, 0, 2).reshape(B, H, S, dv)

def gated_deltanet(x, w_in, conv_w, a_log, dt_bias, norm_w, w_out):
    B, S, _ = x.shape
    proj = x @ w_in
    o1 = GDN_CONV_DIM
    o2 = o1 + GDN_VAL_DIM
    o3 = o2 + GDN_V_HEADS
    qkv, z, b, a = proj[..., :o1], proj[..., o1:o2], proj[..., o2:o3], proj[..., o3:]
    qkv = causal_short_conv(qkv, conv_w)
    q = qkv[..., :GDN_KEY_DIM].reshape(B, S, GDN_QK_HEADS, GDN_HEAD_DIM)
    k = qkv[..., GDN_KEY_DIM:2 * GDN_KEY_DIM].reshape(B, S, GDN_QK_HEADS, GDN_HEAD_DIM)
    v = qkv[..., 2 * GDN_KEY_DIM:].reshape(B, S, GDN_V_HEADS, GDN_HEAD_DIM).astype(jnp.float32)
    rep = GDN_V_HEADS // GDN_QK_HEADS
    q = jnp.repeat(l2norm(q), rep, axis=2)
    k = jnp.repeat(l2norm(k), rep, axis=2)
    beta = jax.nn.sigmoid(b.astype(jnp.float32))
    g = -jnp.exp(a_log.astype(jnp.float32)) * jax.nn.softplus(a.astype(jnp.float32) + dt_bias.astype(jnp.float32))
    to_bhs = lambda t: jnp.swapaxes(t, 1, 2)
    o = chunk_gated_delta_rule(to_bhs(q), to_bhs(k), to_bhs(v), to_bhs(g), to_bhs(beta))
    o = jnp.swapaxes(o, 1, 2)
    o = o * lax.rsqrt(jnp.mean(o * o, -1, keepdims=True) + RMS_EPS) * norm_w.astype(jnp.float32)
    o = o * jax.nn.silu(z.reshape(B, S, GDN_V_HEADS, GDN_HEAD_DIM).astype(jnp.float32))
    return o.reshape(B, S, GDN_VAL_DIM).astype(x.dtype) @ w_out

def stick_breaking_attention(x, w_in, w_out):
    B, S, _ = x.shape
    proj = x @ w_in
    heads = lambda t: t.reshape(B, S, SB_HEADS, SB_HEAD_DIM).transpose(0, 2, 1, 3)
    q = heads(proj[..., :SB_DIM])
    k = heads(proj[..., SB_DIM:2 * SB_DIM])
    v = heads(proj[..., 2 * SB_DIM:])
    scale = SB_HEAD_DIM ** -0.5
    outs = []
    for i in range(S // SB_BLOCK):
        lo, hi = i * SB_BLOCK, (i + 1) * SB_BLOCK
        z = jnp.einsum('bhtd,bhsd->bhts', q[:, :, lo:hi], k[:, :, :hi]).astype(jnp.float32) * scale
        t_pos = lo + jnp.arange(SB_BLOCK)[:, None]
        s_pos = jnp.arange(hi)[None, :]
        causal = s_pos < t_pos
        log_keep = jnp.where(causal, jax.nn.log_sigmoid(-z), 0.0)
        later = lax.cumsum(log_keep, axis=3, reverse=True) - log_keep
        attn = jnp.where(causal, jnp.exp(jax.nn.log_sigmoid(z) + later), 0.0)
        outs.append(jnp.einsum('bhts,bhsd->bhtd', attn.astype(v.dtype), v[:, :, :hi]))
    o = jnp.concatenate(outs, axis=2)
    return o.transpose(0, 2, 1, 3).reshape(B, S, SB_DIM) @ w_out

def swiglu(x, w_gate, w_up, w_down):
    return (jax.nn.silu(x @ w_gate) * (x @ w_up)) @ w_down

def moe_swiglu(x, router, w_gate, w_up, w_down):
    B, S, D = x.shape
    xt = x.reshape(-1, D)
    logits = (xt @ router).astype(jnp.float32)
    top_val, top_idx = lax.top_k(logits, TOP_K)
    gates = jax.nn.softmax(top_val, axis=-1)
    combine = jnp.sum(jax.nn.one_hot(top_idx, N_EXPERTS, dtype=jnp.float32) * gates[..., None], axis=1)
    combine = combine.astype(x.dtype)
    y = jnp.zeros_like(xt)
    for e in range(N_EXPERTS):
        y = y + combine[:, e:e + 1] * swiglu(xt, w_gate[e], w_up[e], w_down[e])
    return y.reshape(B, S, D)

def setup_inputs(seed: int = 0) -> dict:
    key = jax.random.key(seed)
    ks = jax.random.split(key, 20)
    f32 = jnp.float32

    def nrm(k, shape, scale):
        return jax.random.normal(k, shape, f32) * scale

    x = nrm(ks[0], (BATCH, SEQ, D_MODEL), 1.0)
    gdn_cols = jnp.ones((GDN_IN_DIM,), f32).at[2 * GDN_KEY_DIM:GDN_CONV_DIM].set(DEEPNORM_BETA)
    gdn_w_in = nrm(ks[1], (N_GDN_LAYERS, D_MODEL, GDN_IN_DIM), D_MODEL ** -0.5) * gdn_cols
    gdn_conv_w = nrm(ks[2], (N_GDN_LAYERS, GDN_CONV_K, GDN_CONV_DIM), GDN_CONV_K ** -0.5)
    gdn_a_log = jnp.log(jax.random.uniform(ks[3], (N_GDN_LAYERS, GDN_V_HEADS), f32, 1.0, 16.0))
    dt = jnp.exp(jax.random.uniform(ks[4], (N_GDN_LAYERS, GDN_V_HEADS), f32, math.log(1e-3), math.log(1e-1)))
    gdn_dt_bias = dt + jnp.log(-jnp.expm1(-dt))
    gdn_norm_w = 1.0 + nrm(ks[5], (N_GDN_LAYERS, GDN_HEAD_DIM), 0.02)
    gdn_w_out = nrm(ks[6], (N_GDN_LAYERS, GDN_VAL_DIM, D_MODEL), GDN_VAL_DIM ** -0.5 * DEEPNORM_BETA)
    sb_cols = jnp.ones((3 * SB_DIM,), f32).at[2 * SB_DIM:].set(DEEPNORM_BETA)
    sb_w_in = nrm(ks[7], (N_SB_LAYERS, D_MODEL, 3 * SB_DIM), D_MODEL ** -0.5) * sb_cols
    sb_w_out = nrm(ks[8], (N_SB_LAYERS, SB_DIM, D_MODEL), SB_DIM ** -0.5 * DEEPNORM_BETA)
    ffn_w_gate = nrm(ks[9], (N_GDN_LAYERS, D_MODEL, FF_DIM), D_MODEL ** -0.5)
    ffn_w_up = nrm(ks[10], (N_GDN_LAYERS, D_MODEL, FF_DIM), D_MODEL ** -0.5)
    ffn_w_down = nrm(ks[11], (N_GDN_LAYERS, FF_DIM, D_MODEL), FF_DIM ** -0.5 * DEEPNORM_BETA)
    moe_router = nrm(ks[12], (N_SB_LAYERS, D_MODEL, N_EXPERTS), D_MODEL ** -0.5)
    moe_w_gate = nrm(ks[13], (N_SB_LAYERS, N_EXPERTS, D_MODEL, FF_DIM), D_MODEL ** -0.5)
    moe_w_up = nrm(ks[14], (N_SB_LAYERS, N_EXPERTS, D_MODEL, FF_DIM), D_MODEL ** -0.5)
    moe_w_down = nrm(ks[15], (N_SB_LAYERS, N_EXPERTS, FF_DIM, D_MODEL), FF_DIM ** -0.5 * DEEPNORM_BETA)
    ln_g = 1.0 + nrm(ks[16], (DEPTH, 2, D_MODEL), 0.02)
    ln_b = nrm(ks[17], (DEPTH, 2, D_MODEL), 0.02)
    return {'x': x, 'gdn_w_in': gdn_w_in, 'gdn_conv_w': gdn_conv_w, 'gdn_a_log': gdn_a_log,
            'gdn_dt_bias': gdn_dt_bias, 'gdn_norm_w': gdn_norm_w, 'gdn_w_out': gdn_w_out,
            'sb_w_in': sb_w_in, 'sb_w_out': sb_w_out,
            'ffn_w_gate': ffn_w_gate, 'ffn_w_up': ffn_w_up, 'ffn_w_down': ffn_w_down,
            'moe_router': moe_router, 'moe_w_gate': moe_w_gate, 'moe_w_up': moe_w_up,
            'moe_w_down': moe_w_down, 'ln_g': ln_g, 'ln_b': ln_b}

def reference(x, gdn_w_in, gdn_conv_w, gdn_a_log, gdn_dt_bias, gdn_norm_w, gdn_w_out,
              sb_w_in, sb_w_out, ffn_w_gate, ffn_w_up, ffn_w_down,
              moe_router, moe_w_gate, moe_w_up, moe_w_down, ln_g, ln_b):
    h = x
    for i in range(DEPTH):
        j = i // N_MIXERS
        if i % N_MIXERS == 0:
            mix = gated_deltanet(h, gdn_w_in[j], gdn_conv_w[j], gdn_a_log[j], gdn_dt_bias[j],
                                 gdn_norm_w[j], gdn_w_out[j])
        else:
            mix = stick_breaking_attention(h, sb_w_in[j], sb_w_out[j])
        h = layer_norm(DEEPNORM_ALPHA * h + mix, ln_g[i, 0], ln_b[i, 0])
        if i % 2 == 0:
            ff = swiglu(h, ffn_w_gate[j], ffn_w_up[j], ffn_w_down[j])
        else:
            ff = moe_swiglu(h, moe_router[j], moe_w_gate[j], moe_w_up[j], moe_w_down[j])
        h = layer_norm(DEEPNORM_ALPHA * h + ff, ln_g[i, 1], ln_b[i, 1])
    return h


_drawn_inputs = setup_inputs


def setup_inputs(seed=0):
    import zlib

    import numpy as np

    out = dict(_drawn_inputs(seed))
    spreads = {}
    factors = {'gdn_norm_w': 6.827}
    for name, (base, spread) in spreads.items():
        noise = np.random.default_rng([zlib.crc32(name.encode()), seed]).standard_normal(out[name].shape)
        drawn = base * np.exp(spread * noise) if base else spread * noise
        out[name] = __import__('jax').numpy.asarray(drawn.astype(out[name].dtype))
    for name, factor in factors.items():
        out[name] = (out[name] * factor).astype(out[name].dtype)
    return out
```

```python
from contextlib import ExitStack

import concourse.bass as bass
from concourse import mybir

ALU = mybir.AluOpType
ACT = mybir.ActivationFunctionType
AX_X = mybir.AxisListType.X
F32 = mybir.dt.float32
F32R = mybir.dt.float32r
I32 = mybir.dt.int32
ds = bass.ds

P = 128
SEQ = 256
NT = SEQ // P
D = 1024
KD = D // P
QK = 8
VH = 16
HPG = 4
QPG = HPG // 2
CONV_DIM = 4096
Z0 = CONV_DIM
BA0 = CONV_DIM + VH * P
FF = 3584
FC = FF // 512
NE = 8
TOPK = 2
SBH = 8
MAX_OVER = 3
ROUNDS = NE + MAX_OVER + 1
ALPHA = 4.0 ** 0.25
LN_EPS = 1e-5
RMS_EPS = 1e-6
SCALE = float(P) ** -0.5

RAW = 6
SPLIT = 3
CREDIT = 6
UNIT = 2048
A_UNITS = 24
OUT_UNITS = 8
FFN_UNITS = 6 * FC
SBIN_UNITS = 12
SBOUT_UNITS = 4
U_OUT = A_UNITS
U_FFN = U_OUT + OUT_UNITS
U_SBIN = U_FFN + FFN_UNITS
U_SBOUT = U_SBIN + SBIN_UNITS
U_MOE = U_SBOUT + SBOUT_UNITS

LEVELS = [1, 2, 4, 8, 16, 32, 64]
CST = 9 + len(LEVELS) + 5 + 3 * len(LEVELS)
SMALL = 16 * 6


class Stages:

    def __init__(self, sem, names, lead=False):
        self.sem = sem
        self.names = list(names)
        self.lead = len(self.names) if lead else 0
        assert len(set(self.names)) == len(self.names)

    def after(self, name, turn=0):
        return turn * len(self.names) + self.names.index(name) + 1 + self.lead


def hybrid_trunk(nc, x, gdn_w_in, gdn_conv_w, gdn_a_log, gdn_dt_bias, gdn_norm_w, gdn_w_out,
                 sb_w_in, sb_w_out, ffn_w_gate, ffn_w_up, ffn_w_down,
                 moe_router, moe_w_gate, moe_w_up, moe_w_down, ln_g, ln_b, out):
    with ExitStack() as ctx:
        def sb(name, shape, dt=F32, where=ctx):
            return where.enter_context(nc.sbuf_tensor(name, shape, dt))

        def sem(name):
            return ctx.enter_context(nc.semaphore(name))

        raw = sb("raw", [P, RAW, UNIT])
        w_hi = sb("w_hi", [P, SPLIT, UNIT], F32R)
        w_lo = sb("w_lo", [P, SPLIT, UNIT], F32R)
        X = sb("X", [P, NT, D])
        cst = sb("cst", [P, 7 + len(LEVELS), P])
        IDENT, LE, GT, LT, NGE, ONES, NONES = (cst[:, i, :] for i in range(7))
        LEVEL = {b: cst[:, 7 + i, :] for i, b in enumerate(LEVELS)}
        iota = sb("iota", [P, P])
        zeros = sb("zeros", [P, 512], F32R)
        bah = sb("bah", [P, KD, 32], F32R)
        bal = sb("bal", [P, KD, 32], F32R)
        rw = sb("rw", [P, KD, NE])
        rwh = sb("rwh", [P, KD, NE], F32R)
        rwl = sb("rwl", [P, KD, NE], F32R)
        stats = sb("stats", [P, NT, 2, 6])
        mv = sb("mv", [P, NT, 2])
        sdev = sb("sdev", [P, NT, 1])
        rstd = sb("rstd", [P, NT, 1])
        ps = ctx.enter_context(nc.psum_tensor("ps", [P, 8, 512], F32))

        gdn = ExitStack()
        tok = sb("tok", [P, 32, NT, P], F32, gdn)
        zs = sb("zs", [P, NT, VH * P], F32, gdn)
        kT = sb("kT", [P, QK, SEQ], F32, gdn)
        ba = sb("ba", [P, NT, 32], F32, gdn)
        gsb = {n: sb(n, [P, NT, VH], F32, gdn) for n in ("beta", "xdt", "axdt", "lsp", "g")}
        beta, xdt, axdt, lsp, g = gsb.values()
        negA = sb("negA", [P, VH], F32, gdn)
        dtb = sb("dtb", [P, VH], F32, gdn)
        eg1 = sb("eg1", [P, VH], F32, gdn)
        beg1 = sb("beg1", [P, VH], F32, gdn)
        kdec = sb("kdec", [P, VH], F32, gdn)
        ssq = sb("ssq", [P, 2 * QK, NT], F32, gdn)
        rsn = sb("rsn", [P, 2 * QK, NT], F32, gdn)
        cw = sb("cw", [P, P], F32, gdn)
        nw = sb("nw", [P, P], F32, gdn)

        pa = ExitStack()
        xT0h = sb("xT0h", [P, KD, SEQ], F32R, pa)
        xT0l = sb("xT0l", [P, KD, SEQ], F32R, pa)
        pre = sb("pre", [P, 2, NT, 512], F32, pa)
        cacc = sb("cacc", [P, 2, 4, SEQ], F32, pa)
        pa.close()
        pc = ExitStack()
        E_ = sb("E_", [P, NT, HPG, P], F32, pc)
        ET = sb("ET", [P, NT, HPG, P], F32, pc)
        XB = sb("XB", [P, NT, HPG, P], F32, pc)
        DB = sb("DB", [P, NT, HPG, P], F32, pc)
        DTB = sb("DTB", [P, NT, HPG, P], F32, pc)
        CB = sb("CB", [P, NT, HPG, P], F32, pc)
        kTc = sb("kTc", [P, QPG, SEQ], F32, pc)
        qTc = sb("qTc", [P, QPG, SEQ], F32, pc)
        pc.close()
        po = ExitStack()
        oTh = sb("oTh", [P, VH, SEQ], F32R, po)
        oTl = sb("oTl", [P, VH, SEQ], F32R, po)
        po.close()
        baw = tok[:, 0:1].rearrange("p a b c -> p (a b c)").rearrange("p (k n) -> p k n", n=32)
        cwr = tok[:, 1, 0, :]
        gdn.close()

        late = ctx
        lnrow = sb("lnrow", [P, 2, D], F32, late)
        xTh = sb("xTh", [P, KD, SEQ], F32R, late)
        xTl = sb("xTl", [P, KD, SEQ], F32R, late)
        fs = ExitStack()
        qkv = sb("qkv", [P, NT, 3 * D], F32, fs)
        qTs = sb("qTs", [P, 4, SEQ], F32, fs)
        kTs = sb("kTs", [P, 4, SEQ], F32, fs)
        att = sb("att", [P, 4, 384], F32, fs)
        spl = sb("spl", [P, 4, 384], F32, fs)
        aTh = sb("aTh", [P, SBH, SEQ], F32R, fs)
        aTl = sb("aTl", [P, SBH, SEQ], F32R, fs)
        fs.close()
        fd = ExitStack()
        hs0 = sb("hs0", [P, NT, 512], F32, fd)
        hTh0 = sb("hTh0", [P, NT, 4, P], F32R, fd)
        hTl0 = sb("hTl0", [P, NT, 4, P], F32R, fd)
        fd.close()
        fm = ExitStack()
        Xh = sb("Xh", [P, NT, D], F32R, fm)
        Xl = sb("Xl", [P, NT, D], F32R, fm)
        xeh = sb("xeh", [P, KD, P], F32R, fm)
        xel = sb("xel", [P, KD, P], F32R, fm)
        Yh = sb("Yh", [P, D], F32R, fm)
        Yl = sb("Yl", [P, D], F32R, fm)
        hs1 = sb("hs1", [P, 1, 512], F32, fm)
        hTh1 = sb("hTh1", [P, 1, 4, P], F32R, fm)
        hTl1 = sb("hTl1", [P, 1, 4, P], F32R, fm)
        G = sb("G", [P, NT, P], F32R, fm)
        GTr = sb("GTr", [P, SEQ], F32R, fm)
        rt = {n: sb("rt_" + n, [P, NT, NE], F32, fm) for n in
              ("lg", "eq1", "ca", "oh1", "l2", "eq2", "oh2", "mask", "comb", "rank", "c2", "tmp")}
        rs = {n: sb("rs_" + n, [P, NT, 1], F32, fm) for n in
              ("m1", "i1", "m2", "i2", "df", "ex", "sm", "p1", "p2")}
        cnt = sb("cnt", [P, NE], F32, fm)
        ov = sb("ov", [P, NE], F32, fm)
        ovp = sb("ovp", [P, NE], F32, fm)
        ind = sb("ind", [P, MAX_OVER, NE], F32, fm)
        ranks = sb("ranks", [P, NT, ROUNDS], F32, fm)
        gates = sb("gates", [P, NT, ROUNDS], F32, fm)
        ids = sb("ids", [P, 4], F32, fm)
        idi = sb("idi", [P, 4], I32, fm)
        fm.close()

        raw_in = [sem(f"raw_in{i}") for i in range(RAW)]
        hi_done = sem("hi_done")
        lo_done = sem("lo_done")
        unit_used = sem("unit_used")
        x_in = sem("x_in")
        small_in = sem("small_in")
        cst_step = sem("cst_step")
        ln_in = sem("ln_in")
        out_done = sem("out_done")
        xt_pe, xt_hi, xt_lo = sem("xt_pe"), sem("xt_hi"), sem("xt_lo")
        A_pe = Stages(sem("A_pe"), ["t1A", "t1B", "t2A", "t2B"])
        A_act = Stages(sem("A_act"), ["preA", "preB", "siluA", "siluB", "z", "tokA", "tokB"], True)
        A_dve = Stages(sem("A_dve"), [f"{j}{m}{c}" for c in "AB" for j in (3, 2, 1, 0) for m in range(4)])
        S_pe = Stages(sem("S_pe"), ["cw", "ba", "gc", "gl", "qT0", "qT1", "qT2", "qT3", "kT0", "kT1", "kT2", "kT3"])
        S_act = Stages(sem("S_act"), ["bah", "eb", "ax", "ex", "ea", "ln", "eg", "kd", "sq", "sd",
                                      "qT0", "qT1", "qT2", "qT3"])
        S_dve = Stages(sem("S_dve"), ["cw", "bal", "ba", "xdt", "b1", "b2", "sp", "g", "beg", "sq",
                                      "rs", "rq", "kn", "kT0", "kT1", "kT2", "kT3"])
        S_pool = Stages(sem("S_pool"), ["zn0", "zn1", "vb", "qn"])
        inv = LEVELS[1:]
        C_pool = Stages(sem("C_pool"), ["cq", "ck"] + [f"{n}.{t}" for t in range(NT) for n in ("G", "MB")]
                        + [f"C{b}.{t}" for b in LEVELS for t in range(NT)] + ["kd"])
        C_pe = Stages(sem("C_pe"), [f"{n}.{t}" for t in range(NT) for n in ("kk", "df", "dT")]
                      + [f"T1.{t}" for t in range(NT)]
                      + [f"{n}{b}.{t}" for b in inv for n in ("X", "U", "T") for t in range(NT) if b < 64 or n != "T"]
                      + ["v0", "S", "O0", "PK", "PQ", "v1", "AV"], True)
        C_act = Stages(sem("C_act"), [f"{n}.{t}" for t in range(NT) for n in ("e", "eT")]
                       + [f"{n}{b}.{t}" for b in inv for n in ("x", "d") for t in range(NT) if b < 64 or n != "d"]
                       + ["v0s", "Ss", "v1s"], True)
        C_dve = Stages(sem("C_dve"), [f"{n}.{t}" for t in range(NT) for n in ("L1", "L", "A1", "A")]
                       + [f"{n}.{t}" for t in range(NT) for n in ("d1", "dt1")]
                       + [f"u{b}.{t}" for b in inv for t in range(NT)] + ["o0", "r1", "r", "o1a", "o1"], True)
        O_pe, O_act, O_dve, O_pool = (Stages(sem(n), s) for n, s in (
            ("O_pe", [f"t{q}" for q in range(8)]),
            ("O_act", ["sq", "sd"] + [f"h{q}" for q in range(8)]),
            ("O_dve", ["sq", "rs", "n", "z"] + [f"l{q}" for q in range(8)]),
            ("O_pool", ["n", "z"])))
        ln_dve = [Stages(sem(f"ln_dve{k}"), [f"{n}{t}" for t in range(NT) for n in ("r", "sa", "sb", "ag") if n != "r" or k < 3]
                         + [f"{n}{t}" for t in range(NT) for n in ("rc", "n", "g", "b")]) for k in range(4)]
        ln_act = [Stages(sem(f"ln_act{k}"), ["sd0", "sd1"]) for k in range(4)]
        names = ("t", "s", "hh", "h", "hl")
        dense = {n: sem("dense_" + n) for n in names}
        moe = {n: sem("moe_" + n) for n in names}
        B_act = Stages(sem("B_act"), ["c0", "c1", "c2"], True)
        T_pe = Stages(sem("T_pe"), ["q", "k", "z", "R", "o"])
        T_act = Stages(sem("T_act"), ["q", "a", "e", "l", "p", "oh"])
        T_dve = Stages(sem("T_dve"), ["k", "sp", "m0", "m1", "mn", "n0", "n1", "ol"])
        R_pe = Stages(sem("R_pe"), ["lg", "rk"])
        R_act = Stages(sem("R_act"), ["rwh", "ex", "xh"])
        R_dve = Stages(sem("R_dve"), ["rwl", "lg", "m1", "eq1", "ca", "i1", "oh1", "l2", "m2", "eq2", "c2", "i2", "oh2",
                                      "df", "sm", "p1", "p2", "mask", "cm1", "cm2", "comb", "rk1", "rk2",
                                      "cnt", "ov", "z0", "z1", "z2"] + [f"pre{e}" for e in range(1, NE)]
                       + [n + str(q) for q in range(MAX_OVER)
                          for n in ("in", "im", "pr", "sr", "ad", "pg", "sg", "pi", "si")]
                       + ["rt", "gt", "no", "nc", "ni", "xl", "xa"])
        K_pe = Stages(sem("K_pe"), ["hi", "lo", "tr"])
        K_act = Stages(sem("K_act"), ["hi", "gt"])
        K_dve = Stages(sem("K_dve"), ["s0", "s1", "l7", "l0"])
        yh_done, yl_done, scattered, added = sem("yh_done"), sem("yl_done"), sem("scattered"), sem("added")

        def cols(w, half, c0):
            return w[half * 512:(half + 1) * 512, ds(c0, 512)].rearrange("(k p) n -> p k n", p=P)

        def rows(w, r0):
            return w[ds(r0, 256), :].rearrange("(k p) n -> p k n", p=P)

        def unit_hi(j):
            return w_hi[:, j % SPLIT, :]

        def unit_lo(j):
            return w_lo[:, j % SPLIT, :]

        def units(j, turn=0):
            return j + 6 * turn + 1 + CREDIT

        block = ctx.enter_context(nc.Block())

        @block.sync
        def _(sp):
            def load(j, turn, src, k):
                sp.wait_ge(lo_done, units(j - RAW, turn))
                sp.dma_start(raw[:, j % RAW, :].rearrange("p (k n) -> p k n", k=k), src)\
                  .then_inc(raw_in[j % RAW], 16)

            sp.dma_start(X[:], x[0].rearrange("(t p) d -> p t d", p=P)).then_inc(x_in, 16)
            with sp.Fori(0, 4) as i:
                for c, c0 in enumerate((i * 1024, i * 1024 + 512, i * 512 + Z0)):
                    for half in range(2):
                        load(2 * c + half, i, cols(gdn_w_in[0], half, c0), 4)
            for u in range(OUT_UNITS):
                load(U_OUT + u, 0, rows(gdn_w_out[0], u * 256), 2)

            def ffn(base, turn, wg, wu, wd):
                for k, w in enumerate((wg, wu)):
                    for half in range(2):
                        load(base + 2 * k + half, turn, cols(w, half, 0), 4)
                with sp.Fori(0, FC - 1) as c:
                    for k, w in enumerate((wg, wu)):
                        for half in range(2):
                            load(base + 4 + 2 * k + half, turn + c, cols(w, half, (c + 1) * 512), 4)
                    for half in range(2):
                        load(base + 8 + half, turn + c, rows(wd, c * 512 + half * 256), 2)
                for half in range(2):
                    load(base + 4 + half, turn + FC - 1, rows(wd, (FC - 1) * 512 + half * 256), 2)

            ffn(U_FFN, 0, ffn_w_gate[0], ffn_w_up[0], ffn_w_down[0])
            with sp.Fori(0, 2) as i:
                for c in range(3):
                    for half in range(2):
                        load(U_SBIN + 2 * c + half, i, cols(sb_w_in[0], half, i * 1536 + c * 512), 4)
            for u in range(SBOUT_UNITS):
                load(U_SBOUT + u, 0, rows(sb_w_out[0], u * 256), 2)

            wg_all = moe_w_gate[0].rearrange("e k n -> (e k) n")
            wu_all = moe_w_up[0].rearrange("e k n -> (e k) n")
            wd_all = moe_w_down[0].rearrange("e k n -> (e k) n")

            def expert(turn, e):
                ffn(U_MOE, turn, wg_all[ds(e * D, D), :], wu_all[ds(e * D, D), :], wd_all[ds(e * FF, FF), :])

            with sp.Fori(0, NE) as e:
                expert(FC * e, e)
            sp.wait_ge(R_dve.sem, R_dve.after("ni"))
            n = sp.value_load(idi[0:1, 0:1], min_val=NE, max_val=NE + MAX_OVER)
            with sp.If(n > NE):
                with sp.Fori(NE, n) as r:
                    e = sp.value_load(idi[0:1, ds(r - (NE - 1), 1)], min_val=0, max_val=NE - 1)
                    expert(FC * r, e)
            for half in range(2):
                load(U_MOE + half, FC * n, cols(wg_all, half, 0), 4)
            sp.wait_ge(ln_dve[3].sem, ln_dve[3].after("b1"))
            sp.dma_start(out[0].rearrange("(t p) d -> p t d", p=P), X[:]).then_inc(out_done, 16)
            sp.wait_ge(out_done, 16)

        @block.gpsimd
        def _(pool):
            for ap, v in ((IDENT, 0.0), (LE, 1.0), (GT, 1.0), (LT, 1.0), (NGE, -1.0), (ONES, 1.0), (NONES, -1.0),
                          *((LEVEL[b], 1.0) for b in LEVELS)):
                nc.gpsimd.memset(ap, v).then_inc(cst_step, 1)
            nc.gpsimd.memset(zeros[:].bitcast(F32), 0.0).then_inc(cst_step, 1)
            n = 8 + len(LEVELS)
            nc.gpsimd.iota(iota[:], pattern=[[1, P]], base=0, channel_multiplier=0,
                           allow_small_or_imprecise_dtypes=True).then_inc(cst_step, 1)
            n += 1
            pool.wait_ge(cst_step, n)

            def cut(ap, pattern, base, cm, op, fill=0.0):
                nc.gpsimd.affine_select(out=ap, in_=ap, compare_op=op, fill=fill, base=base, pattern=pattern,
                                        channel_multiplier=cm).then_inc(cst_step, 1)

            cut(IDENT, [[-1, P]], 0, 1, ALU.not_equal, 1.0)
            cut(LE, [[1, P]], 0, -1, ALU.is_ge)
            cut(GT, [[-1, P]], 0, 1, ALU.is_gt)
            cut(LT, [[1, P]], 0, -1, ALU.is_gt)
            cut(NGE, [[-1, P]], 0, 1, ALU.is_ge)
            n += 5
            for b in LEVELS:
                v = LEVEL[b].rearrange("p (n h b) -> p n h b", h=2, b=b)
                nc.gpsimd.memset(v[:, :, 1, :], 0.0).then_inc(cst_step, 1)
                cut(v[:, :, 0, :], [[-2 * b, P // (2 * b)], [0, b]], -b, 1, ALU.is_ge)
                n += 2
            pool.wait_ge(cst_step, n)
            for b in LEVELS:
                v = LEVEL[b].rearrange("p (n h b) -> p n h b", h=2, b=b)
                cut(v[:, :, 0, :], [[2 * b, P // (2 * b)], [0, b]], 2 * b - 1, -1, ALU.is_ge)
                n += 1
            assert n == CST
            pool.wait_ge(cst_step, CST)

            pool.wait_ge(A_act.sem, A_act.after("z", 3))
            pool.wait_ge(small_in, SMALL)
            for t in range(NT):
                zv = zs[:, t, :].rearrange("p (h d) -> p h d", d=P)
                nc.gpsimd.tensor_tensor(zv, zv, nw[:].unsqueeze(1).broadcast_to([P, VH, P]), ALU.mult)\
                  .then_inc(S_pool.sem, 1)
            pool.wait_ge(S_dve.sem, S_dve.after("b2"))
            pool.wait_ge(A_act.sem, A_act.after("tokB", 3))
            v = tok[:, 16:32]
            nc.gpsimd.tensor_tensor(v, v, beta[:].rearrange("p t h -> p h t").unsqueeze(3).broadcast_to([P, VH, NT, P]),
                                    ALU.mult).then_inc(S_pool.sem, 1)
            pool.wait_ge(S_dve.sem, S_dve.after("rq"))
            pool.wait_ge(S_act.sem, S_act.after("sq"))
            q = tok[:, 0:QK]
            nc.gpsimd.tensor_tensor(q, q, rsn[:, 0:QK].unsqueeze(3).broadcast_to([P, QK, NT, P]), ALU.mult)\
              .then_inc(S_pool.sem, 1)

            pool.wait_ge(S_dve.sem, S_dve.after("kT3"))
            pool.wait_ge(S_act.sem, S_act.after("qT3"))
            with pool.Fori(0, VH // HPG) as i:
                pool.wait_ge(C_pe.sem, C_pe.after("AV", i - 1))
                nc.gpsimd.tensor_copy(qTc[:], tok[:, ds(QPG * i, QPG)].rearrange("p h t d -> p h (t d)"))\
                  .then_inc(C_pool.sem, 1)
                nc.gpsimd.tensor_copy(kTc[:], kT[:, ds(QPG * i, QPG), :]).then_inc(C_pool.sem, 1)
                for t in range(NT):
                    nc.gpsimd.tensor_tensor(XB[:, t], LE.unsqueeze(1).broadcast_to([P, HPG, P]),
                                            g[:, t, ds(HPG * i, HPG)].unsqueeze(2).broadcast_to([P, HPG, P]),
                                            ALU.mult).then_inc(C_pool.sem, 1)
                    nc.gpsimd.tensor_tensor(DB[:, t], GT.unsqueeze(1).broadcast_to([P, HPG, P]),
                                            beta[:, t, ds(HPG * i, HPG)].unsqueeze(2).broadcast_to([P, HPG, P]),
                                            ALU.mult).then_inc(C_pool.sem, 1)
                for b in LEVELS:
                    for t in range(NT):
                        if b == 1:
                            pool.wait_ge(C_dve.sem, C_dve.after(f"L.{t}", i))
                        elif b == 2:
                            pool.wait_ge(C_dve.sem, C_dve.after(f"d1.{t}", i))
                            pool.wait_ge(C_pe.sem, C_pe.after(f"T1.{t}", i))
                        else:
                            pool.wait_ge(C_pe.sem, C_pe.after(f"X{b // 2}.{t}", i))
                        nc.gpsimd.tensor_tensor(CB[:, t], E_[:, t], LEVEL[b].unsqueeze(1).broadcast_to([P, HPG, P]),
                                                ALU.mult).then_inc(C_pool.sem, 1)
                pool.wait_ge(C_pe.sem, C_pe.after("U64.0", i))
                kq = tok[:, ds(QK + QPG * i, QPG), 0, :]
                nc.gpsimd.tensor_tensor(DB[:, 0].rearrange("p (q r) d -> p q r d", r=2),
                                        kq.unsqueeze(2).broadcast_to([P, QPG, 2, P]),
                                        kdec[:, ds(HPG * i, HPG)].rearrange("p (q r) -> p q r", r=2).unsqueeze(3)
                                        .broadcast_to([P, QPG, 2, P]), ALU.mult).then_inc(C_pool.sem, 1)

            pool.wait_ge(O_dve.sem, O_dve.after("rs"))
            o1 = tok[:, 16:32, 1, :]
            nc.gpsimd.tensor_tensor(o1, o1, rsn[:, :, 1].unsqueeze(2).broadcast_to([P, VH, P]), ALU.mult)\
              .then_inc(O_pool.sem, 1)
            pool.wait_ge(O_pool.sem, O_pool.after("n"))
            nc.gpsimd.tensor_tensor(o1, o1, zs[:, 1, :].rearrange("p (h d) -> p h d", d=P), ALU.mult)\
              .then_inc(O_pool.sem, 1)
        @block.scalar
        def _(act):
            act.sem_inc(A_act.sem, A_act.lead)
            act.sem_inc(B_act.sem, B_act.lead)
            act.sem_inc(C_act.sem, C_act.lead)
            for S in (dense, moe):
                act.sem_inc(S["s"], 1)
                act.sem_inc(S["hh"], 1)
            act.dma_start(baw, gdn_w_in[0, :, BA0:BA0 + 32].rearrange("(k p) n -> p k n", p=P)).then_inc(small_in, 16)
            act.dma_start(cwr, gdn_conv_w[0].rearrange("j (c p) -> (j c) p", p=P)).then_inc(small_in, 16)
            act.dma_start(dtb[:], gdn_dt_bias[0].partition_broadcast(P)).then_inc(small_in, 16)
            act.dma_start(negA[:], gdn_a_log[0].partition_broadcast(P)).then_inc(small_in, 16)
            act.dma_start(nw[:], gdn_norm_w[0].partition_broadcast(P)).then_inc(small_in, 16)
            act.dma_start(rw[:], moe_router[0].rearrange("(k p) n -> p k n", p=P)).then_inc(small_in, 16)

            def hi(j, turn=0):
                act.wait_ge(raw_in[j % RAW], 16 * (turn + j // RAW + 1))
                act.wait_ge(unit_used, units(j - SPLIT, turn))
                nc.scalar.activation(unit_hi(j), raw[:, j % RAW, :], ACT.Copy).then_inc(hi_done, 1)

            def transposed(k, th, bank):
                for q in range(4):
                    act.wait_ge(xt_pe, 4 * k + q + 1)
                    nc.scalar.activation(th[:, 2 * q:2 * q + 2, :].rearrange("p a b -> p (a b)"), ps[:, bank + q, :],
                                         ACT.Copy).then_inc(xt_hi, 1)

            def layer_norm(k):
                for t in range(NT):
                    act.wait_ge(ln_dve[k].sem, ln_dve[k].after(f"ag{t}"))
                    nc.scalar.activation(sdev[:, t], mv[:, t, 1:2], ACT.Sqrt, bias=LN_EPS).then_inc(ln_act[k].sem, 1)

            def load_ln(k):
                act.dma_start(lnrow[:, 0, :], ln_g[k // 2, k % 2].partition_broadcast(P)).then_inc(ln_in, 16)
                act.dma_start(lnrow[:, 1, :], ln_b[k // 2, k % 2].partition_broadcast(P)).then_inc(ln_in, 16)

            act.wait_ge(small_in, SMALL)
            nc.scalar.activation(bah[:], baw, ACT.Copy).then_inc(S_act.sem, 1)
            nc.scalar.activation(rwh[:], rw[:], ACT.Copy).then_inc(R_act.sem, 1)
            transposed(0, xT0h, 0)

            hi(0)
            hi(1)
            with act.Fori(0, 4) as i:
                hi(2, i)
                hi(3, i)
                act.wait_ge(unit_used, units(1, i))
                nc.scalar.activation(pre[:, 0], ps[:, 0:2, :], ACT.Copy).then_inc(A_act.sem, 1)
                hi(4, i)
                act.wait_ge(unit_used, units(3, i))
                nc.scalar.activation(pre[:, 1], ps[:, 2:4, :], ACT.Copy).then_inc(A_act.sem, 1)
                hi(5, i)
                act.wait_ge(A_dve.sem, A_dve.after("03A", i))
                nc.scalar.activation(cacc[:, 0], cacc[:, 0], ACT.Silu).then_inc(A_act.sem, 1)
                hi(6, i)
                act.wait_ge(A_dve.sem, A_dve.after("03B", i))
                nc.scalar.activation(cacc[:, 1], cacc[:, 1], ACT.Silu).then_inc(A_act.sem, 1)
                act.wait_ge(unit_used, units(5, i))
                nc.scalar.activation(zs[:, :, ds(i * 512, 512)], ps[:, 0:2, :], ACT.Silu).then_inc(A_act.sem, 1)
                hi(7, i)
                for c, bank in ((0, 2), (1, 4)):
                    act.wait_ge(A_pe.sem, A_pe.after("t2" + "AB"[c], i))
                    nc.scalar.activation(tok[:, ds(i * 8 + 4 * c, 4), :, :],
                                         ps[:, bank:bank + 2, :].rearrange("p t (m d) -> p m t d", d=P),
                                         ACT.Copy).then_inc(A_act.sem, 1)

            act.wait_ge(S_dve.sem, S_dve.after("ba"))
            nc.scalar.activation(beta[:], ba[:, :, 0:VH], ACT.Exp, scale=-1.0).then_inc(S_act.sem, 1)
            act.wait_ge(S_dve.sem, S_dve.after("xdt"))
            nc.scalar.activation(axdt[:], xdt[:], ACT.Abs).then_inc(S_act.sem, 1)
            act.wait_ge(S_act.sem, S_act.after("ax"))
            nc.scalar.activation(axdt[:], axdt[:], ACT.Exp, scale=-1.0).then_inc(S_act.sem, 1)
            nc.scalar.activation(negA[:], negA[:], ACT.Exp).then_inc(S_act.sem, 1)
            act.wait_ge(S_act.sem, S_act.after("ex"))
            nc.scalar.activation(lsp[:], axdt[:], ACT.Ln, bias=1.0).then_inc(S_act.sem, 1)
            act.wait_ge(S_pe.sem, S_pe.after("gl"))
            nc.scalar.activation(eg1[:], ps[:, 0, 0:VH], ACT.Exp).then_inc(S_act.sem, 1)
            nc.scalar.activation(kdec[:], ps[:, 0, VH:2 * VH], ACT.Exp).then_inc(S_act.sem, 1)
            act.wait_ge(A_act.sem, A_act.after("tokB", 3))
            act.wait_ge(A_pe.sem, A_pe.after("t1B", 3))
            for h in range(QK):
                for t in range(NT):
                    last = nc.scalar.activation(pre[:, h // 4, (h // 2) % 2, (h % 2) * 256 + t * P:(h % 2) * 256 + t * P + P],
                                                tok[:, h, t, :], ACT.Square, accum_out=ssq[:, h, t:t + 1])
            last.then_inc(S_act.sem, 1)
            act.wait_ge(S_act.sem, S_act.after("sq"))
            act.wait_ge(S_dve.sem, S_dve.after("sq"))
            nc.scalar.activation(rsn[:], ssq[:], ACT.Sqrt, bias=RMS_EPS).then_inc(S_act.sem, 1)
            act.wait_ge(S_pe.sem, S_pe.after("qT3"))
            for q in range(4):
                nc.scalar.activation(tok[:, 2 * q:2 * q + 2].rearrange("p h t d -> p (h t d)"), ps[:, q, :],
                                     ACT.Copy).then_inc(S_act.sem, 1)

            with act.Fori(0, VH // HPG) as i:
                for t in range(NT):
                    act.wait_ge(C_pe.sem, C_pe.after(f"df.{t}", i))
                    nc.scalar.activation(E_[:, t].rearrange("p h d -> p (h d)"), ps[:, 2 + t, :], ACT.Exp)\
                      .then_inc(C_act.sem, 1)
                    act.wait_ge(C_pe.sem, C_pe.after(f"dT.{t}", i))
                    nc.scalar.activation(ET[:, t].rearrange("p h d -> p (h d)"), ps[:, 4 + t, :], ACT.Exp)\
                      .then_inc(C_act.sem, 1)
                for b in inv:
                    for t in range(NT):
                        act.wait_ge(C_pe.sem, C_pe.after(f"X{b}.{t}", i))
                        nc.scalar.activation(XB[:, t].rearrange("p h d -> p (h d)"), ps[:, 2 + t, :], ACT.Copy)\
                          .then_inc(C_act.sem, 1)
                    for t in range(NT):
                        if b < 64:
                            act.wait_ge(C_pe.sem, C_pe.after(f"T{b}.{t}", i))
                            nc.scalar.activation(DB[:, t].rearrange("p h d -> p (h d)"), ps[:, 6 + t, :], ACT.Copy)\
                              .then_inc(C_act.sem, 1)
                act.wait_ge(C_pe.sem, C_pe.after("v0", i))
                nc.scalar.activation(XB[:, 0].rearrange("p h d -> p (h d)"), ps[:, 0, :], ACT.Copy).then_inc(C_act.sem, 1)
                act.wait_ge(C_pe.sem, C_pe.after("S", i))
                nc.scalar.activation(CB[:, 0].rearrange("p h d -> p (h d)"), ps[:, 1, :], ACT.Copy).then_inc(C_act.sem, 1)
                act.wait_ge(C_pe.sem, C_pe.after("v1", i))
                nc.scalar.activation(XB[:, 1].rearrange("p h d -> p (h d)"), ps[:, 4, :], ACT.Copy).then_inc(C_act.sem, 1)

            act.wait_ge(C_dve.sem, C_dve.after("o1", 3))
            act.wait_ge(C_pe.sem, C_pe.after("AV", 3))
            for h in range(VH):
                last = nc.scalar.activation((XB, DB)[h // 8][:, (h // 4) % 2, h % 4, :], tok[:, 16 + h, 1, :], ACT.Square,
                                            accum_out=ssq[:, h, 1:2])
            last.then_inc(O_act.sem, 1)
            act.wait_ge(O_act.sem, O_act.after("sq"))
            act.wait_ge(O_dve.sem, O_dve.after("sq"))
            nc.scalar.activation(rsn[:], ssq[:], ACT.Sqrt, scale=1.0 / P, bias=RMS_EPS).then_inc(O_act.sem, 1)
            for q in range(8):
                act.wait_ge(O_pe.sem, O_pe.after(f"t{q}"))
                nc.scalar.activation(oTh[:, 2 * q:2 * q + 2, :].rearrange("p a b -> p (a b)"), ps[:, q, :], ACT.Copy)\
                  .then_inc(O_act.sem, 1)
            act.wait_ge(O_pe.sem, O_pe.after("t7"))
            load_ln(0)
            for u in range(OUT_UNITS):
                hi(U_OUT + 2 + u)
            layer_norm(0)

            def ffn(base, turn, S, done, tiles, g_bank, t_bank, hs, hTh):
                def silu(n, gate):
                    act.wait_ge(unit_used, gate)
                    act.wait_ge(S["t"], n + 1)
                    nc.scalar.activation(hs[:], ps[:, g_bank:g_bank + tiles, :], ACT.Silu).then_inc(S["s"], 1)

                def hidden(n):
                    act.wait_ge(S["t"], n + 2)
                    nc.scalar.activation(hTh[:].rearrange("p t m d -> p t (m d)"), ps[:, t_bank:t_bank + tiles, :],
                                         ACT.Copy).then_inc(S["hh"], 1)

                hi(base + 2, turn)
                hi(base + 3, turn)
                silu(done, units(base + 1, turn))
                hi(base + 4, turn)
                hi(base + 5, turn)
                hidden(done)
                with act.Fori(0, FC - 1) as c:
                    hi(base + 6, turn + c)
                    hi(base + 7, turn + c)
                    hi(base + 8, turn + c)
                    silu(done + c + 1, units(base + 5, turn + c))
                    hi(base + 9, turn + c)
                    hi(base + 10, turn + c)
                    hi(base + 11, turn + c)
                    hidden(done + c + 1)
                return turn + FC - 1

            transposed(1, xTh, 4)
            act.wait_ge(ln_dve[0].sem, ln_dve[0].after("b1"))
            load_ln(1)
            end = ffn(U_FFN, 0, dense, 0, NT, 0, 2, hs0, hTh0)
            hi(U_FFN + 6, end)
            hi(U_FFN + 7, end)
            layer_norm(1)

            transposed(2, xTh, 0)
            act.wait_ge(ln_dve[1].sem, ln_dve[1].after("b1"))
            load_ln(2)
            with act.Fori(0, 2) as i:
                for c, (bank, ahead) in enumerate(((4, (2, 3)), (6, (4,)), (0, (5, 6)))):
                    for j in ahead:
                        hi(U_SBIN + j, i)
                    act.wait_ge(unit_used, units(U_SBIN + 2 * c + 1, i))
                    nc.scalar.activation(qkv[:, :, ds(i * 1536 + c * 512, 512)], ps[:, bank:bank + 2, :], ACT.Copy)\
                      .then_inc(B_act.sem, 1)
                hi(U_SBIN + 7, i)

            for grp in range(2):
                act.wait_ge(T_pe.sem, T_pe.after("q", grp))
                nc.scalar.activation(qTs[:], ps[:, 0:4, 0:SEQ], ACT.Copy, scale=SCALE).then_inc(T_act.sem, 1)
                act.wait_ge(T_pe.sem, T_pe.after("z", grp))
                nc.scalar.activation(spl[:], ps[:, 0:4, 0:384], ACT.Abs).then_inc(T_act.sem, 1)
                act.wait_ge(T_act.sem, T_act.after("a", grp))
                nc.scalar.activation(spl[:], spl[:], ACT.Exp, scale=-1.0).then_inc(T_act.sem, 1)
                act.wait_ge(T_act.sem, T_act.after("e", grp))
                nc.scalar.activation(spl[:], spl[:], ACT.Ln, bias=1.0).then_inc(T_act.sem, 1)
                act.wait_ge(T_dve.sem, T_dve.after("mn", grp))
                nc.scalar.activation(att[:], att[:], ACT.Exp).then_inc(T_act.sem, 1)
                act.wait_ge(T_pe.sem, T_pe.after("o", grp))
                nc.scalar.activation(aTh[:, 4 * grp:4 * grp + 4, :], ps[:, 4:8, 0:SEQ], ACT.Copy).then_inc(T_act.sem, 1)
            for u in range(SBOUT_UNITS):
                hi(U_SBOUT + 2 + u)
            layer_norm(2)

            transposed(3, xTh, 4)
            act.wait_ge(ln_dve[2].sem, ln_dve[2].after("b1"))
            load_ln(3)
            act.wait_ge(R_dve.sem, R_dve.after("df"))
            nc.scalar.activation(rs["ex"][:], rs["df"][:], ACT.Exp).then_inc(R_act.sem, 1)
            nc.scalar.activation(Xh[:], X[:], ACT.Copy).then_inc(R_act.sem, 1)

            def gathered(r):
                act.wait_ge(K_pe.sem, K_pe.after("hi", r))
                nc.scalar.activation(xeh[:].rearrange("p k s -> p (k s)"), ps[:, 5:7, :].rearrange("p b n -> p (b n)"),
                                     ACT.Copy).then_inc(K_act.sem, 1)

            def slots(r):
                act.wait_ge(K_pe.sem, K_pe.after("tr", r))
                nc.scalar.activation(GTr[:], ps[:, 1, 0:SEQ], ACT.Copy).then_inc(K_act.sem, 1)

            gathered(0)
            slots(0)
            act.wait_ge(R_dve.sem, R_dve.after("ni"))
            n = act.value_load(idi[0:1, 0:1], min_val=NE, max_val=NE + MAX_OVER)
            with act.Fori(0, n) as r:
                end = ffn(U_MOE, FC * r, moe, FC * r, 1, 0, 4, hs1, hTh1)
                gathered(r + 1)
                hi(U_MOE + 6, end)
                act.wait_ge(unit_used, units(U_MOE + 5, end))
                nc.scalar.activation(Yh[:], ps[:, 2:4, :].rearrange("p b n -> p (b n)"), ACT.Copy).then_inc(yh_done, 1)
                hi(U_MOE + 7, end)
                act.wait_ge(scattered, r + 1)
                slots(r + 1)
            layer_norm(3)

        @block.tensor
        def _(pe):
            pe.sem_inc(unit_used, CREDIT)
            pe.sem_inc(C_pe.sem, C_pe.lead)
            for S in (dense, moe):
                pe.sem_inc(S["t"], 1)

            def split3(o, lh, ll, rh, rl, start, stop):
                nc.tensor.matmul(o, lh, rh, start=start, stop=False, skip_group_check=True)
                nc.tensor.matmul(o, lh, rl, start=False, stop=False, skip_group_check=True)
                return nc.tensor.matmul(o, ll, rh, start=False, stop=stop, skip_group_check=True)

            def wide(j, turn, half, banks, xh, xl):
                pe.wait_ge(lo_done, units(j, turn))
                for t, bank in enumerate(banks):
                    for k in range(4):
                        kk, w = half * 4 + k, slice(k * 512, (k + 1) * 512)
                        last = split3(ps[:, bank, :], xh[:, kk, t * P:(t + 1) * P], xl[:, kk, t * P:(t + 1) * P],
                                      unit_hi(j)[:, w], unit_lo(j)[:, w], kk == 0, kk == KD - 1)
                return last.then_inc(unit_used, 1)

            def deep(j, turn, banks, lhs, start, stop):
                pe.wait_ge(lo_done, units(j, turn))
                for t, bank in enumerate(banks):
                    for half in range(2):
                        for k in range(2):
                            w = slice(k * D + half * 512, k * D + half * 512 + 512)
                            lh, ll = lhs(t, k)
                            last = split3(ps[:, bank + half, :], lh, ll, unit_hi(j)[:, w], unit_lo(j)[:, w],
                                          start and k == 0, stop and k == 1)
                return last.then_inc(unit_used, 1)

            def transpose_x(bank):
                for q in range(4):
                    for k in range(2):
                        for t in range(NT):
                            c = (2 * q + k) * P
                            last = nc.tensor.transpose(ps[:, bank + q, k * SEQ + t * P:k * SEQ + t * P + P],
                                                       X[:, t, c:c + P], IDENT)
                    last.then_inc(xt_pe, 1)

            pe.wait_ge(cst_step, CST)
            pe.wait_ge(x_in, 16)
            transpose_x(0)
            pe.wait_ge(small_in, SMALL)
            nc.tensor.transpose(ps[:, 4, 0:P], cwr, IDENT).then_inc(S_pe.sem, 1)
            pe.wait_ge(xt_lo, 4)
            pe.wait_ge(S_dve.sem, S_dve.after("bal"))
            for t in range(NT):
                for k in range(KD):
                    last = split3(ps[:, 5, t * 32:t * 32 + 32], xT0h[:, k, t * P:(t + 1) * P], xT0l[:, k, t * P:(t + 1) * P],
                                  bah[:, k, :], bal[:, k, :], k == 0, k == KD - 1)
            last.then_inc(S_pe.sem, 1)
            pe.wait_ge(S_dve.sem, S_dve.after("ba"))

            with pe.Fori(0, 4) as i:
                def to_channels(c):
                    pe.wait_ge(A_act.sem, A_act.after("pre" + "AB"[c], i))
                    if c == 0:
                        pe.wait_ge(A_act.sem, A_act.after("tokB", i - 1))
                    for m in range(4):
                        for t in range(NT):
                            o = (m % 2) * SEQ + t * P
                            last = nc.tensor.transpose(ps[:, 4 + 2 * c + m // 2, o:o + P], pre[:, c, t, m * P:(m + 1) * P],
                                                       IDENT)
                    last.then_inc(A_pe.sem, 1)

                def to_tokens(c):
                    pe.wait_ge(A_act.sem, A_act.after("silu" + "AB"[c], i))
                    for t in range(NT):
                        for m in range(4):
                            last = nc.tensor.transpose(ps[:, 2 + 2 * c + t, m * P:(m + 1) * P], cacc[:, c, m, t * P:(t + 1) * P],
                                                       IDENT)
                    last.then_inc(A_pe.sem, 1)

                pe.wait_ge(A_act.sem, A_act.after("z", i - 1))
                wide(0, i, 0, (0, 1), xT0h, xT0l)
                wide(1, i, 1, (0, 1), xT0h, xT0l)
                pe.wait_ge(A_act.sem, A_act.after("tokA", i - 1))
                wide(2, i, 0, (2, 3), xT0h, xT0l)
                wide(3, i, 1, (2, 3), xT0h, xT0l)
                to_channels(0)
                pe.wait_ge(A_act.sem, A_act.after("preA", i))
                wide(4, i, 0, (0, 1), xT0h, xT0l)
                to_channels(1)
                wide(5, i, 1, (0, 1), xT0h, xT0l)
                to_tokens(0)
                to_tokens(1)

            pe.wait_ge(S_dve.sem, S_dve.after("g"))
            pe.wait_ge(A_act.sem, A_act.after("tokB", 3))
            nc.tensor.matmul(ps[:, 0, 0:VH], LE, g[:, 1, :], start=True, stop=True).then_inc(S_pe.sem, 1)
            nc.tensor.matmul(ps[:, 0, VH:2 * VH], GT, g[:, 0, :], start=True, stop=True).then_inc(S_pe.sem, 1)
            pe.wait_ge(S_act.sem, S_act.after("kd"))
            pe.wait_ge(S_pool.sem, S_pool.after("qn"))
            for c in range(8):
                if c == 4:
                    pe.wait_ge(S_dve.sem, S_dve.after("kn"))
                for h in range(2):
                    for t in range(NT):
                        o = h * SEQ + t * P
                        last = nc.tensor.transpose(ps[:, c, o:o + P], tok[:, 2 * c + h, t, :], IDENT)
                last.then_inc(S_pe.sem, 1)
            pe.wait_ge(S_act.sem, S_act.after("qT3"))
            pe.wait_ge(S_dve.sem, S_dve.after("kT3"))

            with pe.Fori(0, VH // HPG) as i:
                def heads(o, lhs, rhs):
                    for h in range(HPG):
                        last = nc.tensor.matmul(o[:, h * P:(h + 1) * P], lhs(h), rhs(h), start=True, stop=True)
                    return last.then_inc(C_pe.sem, 1)

                pe.wait_ge(C_pool.sem, C_pool.after("ck", i))
                for t in range(NT):
                    tt = slice(t * P, (t + 1) * P)
                    pe.wait_ge(C_dve.sem, C_dve.after("o1", i - 1))
                    pe.wait_ge(C_act.sem, C_act.after("v1s", i - 1))
                    for h in range(QPG):
                        nc.tensor.matmul(ps[:, t, h * P:(h + 1) * P], kTc[:, h, tt], kTc[:, h, tt], start=True, stop=True)
                        last = nc.tensor.matmul(ps[:, t, (2 + h) * P:(3 + h) * P], kTc[:, h, tt], qTc[:, h, tt],
                                                start=True, stop=True)
                    last.then_inc(C_pe.sem, 1)
                    pe.wait_ge(C_pool.sem, C_pool.after(f"G.{t}", i))
                    heads(ps[:, 2 + t, :], lambda h: XB[:, t, h, :], lambda h: GT)
                    nc.tensor.matmul(ps[:, 4 + t, :], GT, XB[:, t].rearrange("p h d -> p (h d)"), start=True, stop=True)\
                      .then_inc(C_pe.sem, 1)
                for t in range(NT):
                    pe.wait_ge(C_pool.sem, C_pool.after(f"C1.{t}", i))
                    for h in range(HPG):
                        last = nc.tensor.transpose(ps[:, 6 + t, h * P:(h + 1) * P], CB[:, t, h, :], IDENT)
                    last.then_inc(C_pe.sem, 1)
                for b in inv:
                    for t in range(NT):
                        pe.wait_ge(C_pool.sem, C_pool.after(f"C{b}.{t}", i))
                        if b == 2:
                            pe.wait_ge(C_act.sem, C_act.after(f"e.{t}", i))
                            pe.wait_ge(C_dve.sem, C_dve.after(f"dt1.{t}", i))
                        else:
                            pe.wait_ge(C_dve.sem, C_dve.after(f"u{b // 2}.{t}", i))
                        heads(ps[:, 2 + t, :], lambda h: CB[:, t, h, :], lambda h: DTB[:, t, h, :])
                    for t in range(NT):
                        pe.wait_ge(C_act.sem, C_act.after(f"x{b}.{t}", i))
                        if b == 2:
                            pe.wait_ge(C_dve.sem, C_dve.after(f"d1.{t}", i))
                            pe.wait_ge(C_act.sem, C_act.after(f"eT.{t}", i))
                        else:
                            pe.wait_ge(C_act.sem, C_act.after(f"d{b // 2}.{t}", i))
                        heads(ps[:, 4 + t, :], lambda h: DB[:, t, h, :], lambda h: XB[:, t, h, :])
                    for t in range(NT):
                        if b < 64:
                            pe.wait_ge(C_dve.sem, C_dve.after(f"u{b}.{t}", i))
                            for h in range(HPG):
                                last = nc.tensor.transpose(ps[:, 6 + t, h * P:(h + 1) * P], DTB[:, t, h, :], IDENT)
                            last.then_inc(C_pe.sem, 1)
                pe.wait_ge(C_dve.sem, C_dve.after("u64.1", i))
                pe.wait_ge(C_dve.sem, C_dve.after("A.1", i))
                heads(ps[:, 0, :], lambda h: DTB[:, 0, h, :], lambda h: tok[:, ds(16 + HPG * i + h, 1), 0, :]
                      .rearrange("p a d -> p (a d)"))
                pe.wait_ge(C_act.sem, C_act.after("v0s", i))
                pe.wait_ge(C_pool.sem, C_pool.after("kd", i))
                heads(ps[:, 1, :], lambda h: DB[:, 0, h, :], lambda h: XB[:, 0, h, :])
                heads(ps[:, 6, :], lambda h: ET[:, 0, h, :], lambda h: XB[:, 0, h, :])
                pe.wait_ge(C_act.sem, C_act.after("Ss", i))
                heads(ps[:, 2, :], lambda h: kTc[:, h // 2, P:SEQ], lambda h: CB[:, 0, h, :])
                heads(ps[:, 3, :], lambda h: qTc[:, h // 2, P:SEQ], lambda h: CB[:, 0, h, :])
                pe.wait_ge(C_dve.sem, C_dve.after("r", i))
                heads(ps[:, 4, :], lambda h: DTB[:, 1, h, :], lambda h: CB[:, 1, h, :])
                pe.wait_ge(C_act.sem, C_act.after("v1s", i))
                heads(ps[:, 5, :], lambda h: ET[:, 1, h, :], lambda h: XB[:, 1, h, :])

            pe.wait_ge(C_dve.sem, C_dve.after("o1", 3))
            pe.wait_ge(O_dve.sem, O_dve.after("z"))
            pe.wait_ge(O_pool.sem, O_pool.after("z"))
            for c in range(8):
                for h in range(2):
                    for t in range(NT):
                        o = h * SEQ + t * P
                        last = nc.tensor.transpose(ps[:, c, o:o + P], tok[:, 16 + 2 * c + h, t, :], IDENT)
                last.then_inc(O_pe.sem, 1)
            pe.wait_ge(O_dve.sem, O_dve.after("l7"))
            for u in range(OUT_UNITS):
                deep(U_OUT + u, 0, (0, 2), lambda t, k: (oTh[:, 2 * u + k, t * P:(t + 1) * P],
                                                         oTl[:, 2 * u + k, t * P:(t + 1) * P]), u == 0, u == OUT_UNITS - 1)

            def ffn(base, turn, S, done, xh, xl, hs, hTh, hTl, g_banks, u_banks, t_banks, y_banks, before_last=None):
                tiles = range(len(g_banks))

                def chunk(j, turn, n, down):
                    pe.wait_ge(S["s"], n + 1)
                    wide(j, turn, 0, g_banks, xh, xl)
                    wide(j + 1, turn, 1, g_banks, xh, xl)
                    pe.wait_ge(S["h"], n + 1)
                    if u_banks == t_banks:
                        pe.wait_ge(S["hl"], n + 1)
                    wide(j + 2, turn, 0, u_banks, xh, xl)
                    wide(j + 3, turn, 1, u_banks, xh, xl)
                    if down:
                        down_units(j + 4, turn, n)
                    pe.wait_ge(S["h"], n + 2)
                    pe.wait_ge(S["hl"], n + 1)
                    for t in tiles:
                        for m in range(4):
                            last = nc.tensor.transpose(ps[:, t_banks[t], m * P:(m + 1) * P], hs[:, t, m * P:(m + 1) * P],
                                                       IDENT)
                    last.then_inc(S["t"], 1)

                def down_units(j, turn, n):
                    pe.wait_ge(S["hl"], n + 1)
                    for half in range(2):
                        deep(j + half, turn, y_banks,
                             lambda t, k: (hTh[:, t, 2 * half + k, :], hTl[:, t, 2 * half + k, :]), False, False)

                chunk(base, turn, done, False)
                for bank in y_banks:
                    for half in range(2):
                        nc.tensor.matmul(ps[:, bank + half, :], zeros[:, 0:P], zeros[:], start=True, stop=True)
                with pe.Fori(0, FC - 1) as c:
                    chunk(base + 4, turn + c, done + c + 1, True)
                if before_last:
                    before_last()
                down_units(base + 4, turn + FC - 1, done + FC)

            pe.wait_ge(ln_dve[0].sem, ln_dve[0].after("b1"))
            transpose_x(4)
            pe.wait_ge(xt_lo, 8)
            ffn(U_FFN, 0, dense, 0, xTh, xTl, hs0, hTh0, hTl0, (0, 1), (2, 3), (2, 3), (4, 6))

            pe.wait_ge(ln_dve[1].sem, ln_dve[1].after("b1"))
            transpose_x(0)
            pe.wait_ge(xt_lo, 12)
            with pe.Fori(0, 2) as i:
                for c, bank in enumerate((4, 6, 0)):
                    pe.wait_ge(B_act.sem, B_act.after(f"c{c}", i - 1))
                    wide(U_SBIN + 2 * c, i, 0, (bank, bank + 1), xTh, xTl)
                    wide(U_SBIN + 2 * c + 1, i, 1, (bank, bank + 1), xTh, xTl)

            pe.wait_ge(B_act.sem, B_act.after("c2", 1))
            for grp in range(2):
                for part, b0 in ((0, 0), (1, 4)):
                    if grp and part:
                        pe.wait_ge(T_act.sem, T_act.after("oh", 0))
                        pe.wait_ge(T_dve.sem, T_dve.after("ol", 0))
                    for h in range(4):
                        for t in range(NT):
                            c = part * D + (4 * grp + h) * P
                            last = nc.tensor.transpose(ps[:, b0 + h, t * P:(t + 1) * P], qkv[:, t, c:c + P], IDENT)
                    last.then_inc(T_pe.sem, 1)
                pe.wait_ge(T_act.sem, T_act.after("q", grp))
                pe.wait_ge(T_dve.sem, T_dve.after("k", grp))
                for h in range(4):
                    nc.tensor.matmul(ps[:, h, 0:SEQ], kTs[:, h, 0:P], qTs[:, h, :], start=True, stop=False,
                                     skip_group_check=True)
                    last = nc.tensor.matmul(ps[:, h, SEQ:384], kTs[:, h, P:SEQ], qTs[:, h, P:SEQ], start=False, stop=False,
                                            skip_group_check=True)
                last.then_inc(T_pe.sem, 1)
                pe.wait_ge(T_dve.sem, T_dve.after("m1", grp))
                for h in range(4):
                    nc.tensor.matmul(ps[:, h, 0:SEQ], NGE, spl[:, h, 0:SEQ], start=False, stop=False, skip_group_check=True)
                    nc.tensor.matmul(ps[:, h, P:SEQ], NONES, spl[:, h, SEQ:384], start=False, stop=False,
                                     skip_group_check=True)
                    last = nc.tensor.matmul(ps[:, h, SEQ:384], NGE, spl[:, h, SEQ:384], start=False, stop=True,
                                            skip_group_check=True)
                last.then_inc(T_pe.sem, 1)
                pe.wait_ge(T_dve.sem, T_dve.after("n1", grp))
                for h in range(4):
                    c = 2 * D + (4 * grp + h) * P
                    nc.tensor.matmul(ps[:, 4 + h, 0:SEQ], qkv[:, 0, c:c + P], att[:, h, 0:SEQ], start=True, stop=False,
                                     skip_group_check=True)
                    last = nc.tensor.matmul(ps[:, 4 + h, P:SEQ], qkv[:, 1, c:c + P], att[:, h, SEQ:384], start=False,
                                            stop=True, skip_group_check=True)
                last.then_inc(T_pe.sem, 1)
            pe.wait_ge(T_act.sem, T_act.after("oh", 1))
            pe.wait_ge(T_dve.sem, T_dve.after("ol", 1))
            for u in range(SBOUT_UNITS):
                deep(U_SBOUT + u, 0, (0, 2), lambda t, k: (aTh[:, 2 * u + k, t * P:(t + 1) * P],
                                                           aTl[:, 2 * u + k, t * P:(t + 1) * P]),
                     u == 0, u == SBOUT_UNITS - 1)

            pe.wait_ge(ln_dve[2].sem, ln_dve[2].after("b1"))
            transpose_x(4)
            pe.wait_ge(xt_lo, 16)
            pe.wait_ge(R_dve.sem, R_dve.after("rwl"))
            for t in range(NT):
                for k in range(KD):
                    last = split3(ps[:, 0, t * NE:(t + 1) * NE], xTh[:, k, t * P:(t + 1) * P], xTl[:, k, t * P:(t + 1) * P],
                                  rwh[:, k, :], rwl[:, k, :], k == 0, k == KD - 1)
            last.then_inc(R_pe.sem, 1)
            pe.wait_ge(R_dve.sem, R_dve.after("mask"))
            mask = rt["mask"]
            nc.tensor.matmul(ps[:, 1, 0:NE], LT, mask[:, 0, :], start=True, stop=True)
            nc.tensor.matmul(ps[:, 1, NE:2 * NE], LT, mask[:, 1, :], start=True, stop=False)
            nc.tensor.matmul(ps[:, 1, NE:2 * NE], ONES, mask[:, 0, :], start=False, stop=True)
            nc.tensor.matmul(ps[:, 1, 2 * NE:3 * NE], ONES, mask[:, 0, :], start=True, stop=False)
            nc.tensor.matmul(ps[:, 1, 2 * NE:3 * NE], ONES, mask[:, 1, :], start=False, stop=True).then_inc(R_pe.sem, 1)

            def gather(r):
                pe.wait_ge(K_dve.sem, K_dve.after("s1", r))
                for part, (src, banks) in enumerate(((Xh, (5, 6)), (Xl, (7, 0)))):
                    for k in range(KD):
                        o = ps[:, banks[k // 4], (k % 4) * P:(k % 4 + 1) * P]
                        for t in range(NT):
                            last = nc.tensor.matmul(o, src[:, t, k * P:(k + 1) * P], G[:, t, :], start=t == 0,
                                                    stop=t == NT - 1)
                    last.then_inc(K_pe.sem, 1)
                for t in range(NT):
                    last = nc.tensor.transpose(ps[:, 1, t * P:(t + 1) * P], G[:, t, :].bitcast(F32), IDENT)
                last.then_inc(K_pe.sem, 1)

            pe.wait_ge(R_dve.sem, R_dve.after("ni"))
            pe.wait_ge(R_act.sem, R_act.after("xh"))
            pe.wait_ge(R_dve.sem, R_dve.after("xl"))
            n = pe.value_load(idi[0:1, 0:1], min_val=NE, max_val=NE + MAX_OVER)
            gather(0)
            with pe.Fori(0, n) as r:
                pe.wait_ge(K_act.sem, K_act.after("gt", r))
                pe.wait_ge(K_dve.sem, K_dve.after("l0", r))
                pe.wait_ge(added, NT * r + 1)

                def next_rows():
                    pe.wait_ge(moe["s"], FC * (r + 1) + 1)
                    gather(r + 1)

                ffn(U_MOE, FC * r, moe, FC * r, xeh, xel, hs1, hTh1, hTl1, (0,), (1,), (4,), (2,), next_rows)
                pe.wait_ge(yl_done, r + 1)
                pe.wait_ge(K_act.sem, K_act.after("hi", r + 1))
                pe.wait_ge(K_dve.sem, K_dve.after("l7", r + 1))
                for t in range(NT):
                    for half in range(2):
                        w = slice(half * 512, half * 512 + 512)
                        o = ps[:, 4 + 2 * t + half, :]
                        nc.tensor.matmul(o, GTr[:, t * P:(t + 1) * P], Yh[:, w], start=True, stop=False)
                        last = nc.tensor.matmul(o, GTr[:, t * P:(t + 1) * P], Yl[:, w], start=False, stop=True)
                last.then_inc(scattered, 1)

        @block.vector
        def _(dve):
            V = nc.vector
            dve.sem_inc(lo_done, CREDIT)
            dve.sem_inc(C_dve.sem, C_dve.lead)
            dve.sem_inc(added, 1)
            for S in (dense, moe):
                dve.sem_inc(S["h"], 1)
                dve.sem_inc(S["hl"], 1)

            def lo(j, turn=0):
                dve.wait_ge(hi_done, j + 6 * turn + 1)
                V.tensor_tensor(unit_lo(j), raw[:, j % RAW, :], unit_hi(j).bitcast(F32), ALU.subtract).then_inc(lo_done, 1)

            def transposed(k, th, tl, bank):
                for q in range(4):
                    dve.wait_ge(xt_hi, 4 * k + q + 1)
                    v = slice(2 * q, 2 * q + 2)
                    V.tensor_tensor(tl[:, v, :].rearrange("p a b -> p (a b)"), ps[:, bank + q, :],
                                    th[:, v, :].rearrange("p a b -> p (a b)").bitcast(F32), ALU.subtract).then_inc(xt_lo, 1)

            def layer_norm(k, y_bank):
                L, A = ln_dve[k], ln_act[k]
                for t in range(NT):
                    if y_bank is not None:
                        V.scalar_tensor_tensor(out=X[:, t], in0=X[:, t], scalar=ALPHA,
                                               in1=ps[:, y_bank + 2 * t:y_bank + 2 * t + 2, :].rearrange("p b n -> p (b n)"),
                                               op0=ALU.mult, op1=ALU.add).then_inc(L.sem, 1)
                        dve.wait_ge(L.sem, L.after(f"r{t}"))
                    for h in range(2):
                        V.bn_stats(stats[:, t, h, :], X[:, t, h * 512:(h + 1) * 512]).then_inc(L.sem, 1)
                    dve.wait_ge(L.sem, L.after(f"sb{t}"))
                    V.bn_aggr(mv[:, t, :], stats[:, t]).then_inc(L.sem, 1)
                dve.wait_ge(ln_in, 32 * (k + 1))
                for t in range(NT):
                    dve.wait_ge(A.sem, A.after(f"sd{t}"))
                    V.reciprocal(rstd[:, t], sdev[:, t]).then_inc(L.sem, 1)
                    dve.wait_ge(L.sem, L.after(f"rc{t}"))
                    V.tensor_scalar(X[:, t], X[:, t], mv[:, t, 0:1], rstd[:, t], ALU.subtract, ALU.mult).then_inc(L.sem, 1)
                    dve.wait_ge(L.sem, L.after(f"n{t}"))
                    V.tensor_tensor(X[:, t], X[:, t], lnrow[:, 0, :], ALU.mult).then_inc(L.sem, 1)
                    dve.wait_ge(L.sem, L.after(f"g{t}"))
                    V.tensor_tensor(X[:, t], X[:, t], lnrow[:, 1, :], ALU.add).then_inc(L.sem, 1)

            dve.wait_ge(S_act.sem, S_act.after("bah"))
            transposed(0, xT0h, xT0l, 0)
            dve.wait_ge(S_pe.sem, S_pe.after("cw"))
            V.tensor_copy(cw[:], ps[:, 4, 0:P]).then_inc(S_dve.sem, 1)
            V.tensor_tensor(bal[:], baw, bah[:].bitcast(F32), ALU.subtract).then_inc(S_dve.sem, 1)
            dve.wait_ge(R_act.sem, R_act.after("rwh"))
            V.tensor_tensor(rwl[:], rw[:], rwh[:].bitcast(F32), ALU.subtract).then_inc(R_dve.sem, 1)
            dve.wait_ge(S_pe.sem, S_pe.after("ba"))
            V.tensor_copy(ba[:].rearrange("p t n -> p (t n)"), ps[:, 5, 0:64]).then_inc(S_dve.sem, 1)

            lo(0)
            lo(1)
            with dve.Fori(0, 4) as i:
                def convolve(c):
                    dve.wait_ge(A_pe.sem, A_pe.after("t1" + "AB"[c], i))
                    if c == 0:
                        dve.wait_ge(S_dve.sem, S_dve.after("cw"))
                    for j in (3, 2, 1, 0):
                        for m in range(4):
                            src = ps[:, 4 + 2 * c + m // 2, (m % 2) * SEQ:(m % 2 + 1) * SEQ]
                            w = cw[:, ds(j * 32 + i * 8 + 4 * c + m, 1)]
                            s = 3 - j
                            if s == 0:
                                V.tensor_scalar(cacc[:, c, m, :], src, w, None, ALU.mult).then_inc(A_dve.sem, 1)
                            else:
                                dve.wait_ge(A_dve.sem, A_dve.after(f"{j + 1}{m}" + "AB"[c], i))
                                V.scalar_tensor_tensor(out=cacc[:, c, m, s:], in0=src[:, 0:SEQ - s], scalar=w,
                                                       in1=cacc[:, c, m, s:], op0=ALU.mult, op1=ALU.add)\
                                 .then_inc(A_dve.sem, 1)

                for j in (2, 3, 4, 5):
                    lo(j, i)
                convolve(0)
                lo(6, i)
                convolve(1)
                lo(7, i)

            V.tensor_tensor(xdt[:], ba[:, :, VH:2 * VH], dtb[:].unsqueeze(1).broadcast_to([P, NT, VH]), ALU.add)\
             .then_inc(S_dve.sem, 1)
            dve.wait_ge(S_act.sem, S_act.after("eb"))
            V.tensor_scalar(beta[:], beta[:], 1.0, None, ALU.add).then_inc(S_dve.sem, 1)
            dve.wait_ge(S_dve.sem, S_dve.after("b1"))
            V.reciprocal(beta[:], beta[:]).then_inc(S_dve.sem, 1)
            dve.wait_ge(S_act.sem, S_act.after("ln"))
            V.scalar_tensor_tensor(out=xdt[:], in0=xdt[:], scalar=0.0, in1=lsp[:], op0=ALU.max, op1=ALU.add)\
             .then_inc(S_dve.sem, 1)
            dve.wait_ge(S_dve.sem, S_dve.after("sp"))
            V.scalar_tensor_tensor(out=g[:], in0=xdt[:], scalar=-1.0, in1=negA[:].unsqueeze(1).broadcast_to([P, NT, VH]),
                                   op0=ALU.mult, op1=ALU.mult).then_inc(S_dve.sem, 1)
            dve.wait_ge(S_act.sem, S_act.after("eg"))
            V.tensor_tensor(beg1[:], beta[:, 1, :], eg1[:], ALU.mult).then_inc(S_dve.sem, 1)
            dve.wait_ge(A_act.sem, A_act.after("tokB", 3))
            dve.wait_ge(A_pe.sem, A_pe.after("t2B", 3))
            for h in range(QK):
                for t in range(NT):
                    k = tok[:, QK + h, t, :]
                    o = (h % 2) * P
                    last = V.tensor_tensor_reduce(cacc[:, t, h // 2, o:o + P], k, k, 1.0, 0.0, ALU.mult, ALU.add,
                                                  ssq[:, QK + h, t:t + 1])
            last.then_inc(S_dve.sem, 1)
            dve.wait_ge(S_act.sem, S_act.after("sd"))
            V.reciprocal(rsn[:], rsn[:]).then_inc(S_dve.sem, 1)
            dve.wait_ge(S_dve.sem, S_dve.after("rs"))
            V.tensor_scalar(rsn[:, 0:QK], rsn[:, 0:QK], SCALE, None, ALU.mult).then_inc(S_dve.sem, 1)
            k = tok[:, QK:2 * QK]
            V.tensor_tensor(k, k, rsn[:, QK:2 * QK].unsqueeze(3).broadcast_to([P, QK, NT, P]), ALU.mult)\
             .then_inc(S_dve.sem, 1)
            for c in range(4):
                dve.wait_ge(S_pe.sem, S_pe.after(f"kT{c}"))
                V.tensor_copy(kT[:, 2 * c:2 * c + 2, :].rearrange("p a b -> p (a b)"), ps[:, 4 + c, :])\
                 .then_inc(S_dve.sem, 1)

            with dve.Fori(0, VH // HPG) as i:
                def flat(buf, t):
                    return buf[:, t].rearrange("p h d -> p (h d)")

                def four(ap):
                    return ap.unsqueeze(1).broadcast_to([P, HPG, P])

                def pairs(ap):
                    return ap.rearrange("p (q d) -> p q d", d=P).unsqueeze(2).broadcast_to([P, QPG, 2, P])

                for t in range(NT):
                    e4 = E_[:, t].rearrange("p (q r) d -> p q r d", r=2)
                    t4 = ET[:, t].rearrange("p (q r) d -> p q r d", r=2)
                    dve.wait_ge(C_act.sem, C_act.after(f"e.{t}", i))
                    V.tensor_tensor(e4, e4, pairs(ps[:, t, 0:2 * P]), ALU.mult).then_inc(C_dve.sem, 1)
                    dve.wait_ge(C_dve.sem, C_dve.after(f"L1.{t}", i))
                    dve.wait_ge(C_pool.sem, C_pool.after(f"MB.{t}", i))
                    V.tensor_tensor(E_[:, t], E_[:, t], DB[:, t], ALU.mult).then_inc(C_dve.sem, 1)
                    dve.wait_ge(C_act.sem, C_act.after(f"eT.{t}", i))
                    V.tensor_tensor(t4, t4, pairs(ps[:, t, 2 * P:4 * P]), ALU.mult).then_inc(C_dve.sem, 1)
                    dve.wait_ge(C_dve.sem, C_dve.after(f"A1.{t}", i))
                    V.tensor_tensor(ET[:, t], ET[:, t], four(LE), ALU.mult).then_inc(C_dve.sem, 1)
                for t in range(NT):
                    dve.wait_ge(C_pool.sem, C_pool.after(f"C1.{t}", i))
                    V.tensor_tensor(DB[:, t], four(IDENT), CB[:, t], ALU.subtract).then_inc(C_dve.sem, 1)
                    dve.wait_ge(C_pe.sem, C_pe.after(f"T1.{t}", i))
                    V.tensor_tensor(DTB[:, t], four(IDENT), ps[:, 6 + t, :].rearrange("p (h d) -> p h d", d=P),
                                    ALU.subtract).then_inc(C_dve.sem, 1)
                for b in inv:
                    for t in range(NT):
                        dve.wait_ge(C_pe.sem, C_pe.after(f"U{b}.{t}", i))
                        V.tensor_tensor(flat(DTB, t), flat(DTB, t), ps[:, 4 + t, :], ALU.subtract).then_inc(C_dve.sem, 1)
                o = [tok[:, ds(16 + HPG * i, HPG), t, :] for t in range(NT)]

                def per_head(v):
                    return v[:, ds(HPG * i, HPG)].unsqueeze(2).broadcast_to([P, HPG, P])

                def heads(bank):
                    return ps[:, bank, :].rearrange("p (h d) -> p h d", d=P)

                dve.wait_ge(C_pe.sem, C_pe.after("O0", i))
                V.tensor_copy(o[0], heads(6)).then_inc(C_dve.sem, 1)
                dve.wait_ge(C_pe.sem, C_pe.after("PK", i))
                V.tensor_tensor(CB[:, 1], heads(2), per_head(beg1), ALU.mult).then_inc(C_dve.sem, 1)
                dve.wait_ge(C_dve.sem, C_dve.after("r1", i))
                V.tensor_tensor(CB[:, 1], o[1], CB[:, 1], ALU.subtract).then_inc(C_dve.sem, 1)
                dve.wait_ge(C_pe.sem, C_pe.after("v1", i))
                V.tensor_tensor(CB[:, 1], heads(3), per_head(eg1), ALU.mult).then_inc(C_dve.sem, 1)
                dve.wait_ge(C_pe.sem, C_pe.after("AV", i))
                dve.wait_ge(C_dve.sem, C_dve.after("o1a", i))
                V.tensor_tensor(o[1], CB[:, 1], heads(5), ALU.add).then_inc(C_dve.sem, 1)

            dve.wait_ge(C_dve.sem, C_dve.after("o1", 3))
            for h in range(VH):
                v = tok[:, 16 + h, 0, :]
                last = V.tensor_tensor_reduce((E_, ET)[h // 8][:, (h // 4) % 2, h % 4, :], v, v, 1.0, 0.0, ALU.mult, ALU.add,
                                              ssq[:, h, 0:1])
            last.then_inc(O_dve.sem, 1)
            dve.wait_ge(O_act.sem, O_act.after("sd"))
            V.reciprocal(rsn[:], rsn[:]).then_inc(O_dve.sem, 1)
            dve.wait_ge(O_dve.sem, O_dve.after("rs"))
            dve.wait_ge(S_pool.sem, S_pool.after("zn0"))
            o0 = tok[:, 16:32, 0, :]
            V.tensor_tensor(o0, o0, rsn[:, :, 0].unsqueeze(2).broadcast_to([P, VH, P]), ALU.mult).then_inc(O_dve.sem, 1)
            dve.wait_ge(O_dve.sem, O_dve.after("n"))
            V.tensor_tensor(o0, o0, zs[:, 0, :].rearrange("p (h d) -> p h d", d=P), ALU.mult).then_inc(O_dve.sem, 1)
            for c in range(8):
                dve.wait_ge(O_act.sem, O_act.after(f"h{c}"))
                v = slice(2 * c, 2 * c + 2)
                V.tensor_tensor(oTl[:, v, :].rearrange("p a b -> p (a b)"), ps[:, c, :],
                                oTh[:, v, :].rearrange("p a b -> p (a b)").bitcast(F32), ALU.subtract).then_inc(O_dve.sem, 1)
            for u in range(OUT_UNITS):
                lo(U_OUT + 2 + u)
            dve.wait_ge(unit_used, units(U_OUT + OUT_UNITS - 1))
            layer_norm(0, 0)

            def ffn(base, turn, S, done, tiles, u_bank, t_bank, hs, hTh, hTl):
                def hidden(n, up):
                    dve.wait_ge(unit_used, up)
                    dve.wait_ge(S["s"], n + 2)
                    V.tensor_tensor(hs[:], hs[:], ps[:, u_bank:u_bank + tiles, :], ALU.mult).then_inc(S["h"], 1)

                def hidden_lo(n):
                    dve.wait_ge(S["hh"], n + 2)
                    V.tensor_tensor(hTl[:].rearrange("p t m d -> p t (m d)"), ps[:, t_bank:t_bank + tiles, :],
                                    hTh[:].rearrange("p t m d -> p t (m d)").bitcast(F32), ALU.subtract).then_inc(S["hl"], 1)

                lo(base + 2, turn)
                lo(base + 3, turn)
                hidden(done, units(base + 3, turn))
                lo(base + 4, turn)
                lo(base + 5, turn)
                hidden_lo(done)
                with dve.Fori(0, FC - 1) as c:
                    for j in (6, 7, 8, 9):
                        lo(base + j, turn + c)
                    hidden(done + c + 1, units(base + 7, turn + c))
                    lo(base + 10, turn + c)
                    lo(base + 11, turn + c)
                    hidden_lo(done + c + 1)
                return turn + FC - 1

            transposed(1, xTh, xTl, 4)
            end = ffn(U_FFN, 0, dense, 0, NT, 2, 2, hs0, hTh0, hTl0)
            lo(U_FFN + 6, end)
            lo(U_FFN + 7, end)
            dve.wait_ge(unit_used, units(U_FFN + FFN_UNITS - 1))
            layer_norm(1, 4)

            transposed(2, xTh, xTl, 0)
            with dve.Fori(0, 2) as i:
                for j in range(2, 8):
                    lo(U_SBIN + j, i)
            for grp in range(2):
                for_diag = LT.unsqueeze(1).broadcast_to([P, 4, P])
                dve.wait_ge(T_pe.sem, T_pe.after("k", grp))
                V.tensor_copy(kTs[:], ps[:, 4:8, 0:SEQ]).then_inc(T_dve.sem, 1)
                dve.wait_ge(T_act.sem, T_act.after("l", grp))
                V.scalar_tensor_tensor(out=spl[:], in0=ps[:, 0:4, 0:384], scalar=0.0, in1=spl[:], op0=ALU.max, op1=ALU.add)\
                 .then_inc(T_dve.sem, 1)
                dve.wait_ge(T_dve.sem, T_dve.after("sp", grp))
                for w in (slice(0, P), slice(SEQ, 384)):
                    V.tensor_tensor(spl[:, :, w], spl[:, :, w], for_diag, ALU.mult).then_inc(T_dve.sem, 1)
                dve.wait_ge(T_pe.sem, T_pe.after("R", grp))
                V.tensor_scalar(att[:], ps[:, 0:4, 0:384], 0.0, None, ALU.min).then_inc(T_dve.sem, 1)
                dve.wait_ge(T_act.sem, T_act.after("p", grp))
                for w in (slice(0, P), slice(SEQ, 384)):
                    V.tensor_tensor(att[:, :, w], att[:, :, w], for_diag, ALU.mult).then_inc(T_dve.sem, 1)
                dve.wait_ge(T_act.sem, T_act.after("oh", grp))
                V.tensor_tensor(aTl[:, 4 * grp:4 * grp + 4, :], ps[:, 4:8, 0:SEQ],
                                aTh[:, 4 * grp:4 * grp + 4, :].bitcast(F32), ALU.subtract).then_inc(T_dve.sem, 1)
            for u in range(SBOUT_UNITS):
                lo(U_SBOUT + 2 + u)
            dve.wait_ge(unit_used, units(U_SBOUT + SBOUT_UNITS - 1))
            layer_norm(2, 0)

            transposed(3, xTh, xTl, 4)

            def step(name, ins):
                ins.then_inc(R_dve.sem, 1)
                dve.wait_ge(R_dve.sem, R_dve.after(name))

            def experts(v):
                return v.broadcast_to([P, NT, NE])

            idx = iota[:, 0:NE].unsqueeze(1).broadcast_to([P, NT, NE])
            dve.wait_ge(R_pe.sem, R_pe.after("lg"))
            step("lg", V.tensor_copy(rt["lg"][:].rearrange("p t e -> p (t e)"), ps[:, 0, 0:NT * NE]))
            for lg, m, eq, ca, i_, oh, rest in (("lg", "m1", "eq1", "ca", "i1", "oh1", "l2"),
                                                ("l2", "m2", "eq2", "c2", "i2", "oh2", None)):
                step(m, V.tensor_reduce(rs[m][:], rt[lg][:], AX_X, ALU.max))
                step(eq, V.tensor_tensor(rt[eq][:], rt[lg][:], experts(rs[m][:]), ALU.is_ge))
                step(ca, V.scalar_tensor_tensor(out=rt[ca][:], in0=rt[eq][:], scalar=-99.0, in1=idx, op0=ALU.mult,
                                                op1=ALU.add))
                step(i_, V.tensor_reduce(rs[i_][:], rt[ca][:], AX_X, ALU.min))
                step(oh, V.tensor_tensor(rt[oh][:], rt[ca][:], experts(rs[i_][:]), ALU.is_equal))
                if rest:
                    step(rest, V.scalar_tensor_tensor(out=rt[rest][:], in0=rt[oh][:], scalar=-3.0e38, in1=rt[lg][:],
                                                      op0=ALU.mult, op1=ALU.add))
            step("df", V.tensor_tensor(rs["df"][:], rs["m2"][:], rs["m1"][:], ALU.subtract))
            dve.wait_ge(R_act.sem, R_act.after("ex"))
            step("sm", V.tensor_scalar(rs["sm"][:], rs["ex"][:], 1.0, None, ALU.add))
            step("p1", V.reciprocal(rs["p1"][:], rs["sm"][:]))
            step("p2", V.tensor_tensor(rs["p2"][:], rs["ex"][:], rs["p1"][:], ALU.mult))
            step("mask", V.tensor_tensor(rt["mask"][:], rt["oh1"][:], rt["oh2"][:], ALU.add))
            step("cm1", V.tensor_tensor(rt["comb"][:], rt["oh1"][:], experts(rs["p1"][:]), ALU.mult))
            step("cm2", V.tensor_tensor(rt["tmp"][:], rt["oh2"][:], experts(rs["p2"][:]), ALU.mult))
            step("comb", V.tensor_tensor(rt["comb"][:], rt["comb"][:], rt["tmp"][:], ALU.add))
            dve.wait_ge(R_pe.sem, R_pe.after("rk"))
            step("rk1", V.scalar_tensor_tensor(out=rt["rank"][:].rearrange("p t e -> p (t e)"), in0=ps[:, 1, 0:NT * NE],
                                               scalar=1.0, in1=rt["mask"][:].rearrange("p t e -> p (t e)"), op0=ALU.add,
                                               op1=ALU.mult))
            step("rk2", V.tensor_scalar(rt["rank"][:], rt["rank"][:], -1.0, None, ALU.add))
            step("cnt", V.tensor_copy(cnt[:], ps[:, 1, NT * NE:(NT + 1) * NE]))
            step("ov", V.tensor_scalar(ov[:], cnt[:], float(P), None, ALU.is_gt))
            step("z0", V.memset(ranks[:], -1.0))
            step("z1", V.memset(gates[:], 0.0))
            step("z2", V.memset(ovp[:, 0:1], 0.0))
            for e in range(1, NE):
                step(f"pre{e}", V.tensor_tensor(ovp[:, e:e + 1], ovp[:, e - 1:e], ov[:, e - 1:e], ALU.add))
            for q in range(MAX_OVER):
                iq = ind[:, q, :]
                iq2 = iq.unsqueeze(1).broadcast_to([P, NT, NE])
                step(f"in{q}", V.tensor_scalar(iq, ovp[:], float(q), None, ALU.is_equal))
                step(f"im{q}", V.tensor_tensor(iq, iq, ov[:], ALU.mult))
                rq = ranks[:, :, NE + q:NE + q + 1]
                step(f"pr{q}", V.tensor_tensor(rt["tmp"][:], rt["rank"][:], iq2, ALU.mult))
                step(f"sr{q}", V.tensor_reduce(rq, rt["tmp"][:], AX_X, ALU.add))
                step(f"ad{q}", V.tensor_scalar(rq, rq, -float(P), None, ALU.add))
                step(f"pg{q}", V.tensor_tensor(rt["tmp"][:], rt["comb"][:], iq2, ALU.mult))
                step(f"sg{q}", V.tensor_reduce(gates[:, :, NE + q:NE + q + 1], rt["tmp"][:], AX_X, ALU.add))
                step(f"pi{q}", V.tensor_tensor(iq, iq, iota[:, 0:NE], ALU.mult))
                step(f"si{q}", V.tensor_reduce(ids[:, 1 + q:2 + q], iq, AX_X, ALU.add))
            step("rt", V.tensor_copy(ranks[:, :, 0:NE], rt["rank"][:]))
            step("gt", V.tensor_copy(gates[:, :, 0:NE], rt["comb"][:]))
            step("no", V.tensor_reduce(ids[:, 0:1], ov[:], AX_X, ALU.add))
            step("nc", V.tensor_scalar(ids[:, 0:1], ids[:, 0:1], float(NE), None, ALU.add))
            step("ni", V.tensor_copy(idi[:], ids[:]))
            dve.wait_ge(R_act.sem, R_act.after("xh"))
            step("xl", V.tensor_tensor(Xl[:], X[:], Xh[:].bitcast(F32), ALU.subtract))
            dve.wait_ge(xt_pe, 16)
            step("xa", V.tensor_scalar(X[:], X[:], ALPHA, None, ALU.mult))

            def select(r):
                for t in range(NT):
                    V.tensor_scalar(G[:, t, :], iota[:], ranks[:, t, ds(r, 1)], None, ALU.is_equal).then_inc(K_dve.sem, 1)

            def gathered(r):
                dve.wait_ge(K_pe.sem, K_pe.after("lo", r))
                for k, bank in ((0, 7), (4, 0)):
                    V.tensor_copy(xel[:, k:k + 4, :].rearrange("p k s -> p (k s)"), ps[:, bank, :]).then_inc(K_dve.sem, 1)

            n = dve.value_load(idi[0:1, 0:1], min_val=NE, max_val=NE + MAX_OVER)
            select(0)
            gathered(0)
            with dve.Fori(0, n) as r:
                dve.wait_ge(K_pe.sem, K_pe.after("tr", r))
                select(r + 1)
                end = ffn(U_MOE, FC * r, moe, FC * r, 1, 1, 4, hs1, hTh1, hTl1)
                gathered(r + 1)
                lo(U_MOE + 6, end)
                dve.wait_ge(yh_done, r + 1)
                V.tensor_tensor(Yl[:], ps[:, 2:4, :].rearrange("p b n -> p (b n)"), Yh[:].bitcast(F32), ALU.subtract)\
                 .then_inc(yl_done, 1)
                lo(U_MOE + 7, end)
                dve.wait_ge(scattered, r + 1)
                for t in range(NT):
                    V.scalar_tensor_tensor(out=X[:, t], in0=ps[:, 4 + 2 * t:6 + 2 * t, :].rearrange("p b n -> p (b n)"),
                                           scalar=gates[:, t, ds(r, 1)], in1=X[:, t], op0=ALU.mult, op1=ALU.add)\
                     .then_inc(added, 1)
            dve.wait_ge(added, NT * n + 1)
            layer_norm(3, None)


_INS = ["x", "gdn_w_in", "gdn_conv_w", "gdn_a_log", "gdn_dt_bias", "gdn_norm_w", "gdn_w_out", "sb_w_in", "sb_w_out",
        "ffn_w_gate", "ffn_w_up", "ffn_w_down", "moe_router", "moe_w_gate", "moe_w_up", "moe_w_down", "ln_g", "ln_b"]


def kernel(**inputs):
    import numpy as np
    import concourse.bacc as bacc
    from concourse.bass_utils import run_bass_kernel_spmd

    nc = bacc.Bacc("TRN2", target_bir_lowering=False, num_devices=1)
    arrays, args = {}, []
    for name in _INS:
        a = np.ascontiguousarray(inputs[name])
        arrays[f"in_{name}"] = a
        args.append(nc.dram_tensor(f"in_{name}", a.shape, mybir.dt.from_np(a.dtype), kind="ExternalInput").ap())
    args.append(nc.dram_tensor("out_0", (1, SEQ, D), F32, kind="ExternalOutput").ap())
    hybrid_trunk(nc, *args)
    r = run_bass_kernel_spmd(nc, [arrays], core_ids=[0])
    return r.results[0]["out_0"]
```

```python
from contextlib import ExitStack

import concourse.bass as bass
from concourse import mybir

ALU = mybir.AluOpType
ACT = mybir.ActivationFunctionType
AX_X = mybir.AxisListType.X
F32 = mybir.dt.float32
F32R = mybir.dt.float32r
I32 = mybir.dt.int32
ds = bass.ds

P = 128
SEQ = 256
NT = SEQ // P
D = 1024
KD = D // P
QK = 8
VH = 16
HPG = 4
QPG = HPG // 2
GROUPS = 2
LANES = GROUPS * NT
CONV_DIM = 4096
Z0 = CONV_DIM
BA0 = CONV_DIM + VH * P
FF = 3584
FC = FF // 512
NE = 8
TOPK = 2
SBH = 8
MAX_OVER = 3
ROUNDS = NE + MAX_OVER + 1
ALPHA = 4.0 ** 0.25
LN_EPS = 1e-5
RMS_EPS = 1e-6
SCALE = float(P) ** -0.5

RAW = 6
SPLIT = 3
CREDIT = 6
UNIT = 2048
A_UNITS = 24
OUT_UNITS = 8
FFN_UNITS = 6 * FC
SBIN_UNITS = 12
SBOUT_UNITS = 4
U_OUT = A_UNITS
U_FFN = U_OUT + OUT_UNITS
U_SBIN = U_FFN + FFN_UNITS
U_SBOUT = U_SBIN + SBIN_UNITS
U_MOE = U_SBOUT + SBOUT_UNITS

TURNS = VH // (GROUPS * HPG)
LEVELS = [1, 2, 4, 8, 16, 32, 64]
CST = 9 + len(LEVELS) + 5 + 3 * len(LEVELS)
SMALL = 16 * 6


class Stages:

    def __init__(self, sem, names, lead=False):
        self.sem = sem
        self.names = list(names)
        self.lead = len(self.names) if lead else 0
        assert len(set(self.names)) == len(self.names)

    def after(self, name, turn=0):
        return turn * len(self.names) + self.names.index(name) + 1 + self.lead


def hybrid_trunk(nc, x, gdn_w_in, gdn_conv_w, gdn_a_log, gdn_dt_bias, gdn_norm_w, gdn_w_out,
                 sb_w_in, sb_w_out, ffn_w_gate, ffn_w_up, ffn_w_down,
                 moe_router, moe_w_gate, moe_w_up, moe_w_down, ln_g, ln_b, out):
    with ExitStack() as ctx:
        def sb(name, shape, dt=F32, where=ctx):
            return where.enter_context(nc.sbuf_tensor(name, shape, dt))

        def sem(name):
            return ctx.enter_context(nc.semaphore(name))

        raw = sb("raw", [P, RAW, UNIT])
        w_hi = sb("w_hi", [P, SPLIT, UNIT], F32R)
        w_lo = sb("w_lo", [P, SPLIT, UNIT], F32R)
        X = sb("X", [P, NT, D])
        cst = sb("cst", [P, 7 + len(LEVELS), P])
        IDENT, LE, GT, LT, NGE, ONES, NONES = (cst[:, i, :] for i in range(7))
        LEVEL = {b: cst[:, 7 + i, :] for i, b in enumerate(LEVELS)}
        iota = sb("iota", [P, P])
        zeros = sb("zeros", [P, 512], F32R)
        bah = sb("bah", [P, KD, 32], F32R)
        bal = sb("bal", [P, KD, 32], F32R)
        rw = sb("rw", [P, KD, NE])
        rwh = sb("rwh", [P, KD, NE], F32R)
        rwl = sb("rwl", [P, KD, NE], F32R)
        stats = sb("stats", [P, NT, 2, 6])
        mv = sb("mv", [P, NT, 2])
        sdev = sb("sdev", [P, NT, 1])
        rstd = sb("rstd", [P, NT, 1])
        ps = ctx.enter_context(nc.psum_tensor("ps", [P, 8, 512], F32))

        gdn = ExitStack()
        tok = sb("tok", [P, 32, NT, P], F32, gdn)
        zs = sb("zs", [P, NT, VH * P], F32, gdn)
        kT = sb("kT", [P, QK, SEQ], F32, gdn)
        ba = sb("ba", [P, NT, 32], F32, gdn)
        gsb = {n: sb(n, [P, NT, VH], F32, gdn) for n in ("beta", "xdt", "axdt", "lsp", "g")}
        beta, xdt, axdt, lsp, g = gsb.values()
        negA = sb("negA", [P, VH], F32, gdn)
        dtb = sb("dtb", [P, VH], F32, gdn)
        eg1 = sb("eg1", [P, VH], F32, gdn)
        beg1 = sb("beg1", [P, VH], F32, gdn)
        kdec = sb("kdec", [P, VH], F32, gdn)
        ssq = sb("ssq", [P, 2 * QK, NT], F32, gdn)
        rsn = sb("rsn", [P, 2 * QK, NT], F32, gdn)
        cw = sb("cw", [P, P], F32, gdn)
        nw = sb("nw", [P, P], F32, gdn)

        pa = ExitStack()
        xT0h = sb("xT0h", [P, KD, SEQ], F32R, pa)
        xT0l = sb("xT0l", [P, KD, SEQ], F32R, pa)
        pre = sb("pre", [P, 2, NT, 512], F32, pa)
        cacc = sb("cacc", [P, 2, 4, SEQ], F32, pa)
        pa.close()
        pc = ExitStack()
        E_ = sb("E_", [P, NT, HPG, P], F32, pc)
        ET = sb("ET", [P, NT, HPG, P], F32, pc)
        XB = sb("XB", [P, NT, HPG, P], F32, pc)
        DB = sb("DB", [P, NT, HPG, P], F32, pc)
        DTB = sb("DTB", [P, NT, HPG, P], F32, pc)
        CB = sb("CB", [P, NT, HPG, P], F32, pc)
        kTc = sb("kTc", [P, GROUPS * QPG, SEQ], F32, pc)
        pc.close()
        spare = raw[:, 2:RAW, :].rearrange("p s n -> p (s n)").rearrange("p (k t h d) -> p k t h d", t=NT, h=HPG, d=P)

        def lanes(first, k):
            return [first[:, 0], first[:, 1], spare[:, k, 0], spare[:, k, 1]]

        Ec, ETc, Xc, Dc, DTc, Cc = (lanes(b, k) for k, b in enumerate((E_, ET, XB, DB, DTB, CB)))
        qTc = spare[:, 6].rearrange("p t h d -> p (t h d)").rearrange("p (h s) -> p h s", s=SEQ)

        def flat(lane):
            return lane.rearrange("p h d -> p (h d)")

        po = ExitStack()
        oTh = sb("oTh", [P, VH, SEQ], F32R, po)
        oTl = sb("oTl", [P, VH, SEQ], F32R, po)
        po.close()
        baw = tok[:, 0:1].rearrange("p a b c -> p (a b c)").rearrange("p (k n) -> p k n", n=32)
        cwr = tok[:, 1, 0, :]
        gdn.close()

        late = ctx
        lnrow = sb("lnrow", [P, 2, D], F32, late)
        xTh = sb("xTh", [P, KD, SEQ], F32R, late)
        xTl = sb("xTl", [P, KD, SEQ], F32R, late)
        fs = ExitStack()
        qkv = sb("qkv", [P, NT, 3 * D], F32, fs)
        qTs = sb("qTs", [P, 4, SEQ], F32, fs)
        kTs = sb("kTs", [P, 4, SEQ], F32, fs)
        att = sb("att", [P, 4, 384], F32, fs)
        spl = sb("spl", [P, 4, 384], F32, fs)
        aTh = sb("aTh", [P, SBH, SEQ], F32R, fs)
        aTl = sb("aTl", [P, SBH, SEQ], F32R, fs)
        fs.close()
        fd = ExitStack()
        hs0 = sb("hs0", [P, NT, 512], F32, fd)
        hTh0 = sb("hTh0", [P, NT, 4, P], F32R, fd)
        hTl0 = sb("hTl0", [P, NT, 4, P], F32R, fd)
        fd.close()
        fm = ExitStack()
        Xh = sb("Xh", [P, NT, D], F32R, fm)
        Xl = sb("Xl", [P, NT, D], F32R, fm)
        xeh = sb("xeh", [P, KD, P], F32R, fm)
        xel = sb("xel", [P, KD, P], F32R, fm)
        Yh = sb("Yh", [P, D], F32R, fm)
        Yl = sb("Yl", [P, D], F32R, fm)
        hs1 = sb("hs1", [P, 1, 512], F32, fm)
        hTh1 = sb("hTh1", [P, 1, 4, P], F32R, fm)
        hTl1 = sb("hTl1", [P, 1, 4, P], F32R, fm)
        G = sb("G", [P, NT, P], F32R, fm)
        GTr = sb("GTr", [P, SEQ], F32R, fm)
        rt = {n: sb("rt_" + n, [P, NT, NE], F32, fm) for n in
              ("lg", "eq1", "ca", "oh1", "l2", "eq2", "oh2", "mask", "comb", "rank", "c2", "tmp")}
        rs = {n: sb("rs_" + n, [P, NT, 1], F32, fm) for n in
              ("m1", "i1", "m2", "i2", "df", "ex", "sm", "p1", "p2")}
        cnt = sb("cnt", [P, NE], F32, fm)
        ov = sb("ov", [P, NE], F32, fm)
        ovp = sb("ovp", [P, NE], F32, fm)
        ind = sb("ind", [P, MAX_OVER, NE], F32, fm)
        ranks = sb("ranks", [P, NT, ROUNDS], F32, fm)
        gates = sb("gates", [P, NT, ROUNDS], F32, fm)
        ids = sb("ids", [P, 4], F32, fm)
        idi = sb("idi", [P, 4], I32, fm)
        fm.close()

        raw_in = [sem(f"raw_in{i}") for i in range(RAW)]
        hi_done = sem("hi_done")
        lo_done = sem("lo_done")
        unit_used = sem("unit_used")
        x_in = sem("x_in")
        small_in = sem("small_in")
        cst_step = sem("cst_step")
        ln_in = sem("ln_in")
        out_done = sem("out_done")
        xt_pe, xt_hi, xt_lo = sem("xt_pe"), sem("xt_hi"), sem("xt_lo")
        A_pe = Stages(sem("A_pe"), ["t1A", "t1B", "t2A", "t2B"])
        A_act = Stages(sem("A_act"), ["preA", "c0A", "preB", "z", "siluA", "c0B", "tokA", "siluB", "tokB"], True)
        A_dve = Stages(sem("A_dve"), [f"{j}{m}{c}" for c in "AB" for j in (2, 1, 0) for m in range(4)])
        S_pe = Stages(sem("S_pe"), ["cw", "ba", "gc", "gl", "kT0", "kT1", "kT2", "kT3", "qT0", "qT1", "qT2", "qT3"])
        S_act = Stages(sem("S_act"), ["bah", "eb", "ax", "ex", "ea", "ln", "sq", "sd",
                                      "qT0", "qT1", "qT2", "qT3", "eg", "kd"])
        S_dve = Stages(sem("S_dve"), ["cw", "bal", "ba", "xdt", "b1", "b2", "sp", "g", "sq", "rs", "rq",
                                      "kT0", "kT1", "kT2", "kT3", "beg"])
        S_pool = Stages(sem("S_pool"), ["qn", "kn"])
        inv = LEVELS[1:]
        ln = range(LANES)
        C_pool = Stages(sem("C_pool"), ["G.0", "MB.0", "G.2", "MB.2", "MB.1", "MB.3", "G.1", "G.3"]
                        + [f"C{b}.{c}" for b in LEVELS for c in ln] + ["vb", "zn", "kd.0", "kd.1"])
        C_pe = Stages(sem("C_pe"), [f"{n}.{c}" for n in ("kk", "df", "dT", "T1") for c in ln]
                      + [f"{n}{b}.{c}" for b in inv for n in ("X", "U", "T") for c in ln if b < 64 or n != "T"]
                      + ["v0.0", "v0.1", "S.0", "O0.0", "S.1", "O0.1", "PK.0", "PQ.0", "PK.1", "PQ.1",
                         "v1.0", "v1.1", "AV.0", "AV.1"], True)
        C_act = Stages(sem("C_act"), ["cq"] + [f"{n}.{c}" for n in ("e", "eT") for c in ln]
                       + [f"{n}{b}.{c}" for b in inv for n in ("x", "d") for c in ln if b < 64 or n != "d"]
                       + [f"{n}.{g}" for n in ("v0s", "Ss", "v1s") for g in range(GROUPS)], True)
        C_dve = Stages(sem("C_dve"), ["ck"] + [f"{n}.{c}" for c in ln for n in ("L1", "L")]
                       + [f"A1.{c}" for c in ln] + [f"{n}.{c}" for c in ln for n in ("d1", "dt1")]
                       + [f"u2.{c}" for c in ln] + [f"A.{c}" for c in ln]
                       + [f"u{b}.{c}" for b in inv[1:] for c in ln]
                       + [f"{n}.{g}" for n in ("o0", "r1", "r", "o1a", "o1") for g in range(GROUPS)], True)
        O_pe, O_act, O_dve, O_pool = (Stages(sem(n), s) for n, s in (
            ("O_pe", [f"t{q}" for q in range(8)]),
            ("O_act", ["sq", "sd"] + [f"h{q}" for q in range(8)]),
            ("O_dve", ["sq", "rs", "n", "z"] + [f"l{q}" for q in range(8)]),
            ("O_pool", ["n", "z"])))
        ln_dve = [Stages(sem(f"ln_dve{k}"), [f"{n}{t}" for t in range(NT) for n in ("r", "sa", "sb", "ag") if n != "r" or k < 3]
                         + [f"{n}{t}" for t in range(NT) for n in ("rc", "n", "g", "b")]) for k in range(4)]
        ln_act = [Stages(sem(f"ln_act{k}"), ["sd0", "sd1"]) for k in range(4)]
        names = ("t", "s", "hh", "h", "hl")
        dense = {n: sem("dense_" + n) for n in names}
        moe = {n: sem("moe_" + n) for n in names}
        B_act = Stages(sem("B_act"), ["c0", "c1", "c2"], True)
        T_pe = Stages(sem("T_pe"), ["q", "k", "z", "R", "o"])
        T_act = Stages(sem("T_act"), ["q", "a", "e", "l", "p", "oh"])
        T_dve = Stages(sem("T_dve"), ["k", "sp", "m0", "m1", "mn", "n0", "n1", "ol"])
        R_pe = Stages(sem("R_pe"), ["lg", "rk"])
        R_act = Stages(sem("R_act"), ["rwh", "ex", "xh"])
        R_dve = Stages(sem("R_dve"), ["rwl", "lg", "m1", "eq1", "ca", "i1", "oh1", "l2", "m2", "eq2", "c2", "i2", "oh2",
                                      "df", "sm", "p1", "p2", "mask", "cm1", "cm2", "comb", "rk1", "rk2",
                                      "cnt", "ov", "z0", "z1", "z2"] + [f"pre{e}" for e in range(1, NE)]
                       + [n + str(q) for q in range(MAX_OVER)
                          for n in ("in", "im", "pr", "sr", "ad", "pg", "sg", "pi", "si")]
                       + ["rt", "gt", "no", "nc", "ni", "xl", "xa"])
        K_pe = Stages(sem("K_pe"), ["hi", "lo", "tr"])
        K_act = Stages(sem("K_act"), ["hi", "gt"])
        K_dve = Stages(sem("K_dve"), ["s0", "s1", "l7", "l0"])
        yh_done, yl_done, scattered, added = sem("yh_done"), sem("yl_done"), sem("scattered"), sem("added")

        def cols(w, half, c0):
            return w[half * 512:(half + 1) * 512, ds(c0, 512)].rearrange("(k p) n -> p k n", p=P)

        def rows(w, r0):
            return w[ds(r0, 256), :].rearrange("(k p) n -> p k n", p=P)

        def unit_hi(j):
            return w_hi[:, j % SPLIT, :]

        def unit_lo(j):
            return w_lo[:, j % SPLIT, :]

        def units(j, turn=0):
            return j + 6 * turn + 1 + CREDIT

        block = ctx.enter_context(nc.Block())

        @block.sync
        def _(sp):
            def load(j, turn, src, k):
                sp.wait_ge(lo_done, units(j - RAW, turn))
                sp.dma_start(raw[:, j % RAW, :].rearrange("p (k n) -> p k n", k=k), src)\
                  .then_inc(raw_in[j % RAW], 16)

            sp.dma_start(X[:], x[0].rearrange("(t p) d -> p t d", p=P)).then_inc(x_in, 16)
            with sp.Fori(0, 4) as i:
                for c, c0 in enumerate((i * 1024, i * 1024 + 512, i * 512 + Z0)):
                    for half in range(2):
                        load(2 * c + half, i, cols(gdn_w_in[0], half, c0), 4)
            for u in range(OUT_UNITS):
                if u == 2:
                    sp.wait_ge(C_dve.sem, C_dve.after("o1.1", TURNS - 1))
                load(U_OUT + u, 0, rows(gdn_w_out[0], u * 256), 2)

            def ffn(base, turn, wg, wu, wd):
                for k, w in enumerate((wg, wu)):
                    for half in range(2):
                        load(base + 2 * k + half, turn, cols(w, half, 0), 4)
                with sp.Fori(0, FC - 1) as c:
                    for k, w in enumerate((wg, wu)):
                        for half in range(2):
                            load(base + 4 + 2 * k + half, turn + c, cols(w, half, (c + 1) * 512), 4)
                    for half in range(2):
                        load(base + 8 + half, turn + c, rows(wd, c * 512 + half * 256), 2)
                for half in range(2):
                    load(base + 4 + half, turn + FC - 1, rows(wd, (FC - 1) * 512 + half * 256), 2)

            ffn(U_FFN, 0, ffn_w_gate[0], ffn_w_up[0], ffn_w_down[0])
            with sp.Fori(0, 2) as i:
                for c in range(3):
                    for half in range(2):
                        load(U_SBIN + 2 * c + half, i, cols(sb_w_in[0], half, i * 1536 + c * 512), 4)
            for u in range(SBOUT_UNITS):
                load(U_SBOUT + u, 0, rows(sb_w_out[0], u * 256), 2)

            wg_all = moe_w_gate[0].rearrange("e k n -> (e k) n")
            wu_all = moe_w_up[0].rearrange("e k n -> (e k) n")
            wd_all = moe_w_down[0].rearrange("e k n -> (e k) n")

            def expert(turn, e):
                ffn(U_MOE, turn, wg_all[ds(e * D, D), :], wu_all[ds(e * D, D), :], wd_all[ds(e * FF, FF), :])

            with sp.Fori(0, NE) as e:
                expert(FC * e, e)
            sp.wait_ge(R_dve.sem, R_dve.after("ni"))
            n = sp.value_load(idi[0:1, 0:1], min_val=NE, max_val=NE + MAX_OVER)
            with sp.If(n > NE):
                with sp.Fori(NE, n) as r:
                    e = sp.value_load(idi[0:1, ds(r - (NE - 1), 1)], min_val=0, max_val=NE - 1)
                    expert(FC * r, e)
            for half in range(2):
                load(U_MOE + half, FC * n, cols(wg_all, half, 0), 4)
            sp.wait_ge(ln_dve[3].sem, ln_dve[3].after("b1"))
            sp.dma_start(out[0].rearrange("(t p) d -> p t d", p=P), X[:]).then_inc(out_done, 16)
            sp.wait_ge(out_done, 16)

        @block.gpsimd
        def _(pool):
            for ap, v in ((IDENT, 0.0), (LE, 1.0), (GT, 1.0), (LT, 1.0), (NGE, -1.0), (ONES, 1.0), (NONES, -1.0),
                          *((LEVEL[b], 1.0) for b in LEVELS)):
                nc.gpsimd.memset(ap, v).then_inc(cst_step, 1)
            nc.gpsimd.memset(zeros[:].bitcast(F32), 0.0).then_inc(cst_step, 1)
            n = 8 + len(LEVELS)
            nc.gpsimd.iota(iota[:], pattern=[[1, P]], base=0, channel_multiplier=0,
                           allow_small_or_imprecise_dtypes=True).then_inc(cst_step, 1)
            n += 1
            pool.wait_ge(cst_step, n)

            def cut(ap, pattern, base, cm, op, fill=0.0):
                nc.gpsimd.affine_select(out=ap, in_=ap, compare_op=op, fill=fill, base=base, pattern=pattern,
                                        channel_multiplier=cm).then_inc(cst_step, 1)

            cut(IDENT, [[-1, P]], 0, 1, ALU.not_equal, 1.0)
            cut(LE, [[1, P]], 0, -1, ALU.is_ge)
            cut(GT, [[-1, P]], 0, 1, ALU.is_gt)
            cut(LT, [[1, P]], 0, -1, ALU.is_gt)
            cut(NGE, [[-1, P]], 0, 1, ALU.is_ge)
            n += 5
            for b in LEVELS:
                v = LEVEL[b].rearrange("p (n h b) -> p n h b", h=2, b=b)
                nc.gpsimd.memset(v[:, :, 1, :], 0.0).then_inc(cst_step, 1)
                cut(v[:, :, 0, :], [[-2 * b, P // (2 * b)], [0, b]], -b, 1, ALU.is_ge)
                n += 2
            pool.wait_ge(cst_step, n)
            for b in LEVELS:
                v = LEVEL[b].rearrange("p (n h b) -> p n h b", h=2, b=b)
                cut(v[:, :, 0, :], [[2 * b, P // (2 * b)], [0, b]], 2 * b - 1, -1, ALU.is_ge)
                n += 1
            assert n == CST
            pool.wait_ge(cst_step, CST)

            for h0 in (0, QK):
                pool.wait_ge(S_dve.sem, S_dve.after("rq" if h0 == 0 else "rs"))
                v = tok[:, h0:h0 + QK]
                nc.gpsimd.tensor_tensor(v, v, rsn[:, h0:h0 + QK].unsqueeze(3).broadcast_to([P, QK, NT, P]), ALU.mult)\
                  .then_inc(S_pool.sem, 1)

            pool.wait_ge(S_dve.sem, S_dve.after("g"))
            pool.wait_ge(unit_used, units(A_UNITS - 1))
            with pool.Fori(0, TURNS) as i:
                def triangle(dst, mask, v, c):
                    nc.gpsimd.tensor_tensor(dst[c], mask.unsqueeze(1).broadcast_to([P, HPG, P]),
                                            v[:, c % 2, ds(8 * i + 4 * (c // 2), HPG)].unsqueeze(2)
                                            .broadcast_to([P, HPG, P]), ALU.mult).then_inc(C_pool.sem, 1)

                pool.wait_ge(C_pe.sem, C_pe.after("O0.1", i - 1))
                for c in (0, 2):
                    triangle(Xc, LE, g, c)
                    triangle(Dc, GT, beta, c)
                for c in (1, 3):
                    triangle(Dc, GT, beta, c)
                for c in (1, 3):
                    pool.wait_ge(C_pe.sem, C_pe.after(f"AV.{c // 2}", i - 1))
                    triangle(Xc, LE, g, c)
                for b in LEVELS:
                    for c in range(LANES):
                        if b == 1:
                            pool.wait_ge(C_dve.sem, C_dve.after(f"L.{c}", i))
                        elif b == 2:
                            pool.wait_ge(C_dve.sem, C_dve.after(f"d1.{c}", i))
                            pool.wait_ge(C_pe.sem, C_pe.after(f"T1.{c}", i))
                        else:
                            pool.wait_ge(C_pe.sem, C_pe.after(f"X{b // 2}.{c}", i))
                        nc.gpsimd.tensor_tensor(Cc[c], Ec[c], LEVEL[b].unsqueeze(1).broadcast_to([P, HPG, P]),
                                                ALU.mult).then_inc(C_pool.sem, 1)
                pool.wait_ge(A_act.sem, A_act.after("tokB", 3))
                v = tok[:, ds(16 + 8 * i, 8)]
                nc.gpsimd.tensor_tensor(v, v, beta[:, :, ds(8 * i, 8)].rearrange("p t h -> p h t").unsqueeze(3)
                                        .broadcast_to([P, 8, NT, P]), ALU.mult).then_inc(C_pool.sem, 1)
                zv = zs[:, ds(i, 1), :].rearrange("p t (h d) -> p (t h) d", d=P)
                nc.gpsimd.tensor_tensor(zv, zv, nw[:].unsqueeze(1).broadcast_to([P, VH, P]), ALU.mult)\
                  .then_inc(C_pool.sem, 1)
                for grp in range(GROUPS):
                    pool.wait_ge(C_pe.sem, C_pe.after(f"U64.{2 * grp}", i))
                    kq = tok[:, ds(QK + 4 * i + QPG * grp, QPG), 0, :]
                    nc.gpsimd.tensor_tensor(Dc[2 * grp].rearrange("p (q r) d -> p q r d", r=2),
                                            kq.unsqueeze(2).broadcast_to([P, QPG, 2, P]),
                                            kdec[:, ds(8 * i + 4 * grp, HPG)].rearrange("p (q r) -> p q r", r=2)
                                            .unsqueeze(3).broadcast_to([P, QPG, 2, P]), ALU.mult).then_inc(C_pool.sem, 1)

            pool.wait_ge(O_dve.sem, O_dve.after("rs"))
            pool.wait_ge(C_pool.sem, C_pool.after("zn", TURNS - 1))
            o1 = tok[:, 16:32, 1, :]
            nc.gpsimd.tensor_tensor(o1, o1, rsn[:, :, 1].unsqueeze(2).broadcast_to([P, VH, P]), ALU.mult)\
              .then_inc(O_pool.sem, 1)
            pool.wait_ge(O_pool.sem, O_pool.after("n"))
            nc.gpsimd.tensor_tensor(o1, o1, zs[:, 1, :].rearrange("p (h d) -> p h d", d=P), ALU.mult)\
              .then_inc(O_pool.sem, 1)
        @block.scalar
        def _(act):
            act.sem_inc(A_act.sem, A_act.lead)
            act.sem_inc(B_act.sem, B_act.lead)
            act.sem_inc(C_act.sem, C_act.lead)
            for S in (dense, moe):
                act.sem_inc(S["s"], 1)
                act.sem_inc(S["hh"], 1)
            act.dma_start(baw, gdn_w_in[0, :, BA0:BA0 + 32].rearrange("(k p) n -> p k n", p=P)).then_inc(small_in, 16)
            act.dma_start(cwr, gdn_conv_w[0].rearrange("j (c p) -> (j c) p", p=P)).then_inc(small_in, 16)
            act.dma_start(dtb[:], gdn_dt_bias[0].partition_broadcast(P)).then_inc(small_in, 16)
            act.dma_start(negA[:], gdn_a_log[0].partition_broadcast(P)).then_inc(small_in, 16)
            act.dma_start(nw[:], gdn_norm_w[0].partition_broadcast(P)).then_inc(small_in, 16)
            act.dma_start(rw[:], moe_router[0].rearrange("(k p) n -> p k n", p=P)).then_inc(small_in, 16)

            def hi(j, turn=0):
                act.wait_ge(raw_in[j % RAW], 16 * (turn + j // RAW + 1))
                act.wait_ge(unit_used, units(j - SPLIT, turn))
                nc.scalar.activation(unit_hi(j), raw[:, j % RAW, :], ACT.Copy).then_inc(hi_done, 1)

            def transposed(k, th, bank):
                for q in range(4):
                    act.wait_ge(xt_pe, 4 * k + q + 1)
                    nc.scalar.activation(th[:, 2 * q:2 * q + 2, :].rearrange("p a b -> p (a b)"), ps[:, bank + q, :],
                                         ACT.Copy).then_inc(xt_hi, 1)

            def layer_norm(k):
                for t in range(NT):
                    act.wait_ge(ln_dve[k].sem, ln_dve[k].after(f"ag{t}"))
                    nc.scalar.activation(sdev[:, t], mv[:, t, 1:2], ACT.Sqrt, bias=LN_EPS).then_inc(ln_act[k].sem, 1)

            def load_ln(k):
                act.dma_start(lnrow[:, 0, :], ln_g[k // 2, k % 2].partition_broadcast(P)).then_inc(ln_in, 16)
                act.dma_start(lnrow[:, 1, :], ln_b[k // 2, k % 2].partition_broadcast(P)).then_inc(ln_in, 16)

            act.wait_ge(small_in, SMALL)
            nc.scalar.activation(bah[:], baw, ACT.Copy).then_inc(S_act.sem, 1)
            nc.scalar.activation(rwh[:], rw[:], ACT.Copy).then_inc(R_act.sem, 1)
            transposed(0, xT0h, 0)

            hi(0)
            hi(1)
            def first_tap(c, i):
                act.wait_ge(S_dve.sem, S_dve.after("cw"))
                act.wait_ge(A_pe.sem, A_pe.after("t1" + "AB"[c], i))
                for m in range(4):
                    last = nc.scalar.activation(cacc[:, c, m, :], ps[:, 4 + 2 * c + m // 2, (m % 2) * SEQ:(m % 2 + 1) * SEQ],
                                                ACT.Copy, scale=cw[:, ds(3 * 32 + i * 8 + 4 * c + m, 1)])
                last.then_inc(A_act.sem, 1)

            def silu(c, i):
                act.wait_ge(A_dve.sem, A_dve.after("03" + "AB"[c], i))
                nc.scalar.activation(cacc[:, c], cacc[:, c], ACT.Silu).then_inc(A_act.sem, 1)

            def by_token(c, i):
                act.wait_ge(A_pe.sem, A_pe.after("t2" + "AB"[c], i))
                nc.scalar.activation(tok[:, ds(i * 8 + 4 * c, 4), :, :],
                                     ps[:, 4 + 2 * c:6 + 2 * c, :].rearrange("p t (m d) -> p m t d", d=P),
                                     ACT.Copy).then_inc(A_act.sem, 1)

            def project(i, first=False):
                if not first:
                    silu(0, i - 1)
                hi(2, i)
                if not first:
                    first_tap(1, i - 1)
                    by_token(0, i - 1)
                hi(3, i)
                if not first:
                    silu(1, i - 1)
                hi(4, i)
                hi(5, i)
                if not first:
                    by_token(1, i - 1)
                act.wait_ge(unit_used, units(1, i))
                nc.scalar.activation(pre[:, 0], ps[:, 0:2, :], ACT.Copy).then_inc(A_act.sem, 1)
                hi(6, i)
                first_tap(0, i)
                act.wait_ge(unit_used, units(3, i))
                nc.scalar.activation(pre[:, 1], ps[:, 2:4, :], ACT.Copy).then_inc(A_act.sem, 1)
                hi(7, i)
                act.wait_ge(unit_used, units(5, i))
                nc.scalar.activation(zs[:, :, ds(i * 512, 512)], ps[:, 0:2, :], ACT.Silu).then_inc(A_act.sem, 1)

            project(0, True)
            act.wait_ge(S_dve.sem, S_dve.after("ba"))
            nc.scalar.activation(beta[:], ba[:, :, 0:VH], ACT.Exp, scale=-1.0).then_inc(S_act.sem, 1)
            act.wait_ge(S_dve.sem, S_dve.after("xdt"))
            nc.scalar.activation(axdt[:], xdt[:], ACT.Abs).then_inc(S_act.sem, 1)
            act.wait_ge(S_act.sem, S_act.after("ax"))
            nc.scalar.activation(axdt[:], axdt[:], ACT.Exp, scale=-1.0).then_inc(S_act.sem, 1)
            nc.scalar.activation(negA[:], negA[:], ACT.Exp).then_inc(S_act.sem, 1)
            act.wait_ge(S_act.sem, S_act.after("ex"))
            nc.scalar.activation(lsp[:], axdt[:], ACT.Ln, bias=1.0).then_inc(S_act.sem, 1)
            with act.Fori(1, 3) as i:
                project(i)
            act.wait_ge(A_act.sem, A_act.after("tokB", 1))
            for h in range(QK):
                for t in range(NT):
                    last = nc.scalar.activation(kT[:, h, t * P:(t + 1) * P], tok[:, h, t, :], ACT.Square,
                                                accum_out=ssq[:, h, t:t + 1])
            last.then_inc(S_act.sem, 1)
            act.wait_ge(S_act.sem, S_act.after("sq"))
            act.wait_ge(S_dve.sem, S_dve.after("sq"))
            nc.scalar.activation(rsn[:], ssq[:], ACT.Sqrt, bias=RMS_EPS).then_inc(S_act.sem, 1)
            project(3)
            silu(0, 3)
            first_tap(1, 3)
            by_token(0, 3)
            silu(1, 3)
            by_token(1, 3)

            for q, bank in enumerate((3, 0, 1, 4)):
                act.wait_ge(S_pe.sem, S_pe.after(f"qT{q}"))
                nc.scalar.activation(tok[:, 2 * q:2 * q + 2].rearrange("p h t d -> p (h t d)"), ps[:, bank, :],
                                     ACT.Copy).then_inc(S_act.sem, 1)
            act.wait_ge(S_pe.sem, S_pe.after("gl"))
            nc.scalar.activation(eg1[:], ps[:, 2, 0:VH], ACT.Exp).then_inc(S_act.sem, 1)
            nc.scalar.activation(kdec[:], ps[:, 2, VH:2 * VH], ACT.Exp).then_inc(S_act.sem, 1)

            act.wait_ge(lo_done, units(A_UNITS - 1))
            act.wait_ge(S_act.sem, S_act.after("qT3"))
            with act.Fori(0, TURNS) as i:
                act.wait_ge(C_pe.sem, C_pe.after("PQ.1", i - 1))
                nc.scalar.activation(qTc, tok[:, ds(4 * i, 4)].rearrange("p h t d -> p h (t d)"), ACT.Copy)\
                  .then_inc(C_act.sem, 1)
                for n, dst in (("df", Ec), ("dT", ETc)):
                    for c in range(LANES):
                        act.wait_ge(C_pe.sem, C_pe.after(f"{n}.{c}", i))
                        nc.scalar.activation(flat(dst[c]), ps[:, 4 + c, :], ACT.Exp).then_inc(C_act.sem, 1)
                for b in inv:
                    for c in range(LANES):
                        act.wait_ge(C_pe.sem, C_pe.after(f"X{b}.{c}", i))
                        nc.scalar.activation(flat(Xc[c]), ps[:, c, :], ACT.Copy).then_inc(C_act.sem, 1)
                    for c in range(LANES):
                        if b < 64:
                            act.wait_ge(C_pe.sem, C_pe.after(f"T{b}.{c}", i))
                            nc.scalar.activation(flat(Dc[c]), ps[:, 4 + c, :], ACT.Copy).then_inc(C_act.sem, 1)
                for n, dst, bank in (("v0", Xc, 0), ("S", Cc, 1)):
                    for grp in range(GROUPS):
                        act.wait_ge(C_pe.sem, C_pe.after(f"{n}.{grp}", i))
                        nc.scalar.activation(flat(dst[2 * grp]), ps[:, 2 * grp + bank, :], ACT.Copy).then_inc(C_act.sem, 1)
                for grp in range(GROUPS):
                    act.wait_ge(C_pe.sem, C_pe.after(f"v1.{grp}", i))
                    nc.scalar.activation(flat(Xc[2 * grp + 1]), ps[:, 2 * grp + 1, :], ACT.Copy).then_inc(C_act.sem, 1)

            act.wait_ge(C_dve.sem, C_dve.after("o1.1", TURNS - 1))
            act.wait_ge(C_pe.sem, C_pe.after("AV.1", TURNS - 1))
            for h in range(VH):
                last = nc.scalar.activation((XB, DB)[h // 8][:, (h // 4) % 2, h % 4, :], tok[:, 16 + h, 1, :], ACT.Square,
                                            accum_out=ssq[:, h, 1:2])
            last.then_inc(O_act.sem, 1)
            act.wait_ge(O_act.sem, O_act.after("sq"))
            act.wait_ge(O_dve.sem, O_dve.after("sq"))
            nc.scalar.activation(rsn[:], ssq[:], ACT.Sqrt, scale=1.0 / P, bias=RMS_EPS).then_inc(O_act.sem, 1)
            for q in range(8):
                act.wait_ge(O_pe.sem, O_pe.after(f"t{q}"))
                nc.scalar.activation(oTh[:, 2 * q:2 * q + 2, :].rearrange("p a b -> p (a b)"), ps[:, q, :], ACT.Copy)\
                  .then_inc(O_act.sem, 1)
            act.wait_ge(O_pe.sem, O_pe.after("t7"))
            load_ln(0)
            for u in range(OUT_UNITS):
                hi(U_OUT + 2 + u)
            layer_norm(0)

            def ffn(base, turn, S, done, tiles, g_bank, t_bank, hs, hTh):
                def silu(n, gate):
                    act.wait_ge(unit_used, gate)
                    act.wait_ge(S["t"], n + 1)
                    nc.scalar.activation(hs[:], ps[:, g_bank:g_bank + tiles, :], ACT.Silu).then_inc(S["s"], 1)

                def hidden(n):
                    act.wait_ge(S["t"], n + 2)
                    nc.scalar.activation(hTh[:].rearrange("p t m d -> p t (m d)"), ps[:, t_bank:t_bank + tiles, :],
                                         ACT.Copy).then_inc(S["hh"], 1)

                hi(base + 2, turn)
                hi(base + 3, turn)
                silu(done, units(base + 1, turn))
                hi(base + 4, turn)
                hi(base + 5, turn)
                hidden(done)
                with act.Fori(0, FC - 1) as c:
                    hi(base + 6, turn + c)
                    hi(base + 7, turn + c)
                    hi(base + 8, turn + c)
                    silu(done + c + 1, units(base + 5, turn + c))
                    hi(base + 9, turn + c)
                    hi(base + 10, turn + c)
                    hi(base + 11, turn + c)
                    hidden(done + c + 1)
                return turn + FC - 1

            transposed(1, xTh, 4)
            act.wait_ge(ln_dve[0].sem, ln_dve[0].after("b1"))
            load_ln(1)
            end = ffn(U_FFN, 0, dense, 0, NT, 0, 2, hs0, hTh0)
            hi(U_FFN + 6, end)
            hi(U_FFN + 7, end)
            layer_norm(1)

            transposed(2, xTh, 0)
            act.wait_ge(ln_dve[1].sem, ln_dve[1].after("b1"))
            load_ln(2)
            with act.Fori(0, 2) as i:
                for c, (bank, ahead) in enumerate(((4, (2, 3)), (6, (4,)), (0, (5, 6)))):
                    for j in ahead:
                        hi(U_SBIN + j, i)
                    act.wait_ge(unit_used, units(U_SBIN + 2 * c + 1, i))
                    nc.scalar.activation(qkv[:, :, ds(i * 1536 + c * 512, 512)], ps[:, bank:bank + 2, :], ACT.Copy)\
                      .then_inc(B_act.sem, 1)
                hi(U_SBIN + 7, i)

            for grp in range(2):
                act.wait_ge(T_pe.sem, T_pe.after("q", grp))
                nc.scalar.activation(qTs[:], ps[:, 0:4, 0:SEQ], ACT.Copy, scale=SCALE).then_inc(T_act.sem, 1)
                act.wait_ge(T_pe.sem, T_pe.after("z", grp))
                nc.scalar.activation(spl[:], ps[:, 0:4, 0:384], ACT.Abs).then_inc(T_act.sem, 1)
                act.wait_ge(T_act.sem, T_act.after("a", grp))
                nc.scalar.activation(spl[:], spl[:], ACT.Exp, scale=-1.0).then_inc(T_act.sem, 1)
                act.wait_ge(T_act.sem, T_act.after("e", grp))
                nc.scalar.activation(spl[:], spl[:], ACT.Ln, bias=1.0).then_inc(T_act.sem, 1)
                act.wait_ge(T_dve.sem, T_dve.after("mn", grp))
                nc.scalar.activation(att[:], att[:], ACT.Exp).then_inc(T_act.sem, 1)
                act.wait_ge(T_pe.sem, T_pe.after("o", grp))
                nc.scalar.activation(aTh[:, 4 * grp:4 * grp + 4, :], ps[:, 4:8, 0:SEQ], ACT.Copy).then_inc(T_act.sem, 1)
            for u in range(SBOUT_UNITS):
                hi(U_SBOUT + 2 + u)
            layer_norm(2)

            transposed(3, xTh, 4)
            act.wait_ge(ln_dve[2].sem, ln_dve[2].after("b1"))
            load_ln(3)
            act.wait_ge(R_dve.sem, R_dve.after("df"))
            nc.scalar.activation(rs["ex"][:], rs["df"][:], ACT.Exp).then_inc(R_act.sem, 1)
            nc.scalar.activation(Xh[:], X[:], ACT.Copy).then_inc(R_act.sem, 1)

            def gathered(r):
                act.wait_ge(K_pe.sem, K_pe.after("hi", r))
                nc.scalar.activation(xeh[:].rearrange("p k s -> p (k s)"), ps[:, 5:7, :].rearrange("p b n -> p (b n)"),
                                     ACT.Copy).then_inc(K_act.sem, 1)

            def slots(r):
                act.wait_ge(K_pe.sem, K_pe.after("tr", r))
                nc.scalar.activation(GTr[:], ps[:, 1, 0:SEQ], ACT.Copy).then_inc(K_act.sem, 1)

            gathered(0)
            slots(0)
            act.wait_ge(R_dve.sem, R_dve.after("ni"))
            n = act.value_load(idi[0:1, 0:1], min_val=NE, max_val=NE + MAX_OVER)
            with act.Fori(0, n) as r:
                end = ffn(U_MOE, FC * r, moe, FC * r, 1, 0, 4, hs1, hTh1)
                gathered(r + 1)
                hi(U_MOE + 6, end)
                act.wait_ge(unit_used, units(U_MOE + 5, end))
                nc.scalar.activation(Yh[:], ps[:, 2:4, :].rearrange("p b n -> p (b n)"), ACT.Copy).then_inc(yh_done, 1)
                hi(U_MOE + 7, end)
                act.wait_ge(scattered, r + 1)
                slots(r + 1)
            layer_norm(3)

        @block.tensor
        def _(pe):
            pe.sem_inc(unit_used, CREDIT)
            pe.sem_inc(C_pe.sem, C_pe.lead)
            for S in (dense, moe):
                pe.sem_inc(S["t"], 1)

            def split3(o, lh, ll, rh, rl, start, stop):
                nc.tensor.matmul(o, lh, rh, start=start, stop=False, skip_group_check=True)
                nc.tensor.matmul(o, lh, rl, start=False, stop=False, skip_group_check=True)
                return nc.tensor.matmul(o, ll, rh, start=False, stop=stop, skip_group_check=True)

            def wide(j, turn, half, banks, xh, xl):
                pe.wait_ge(lo_done, units(j, turn))
                for t, bank in enumerate(banks):
                    for k in range(4):
                        kk, w = half * 4 + k, slice(k * 512, (k + 1) * 512)
                        last = split3(ps[:, bank, :], xh[:, kk, t * P:(t + 1) * P], xl[:, kk, t * P:(t + 1) * P],
                                      unit_hi(j)[:, w], unit_lo(j)[:, w], kk == 0, kk == KD - 1)
                return last.then_inc(unit_used, 1)

            def deep(j, turn, banks, lhs, start, stop):
                pe.wait_ge(lo_done, units(j, turn))
                for t, bank in enumerate(banks):
                    for half in range(2):
                        for k in range(2):
                            w = slice(k * D + half * 512, k * D + half * 512 + 512)
                            lh, ll = lhs(t, k)
                            last = split3(ps[:, bank + half, :], lh, ll, unit_hi(j)[:, w], unit_lo(j)[:, w],
                                          start and k == 0, stop and k == 1)
                return last.then_inc(unit_used, 1)

            def transpose_x(bank):
                for q in range(4):
                    for k in range(2):
                        for t in range(NT):
                            c = (2 * q + k) * P
                            last = nc.tensor.transpose(ps[:, bank + q, k * SEQ + t * P:k * SEQ + t * P + P],
                                                       X[:, t, c:c + P], IDENT)
                    last.then_inc(xt_pe, 1)

            pe.wait_ge(cst_step, CST)
            pe.wait_ge(x_in, 16)
            transpose_x(0)
            pe.wait_ge(small_in, SMALL)
            nc.tensor.transpose(ps[:, 4, 0:P], cwr, IDENT).then_inc(S_pe.sem, 1)
            pe.wait_ge(xt_lo, 4)
            pe.wait_ge(S_dve.sem, S_dve.after("bal"))
            for t in range(NT):
                for k in range(KD):
                    last = split3(ps[:, 5, t * 32:t * 32 + 32], xT0h[:, k, t * P:(t + 1) * P], xT0l[:, k, t * P:(t + 1) * P],
                                  bah[:, k, :], bal[:, k, :], k == 0, k == KD - 1)
            last.then_inc(S_pe.sem, 1)
            pe.wait_ge(S_dve.sem, S_dve.after("ba"))

            def to_channels(c, i):
                pe.wait_ge(A_act.sem, A_act.after("pre" + "AB"[c], i))
                pe.wait_ge(A_act.sem, A_act.after("tok" + "AB"[c], i - 1))
                for m in range(4):
                    for t in range(NT):
                        o = (m % 2) * SEQ + t * P
                        last = nc.tensor.transpose(ps[:, 4 + 2 * c + m // 2, o:o + P], pre[:, c, t, m * P:(m + 1) * P],
                                                   IDENT)
                last.then_inc(A_pe.sem, 1)

            def to_tokens(c, i):
                pe.wait_ge(A_act.sem, A_act.after("silu" + "AB"[c], i))
                for t in range(NT):
                    for m in range(4):
                        last = nc.tensor.transpose(ps[:, 4 + 2 * c + t, m * P:(m + 1) * P], cacc[:, c, m, t * P:(t + 1) * P],
                                                   IDENT)
                last.then_inc(A_pe.sem, 1)

            def project(i, first=False):
                pe.wait_ge(A_act.sem, A_act.after("z", i - 1))
                wide(0, i, 0, (0, 1), xT0h, xT0l)
                if not first:
                    to_tokens(0, i - 1)
                wide(1, i, 1, (0, 1), xT0h, xT0l)
                pe.wait_ge(A_act.sem, A_act.after("preB", i - 1))
                wide(2, i, 0, (2, 3), xT0h, xT0l)
                if not first:
                    to_tokens(1, i - 1)
                wide(3, i, 1, (2, 3), xT0h, xT0l)
                to_channels(0, i)
                wide(4, i, 0, (0, 1), xT0h, xT0l)
                wide(5, i, 1, (0, 1), xT0h, xT0l)
                to_channels(1, i)

            project(0, True)
            with pe.Fori(1, 4) as i:
                project(i)

            def turned(name, h0, bank):
                for h in range(2):
                    for t in range(NT):
                        o = h * SEQ + t * P
                        last = nc.tensor.transpose(ps[:, bank, o:o + P], tok[:, h0 + h, t, :], IDENT)
                last.then_inc(S_pe.sem, 1)

            pe.wait_ge(S_dve.sem, S_dve.after("g"))
            nc.tensor.matmul(ps[:, 2, 0:VH], LE, g[:, 1, :], start=True, stop=True).then_inc(S_pe.sem, 1)
            nc.tensor.matmul(ps[:, 2, VH:2 * VH], GT, g[:, 0, :], start=True, stop=True).then_inc(S_pe.sem, 1)
            pe.wait_ge(S_pool.sem, S_pool.after("kn"))
            turned("kT0", 8, 3)
            pe.wait_ge(A_act.sem, A_act.after("z", 3))
            turned("kT1", 10, 0)
            turned("kT2", 12, 1)
            to_tokens(0, 3)
            pe.wait_ge(A_act.sem, A_act.after("tokA", 3))
            turned("kT3", 14, 5)
            for q, bank in enumerate((3, 0, 1, 4)):
                if q < 3:
                    pe.wait_ge(S_dve.sem, S_dve.after(f"kT{q}"))
                turned(f"qT{q}", 2 * q, bank)
            to_tokens(1, 3)
            pe.wait_ge(A_act.sem, A_act.after("tokB", 3))
            pe.wait_ge(S_act.sem, S_act.after("kd"))
            pe.wait_ge(S_dve.sem, S_dve.after("kT3"))

            with pe.Fori(0, TURNS) as i:
                def heads(bank, lhs, rhs):
                    for h in range(HPG):
                        last = nc.tensor.matmul(ps[:, bank, h * P:(h + 1) * P], lhs(h), rhs(h), start=True, stop=True)
                    return last.then_inc(C_pe.sem, 1)

                def turned(bank, src):
                    for h in range(HPG):
                        last = nc.tensor.transpose(ps[:, bank, h * P:(h + 1) * P], src[:, h, :], IDENT)
                    last.then_inc(C_pe.sem, 1)

                pe.wait_ge(C_act.sem, C_act.after("cq", i))
                pe.wait_ge(C_dve.sem, C_dve.after("ck", i))
                pe.wait_ge(C_dve.sem, C_dve.after("o1.1", i - 1))
                pe.wait_ge(C_act.sem, C_act.after("v1s.1", i - 1))
                for c in range(LANES):
                    tt = slice(c % 2 * P, c % 2 * P + P)
                    for h in range(QPG):
                        kh = kTc[:, QPG * (c // 2) + h, tt]
                        nc.tensor.matmul(ps[:, c, h * P:(h + 1) * P], kh, kh, start=True, stop=True)
                        last = nc.tensor.matmul(ps[:, c, (2 + h) * P:(3 + h) * P], kh, qTc[:, QPG * (c // 2) + h, tt],
                                                start=True, stop=True)
                    last.then_inc(C_pe.sem, 1)
                for c in range(LANES):
                    pe.wait_ge(C_pool.sem, C_pool.after(f"G.{c}", i))
                    heads(4 + c, lambda h: Xc[c][:, h, :], lambda h: GT)
                for c in range(LANES):
                    pe.wait_ge(C_act.sem, C_act.after(f"e.{c}", i))
                    nc.tensor.matmul(ps[:, 4 + c, :], GT, flat(Xc[c]), start=True, stop=True).then_inc(C_pe.sem, 1)
                for c in range(LANES):
                    pe.wait_ge(C_pool.sem, C_pool.after(f"C1.{c}", i))
                    pe.wait_ge(C_act.sem, C_act.after(f"eT.{c}", i))
                    turned(4 + c, Cc[c])
                for b in inv:
                    for c in range(LANES):
                        pe.wait_ge(C_pool.sem, C_pool.after(f"C{b}.{c}", i))
                        if b == 2:
                            pe.wait_ge(C_dve.sem, C_dve.after(f"A1.{c}", i))
                            pe.wait_ge(C_dve.sem, C_dve.after(f"dt1.{c}", i))
                        else:
                            pe.wait_ge(C_dve.sem, C_dve.after(f"u{b // 2}.{c}", i))
                        heads(c, lambda h: Cc[c][:, h, :], lambda h: DTc[c][:, h, :])
                    for c in range(LANES):
                        pe.wait_ge(C_act.sem, C_act.after(f"x{b}.{c}", i))
                        if b == 2:
                            pe.wait_ge(C_dve.sem, C_dve.after(f"dt1.{c}", i))
                        else:
                            pe.wait_ge(C_act.sem, C_act.after(f"d{b // 2}.{c}", i))
                        heads(4 + c, lambda h: Dc[c][:, h, :], lambda h: Xc[c][:, h, :])
                    for c in range(LANES):
                        if b < 64:
                            pe.wait_ge(C_dve.sem, C_dve.after(f"u{b}.{c}", i))
                            turned(4 + c, DTc[c])
                pe.wait_ge(C_pool.sem, C_pool.after("vb", i))
                for grp in range(GROUPS):
                    c0 = 2 * grp
                    pe.wait_ge(C_dve.sem, C_dve.after(f"u64.{c0}", i))
                    heads(c0, lambda h: DTc[c0][:, h, :], lambda h: tok[:, ds(16 + 8 * i + HPG * grp + h, 1), 0, :]
                          .rearrange("p a d -> p (a d)"))
                for grp in range(GROUPS):
                    c0 = 2 * grp
                    pe.wait_ge(C_act.sem, C_act.after(f"v0s.{grp}", i))
                    pe.wait_ge(C_pool.sem, C_pool.after(f"kd.{grp}", i))
                    pe.wait_ge(C_dve.sem, C_dve.after("A.3", i))
                    heads(c0 + 1, lambda h: Dc[c0][:, h, :], lambda h: Xc[c0][:, h, :])
                    heads(c0, lambda h: ETc[c0][:, h, :], lambda h: Xc[c0][:, h, :])
                for grp in range(GROUPS):
                    c0 = 2 * grp
                    pe.wait_ge(C_dve.sem, C_dve.after(f"u64.{c0 + 1}", i))
                    pe.wait_ge(C_act.sem, C_act.after(f"Ss.{grp}", i))
                    heads(4 + c0, lambda h: kTc[:, QPG * grp + h // 2, P:SEQ], lambda h: Cc[c0][:, h, :])
                    heads(5 + c0, lambda h: qTc[:, QPG * grp + h // 2, P:SEQ], lambda h: Cc[c0][:, h, :])
                for grp in range(GROUPS):
                    c0 = 2 * grp
                    pe.wait_ge(C_dve.sem, C_dve.after(f"r.{grp}", i))
                    heads(c0 + 1, lambda h: DTc[c0 + 1][:, h, :], lambda h: Cc[c0 + 1][:, h, :])
                for grp in range(GROUPS):
                    c0 = 2 * grp
                    pe.wait_ge(C_act.sem, C_act.after(f"v1s.{grp}", i))
                    heads(c0, lambda h: ETc[c0 + 1][:, h, :], lambda h: Xc[c0 + 1][:, h, :])

            pe.wait_ge(C_dve.sem, C_dve.after("o1.1", TURNS - 1))
            pe.wait_ge(O_dve.sem, O_dve.after("z"))
            pe.wait_ge(O_pool.sem, O_pool.after("z"))
            for c in range(8):
                for h in range(2):
                    for t in range(NT):
                        o = h * SEQ + t * P
                        last = nc.tensor.transpose(ps[:, c, o:o + P], tok[:, 16 + 2 * c + h, t, :], IDENT)
                last.then_inc(O_pe.sem, 1)
            pe.wait_ge(O_dve.sem, O_dve.after("l7"))
            for u in range(OUT_UNITS):
                deep(U_OUT + u, 0, (0, 2), lambda t, k: (oTh[:, 2 * u + k, t * P:(t + 1) * P],
                                                         oTl[:, 2 * u + k, t * P:(t + 1) * P]), u == 0, u == OUT_UNITS - 1)

            def ffn(base, turn, S, done, xh, xl, hs, hTh, hTl, g_banks, u_banks, t_banks, y_banks, before_last=None):
                tiles = range(len(g_banks))

                def chunk(j, turn, n, down):
                    pe.wait_ge(S["s"], n + 1)
                    wide(j, turn, 0, g_banks, xh, xl)
                    wide(j + 1, turn, 1, g_banks, xh, xl)
                    pe.wait_ge(S["h"], n + 1)
                    if u_banks == t_banks:
                        pe.wait_ge(S["hl"], n + 1)
                    wide(j + 2, turn, 0, u_banks, xh, xl)
                    wide(j + 3, turn, 1, u_banks, xh, xl)
                    if down:
                        down_units(j + 4, turn, n)
                    pe.wait_ge(S["h"], n + 2)
                    pe.wait_ge(S["hl"], n + 1)
                    for t in tiles:
                        for m in range(4):
                            last = nc.tensor.transpose(ps[:, t_banks[t], m * P:(m + 1) * P], hs[:, t, m * P:(m + 1) * P],
                                                       IDENT)
                    last.then_inc(S["t"], 1)

                def down_units(j, turn, n):
                    pe.wait_ge(S["hl"], n + 1)
                    for half in range(2):
                        deep(j + half, turn, y_banks,
                             lambda t, k: (hTh[:, t, 2 * half + k, :], hTl[:, t, 2 * half + k, :]), False, False)

                chunk(base, turn, done, False)
                for bank in y_banks:
                    for half in range(2):
                        nc.tensor.matmul(ps[:, bank + half, :], zeros[:, 0:P], zeros[:], start=True, stop=True)
                with pe.Fori(0, FC - 1) as c:
                    chunk(base + 4, turn + c, done + c + 1, True)
                if before_last:
                    before_last()
                down_units(base + 4, turn + FC - 1, done + FC)

            pe.wait_ge(ln_dve[0].sem, ln_dve[0].after("b1"))
            transpose_x(4)
            pe.wait_ge(xt_lo, 8)
            ffn(U_FFN, 0, dense, 0, xTh, xTl, hs0, hTh0, hTl0, (0, 1), (2, 3), (2, 3), (4, 6))

            pe.wait_ge(ln_dve[1].sem, ln_dve[1].after("b1"))
            transpose_x(0)
            pe.wait_ge(xt_lo, 12)
            with pe.Fori(0, 2) as i:
                for c, bank in enumerate((4, 6, 0)):
                    pe.wait_ge(B_act.sem, B_act.after(f"c{c}", i - 1))
                    wide(U_SBIN + 2 * c, i, 0, (bank, bank + 1), xTh, xTl)
                    wide(U_SBIN + 2 * c + 1, i, 1, (bank, bank + 1), xTh, xTl)

            pe.wait_ge(B_act.sem, B_act.after("c2", 1))
            for grp in range(2):
                for part, b0 in ((0, 0), (1, 4)):
                    if grp and part:
                        pe.wait_ge(T_act.sem, T_act.after("oh", 0))
                        pe.wait_ge(T_dve.sem, T_dve.after("ol", 0))
                    for h in range(4):
                        for t in range(NT):
                            c = part * D + (4 * grp + h) * P
                            last = nc.tensor.transpose(ps[:, b0 + h, t * P:(t + 1) * P], qkv[:, t, c:c + P], IDENT)
                    last.then_inc(T_pe.sem, 1)
                pe.wait_ge(T_act.sem, T_act.after("q", grp))
                pe.wait_ge(T_dve.sem, T_dve.after("k", grp))
                for h in range(4):
                    nc.tensor.matmul(ps[:, h, 0:SEQ], kTs[:, h, 0:P], qTs[:, h, :], start=True, stop=False,
                                     skip_group_check=True)
                    last = nc.tensor.matmul(ps[:, h, SEQ:384], kTs[:, h, P:SEQ], qTs[:, h, P:SEQ], start=False, stop=False,
                                            skip_group_check=True)
                last.then_inc(T_pe.sem, 1)
                pe.wait_ge(T_dve.sem, T_dve.after("m1", grp))
                for h in range(4):
                    nc.tensor.matmul(ps[:, h, 0:SEQ], NGE, spl[:, h, 0:SEQ], start=False, stop=False, skip_group_check=True)
                    nc.tensor.matmul(ps[:, h, P:SEQ], NONES, spl[:, h, SEQ:384], start=False, stop=False,
                                     skip_group_check=True)
                    last = nc.tensor.matmul(ps[:, h, SEQ:384], NGE, spl[:, h, SEQ:384], start=False, stop=True,
                                            skip_group_check=True)
                last.then_inc(T_pe.sem, 1)
                pe.wait_ge(T_dve.sem, T_dve.after("n1", grp))
                for h in range(4):
                    c = 2 * D + (4 * grp + h) * P
                    nc.tensor.matmul(ps[:, 4 + h, 0:SEQ], qkv[:, 0, c:c + P], att[:, h, 0:SEQ], start=True, stop=False,
                                     skip_group_check=True)
                    last = nc.tensor.matmul(ps[:, 4 + h, P:SEQ], qkv[:, 1, c:c + P], att[:, h, SEQ:384], start=False,
                                            stop=True, skip_group_check=True)
                last.then_inc(T_pe.sem, 1)
            pe.wait_ge(T_act.sem, T_act.after("oh", 1))
            pe.wait_ge(T_dve.sem, T_dve.after("ol", 1))
            for u in range(SBOUT_UNITS):
                deep(U_SBOUT + u, 0, (0, 2), lambda t, k: (aTh[:, 2 * u + k, t * P:(t + 1) * P],
                                                           aTl[:, 2 * u + k, t * P:(t + 1) * P]),
                     u == 0, u == SBOUT_UNITS - 1)

            pe.wait_ge(ln_dve[2].sem, ln_dve[2].after("b1"))
            transpose_x(4)
            pe.wait_ge(xt_lo, 16)
            pe.wait_ge(R_dve.sem, R_dve.after("rwl"))
            for t in range(NT):
                for k in range(KD):
                    last = split3(ps[:, 0, t * NE:(t + 1) * NE], xTh[:, k, t * P:(t + 1) * P], xTl[:, k, t * P:(t + 1) * P],
                                  rwh[:, k, :], rwl[:, k, :], k == 0, k == KD - 1)
            last.then_inc(R_pe.sem, 1)
            pe.wait_ge(R_dve.sem, R_dve.after("mask"))
            mask = rt["mask"]
            nc.tensor.matmul(ps[:, 1, 0:NE], LT, mask[:, 0, :], start=True, stop=True)
            nc.tensor.matmul(ps[:, 1, NE:2 * NE], LT, mask[:, 1, :], start=True, stop=False)
            nc.tensor.matmul(ps[:, 1, NE:2 * NE], ONES, mask[:, 0, :], start=False, stop=True)
            nc.tensor.matmul(ps[:, 1, 2 * NE:3 * NE], ONES, mask[:, 0, :], start=True, stop=False)
            nc.tensor.matmul(ps[:, 1, 2 * NE:3 * NE], ONES, mask[:, 1, :], start=False, stop=True).then_inc(R_pe.sem, 1)

            def gather(r):
                pe.wait_ge(K_dve.sem, K_dve.after("s1", r))
                for part, (src, banks) in enumerate(((Xh, (5, 6)), (Xl, (7, 0)))):
                    for k in range(KD):
                        o = ps[:, banks[k // 4], (k % 4) * P:(k % 4 + 1) * P]
                        for t in range(NT):
                            last = nc.tensor.matmul(o, src[:, t, k * P:(k + 1) * P], G[:, t, :], start=t == 0,
                                                    stop=t == NT - 1)
                    last.then_inc(K_pe.sem, 1)
                for t in range(NT):
                    last = nc.tensor.transpose(ps[:, 1, t * P:(t + 1) * P], G[:, t, :].bitcast(F32), IDENT)
                last.then_inc(K_pe.sem, 1)

            pe.wait_ge(R_dve.sem, R_dve.after("ni"))
            pe.wait_ge(R_act.sem, R_act.after("xh"))
            pe.wait_ge(R_dve.sem, R_dve.after("xl"))
            n = pe.value_load(idi[0:1, 0:1], min_val=NE, max_val=NE + MAX_OVER)
            gather(0)
            with pe.Fori(0, n) as r:
                pe.wait_ge(K_act.sem, K_act.after("gt", r))
                pe.wait_ge(K_dve.sem, K_dve.after("l0", r))
                pe.wait_ge(added, NT * r + 1)

                def next_rows():
                    pe.wait_ge(moe["s"], FC * (r + 1) + 1)
                    gather(r + 1)

                ffn(U_MOE, FC * r, moe, FC * r, xeh, xel, hs1, hTh1, hTl1, (0,), (1,), (4,), (2,), next_rows)
                pe.wait_ge(yl_done, r + 1)
                pe.wait_ge(K_act.sem, K_act.after("hi", r + 1))
                pe.wait_ge(K_dve.sem, K_dve.after("l7", r + 1))
                for t in range(NT):
                    for half in range(2):
                        w = slice(half * 512, half * 512 + 512)
                        o = ps[:, 4 + 2 * t + half, :]
                        nc.tensor.matmul(o, GTr[:, t * P:(t + 1) * P], Yh[:, w], start=True, stop=False)
                        last = nc.tensor.matmul(o, GTr[:, t * P:(t + 1) * P], Yl[:, w], start=False, stop=True)
                last.then_inc(scattered, 1)

        @block.vector
        def _(dve):
            V = nc.vector
            dve.sem_inc(lo_done, CREDIT)
            dve.sem_inc(C_dve.sem, C_dve.lead)
            dve.sem_inc(added, 1)
            for S in (dense, moe):
                dve.sem_inc(S["h"], 1)
                dve.sem_inc(S["hl"], 1)

            def lo(j, turn=0):
                dve.wait_ge(hi_done, j + 6 * turn + 1)
                V.tensor_tensor(unit_lo(j), raw[:, j % RAW, :], unit_hi(j).bitcast(F32), ALU.subtract).then_inc(lo_done, 1)

            def transposed(k, th, tl, bank):
                for q in range(4):
                    dve.wait_ge(xt_hi, 4 * k + q + 1)
                    v = slice(2 * q, 2 * q + 2)
                    V.tensor_tensor(tl[:, v, :].rearrange("p a b -> p (a b)"), ps[:, bank + q, :],
                                    th[:, v, :].rearrange("p a b -> p (a b)").bitcast(F32), ALU.subtract).then_inc(xt_lo, 1)

            def layer_norm(k, y_bank):
                L, A = ln_dve[k], ln_act[k]
                for t in range(NT):
                    if y_bank is not None:
                        V.scalar_tensor_tensor(out=X[:, t], in0=X[:, t], scalar=ALPHA,
                                               in1=ps[:, y_bank + 2 * t:y_bank + 2 * t + 2, :].rearrange("p b n -> p (b n)"),
                                               op0=ALU.mult, op1=ALU.add).then_inc(L.sem, 1)
                        dve.wait_ge(L.sem, L.after(f"r{t}"))
                    for h in range(2):
                        V.bn_stats(stats[:, t, h, :], X[:, t, h * 512:(h + 1) * 512]).then_inc(L.sem, 1)
                    dve.wait_ge(L.sem, L.after(f"sb{t}"))
                    V.bn_aggr(mv[:, t, :], stats[:, t]).then_inc(L.sem, 1)
                dve.wait_ge(ln_in, 32 * (k + 1))
                for t in range(NT):
                    dve.wait_ge(A.sem, A.after(f"sd{t}"))
                    V.reciprocal(rstd[:, t], sdev[:, t]).then_inc(L.sem, 1)
                    dve.wait_ge(L.sem, L.after(f"rc{t}"))
                    V.tensor_scalar(X[:, t], X[:, t], mv[:, t, 0:1], rstd[:, t], ALU.subtract, ALU.mult).then_inc(L.sem, 1)
                    dve.wait_ge(L.sem, L.after(f"n{t}"))
                    V.tensor_tensor(X[:, t], X[:, t], lnrow[:, 0, :], ALU.mult).then_inc(L.sem, 1)
                    dve.wait_ge(L.sem, L.after(f"g{t}"))
                    V.tensor_tensor(X[:, t], X[:, t], lnrow[:, 1, :], ALU.add).then_inc(L.sem, 1)

            dve.wait_ge(S_act.sem, S_act.after("bah"))
            transposed(0, xT0h, xT0l, 0)
            dve.wait_ge(S_pe.sem, S_pe.after("cw"))
            V.tensor_copy(cw[:], ps[:, 4, 0:P]).then_inc(S_dve.sem, 1)
            V.tensor_tensor(bal[:], baw, bah[:].bitcast(F32), ALU.subtract).then_inc(S_dve.sem, 1)
            dve.wait_ge(R_act.sem, R_act.after("rwh"))
            V.tensor_tensor(rwl[:], rw[:], rwh[:].bitcast(F32), ALU.subtract).then_inc(R_dve.sem, 1)
            dve.wait_ge(S_pe.sem, S_pe.after("ba"))
            V.tensor_copy(ba[:].rearrange("p t n -> p (t n)"), ps[:, 5, 0:64]).then_inc(S_dve.sem, 1)

            lo(0)
            lo(1)
            def convolve(c, i):
                for j in (2, 1, 0):
                    for m in range(4):
                        src = ps[:, 4 + 2 * c + m // 2, (m % 2) * SEQ:(m % 2 + 1) * SEQ]
                        w = cw[:, ds(j * 32 + i * 8 + 4 * c + m, 1)]
                        s = 3 - j
                        if s == 1:
                            dve.wait_ge(A_act.sem, A_act.after("c0" + "AB"[c], i))
                        else:
                            dve.wait_ge(A_dve.sem, A_dve.after(f"{j + 1}{m}" + "AB"[c], i))
                        V.scalar_tensor_tensor(out=cacc[:, c, m, s:], in0=src[:, 0:SEQ - s], scalar=w,
                                               in1=cacc[:, c, m, s:], op0=ALU.mult, op1=ALU.add)\
                         .then_inc(A_dve.sem, 1)

            def project(i, first=False):
                lo(2, i)
                if not first:
                    convolve(1, i - 1)
                for j in (3, 4, 5, 6):
                    lo(j, i)
                convolve(0, i)
                lo(7, i)

            project(0, True)
            V.tensor_tensor(xdt[:], ba[:, :, VH:2 * VH], dtb[:].unsqueeze(1).broadcast_to([P, NT, VH]), ALU.add)\
             .then_inc(S_dve.sem, 1)
            dve.wait_ge(S_act.sem, S_act.after("eb"))
            V.tensor_scalar(beta[:], beta[:], 1.0, None, ALU.add).then_inc(S_dve.sem, 1)
            dve.wait_ge(S_dve.sem, S_dve.after("b1"))
            V.reciprocal(beta[:], beta[:]).then_inc(S_dve.sem, 1)
            with dve.Fori(1, 3) as i:
                project(i)
            dve.wait_ge(S_act.sem, S_act.after("ln"))
            V.scalar_tensor_tensor(out=xdt[:], in0=xdt[:], scalar=0.0, in1=lsp[:], op0=ALU.max, op1=ALU.add)\
             .then_inc(S_dve.sem, 1)
            dve.wait_ge(S_dve.sem, S_dve.after("sp"))
            V.scalar_tensor_tensor(out=g[:], in0=xdt[:], scalar=-1.0, in1=negA[:].unsqueeze(1).broadcast_to([P, NT, VH]),
                                   op0=ALU.mult, op1=ALU.mult).then_inc(S_dve.sem, 1)
            dve.wait_ge(A_act.sem, A_act.after("tokB", 1))
            dve.wait_ge(A_pe.sem, A_pe.after("t1B", 2))
            for h in range(QK):
                for t in range(NT):
                    k = tok[:, QK + h, t, :]
                    last = V.tensor_tensor_reduce(pre[:, h // 4, t, h % 4 * P:h % 4 * P + P], k, k, 1.0, 0.0, ALU.mult,
                                                  ALU.add, ssq[:, QK + h, t:t + 1])
            last.then_inc(S_dve.sem, 1)
            dve.wait_ge(S_act.sem, S_act.after("sd"))
            V.reciprocal(rsn[:], rsn[:]).then_inc(S_dve.sem, 1)
            dve.wait_ge(S_dve.sem, S_dve.after("rs"))
            V.tensor_scalar(rsn[:, 0:QK], rsn[:, 0:QK], SCALE, None, ALU.mult).then_inc(S_dve.sem, 1)
            project(3)

            for c, bank in enumerate((3, 0, 1, 5)):
                if c == 3:
                    convolve(1, 3)
                dve.wait_ge(S_pe.sem, S_pe.after(f"kT{c}"))
                V.tensor_copy(kT[:, 2 * c:2 * c + 2, :].rearrange("p a b -> p (a b)"), ps[:, bank, :])\
                 .then_inc(S_dve.sem, 1)
            dve.wait_ge(S_act.sem, S_act.after("eg"))
            V.tensor_tensor(beg1[:], beta[:, 1, :], eg1[:], ALU.mult).then_inc(S_dve.sem, 1)

            dve.wait_ge(S_dve.sem, S_dve.after("kT3"))
            dve.wait_ge(A_act.sem, A_act.after("tokB", 3))
            with dve.Fori(0, TURNS) as i:
                dve.wait_ge(C_pe.sem, C_pe.after("PK.1", i - 1))
                V.tensor_copy(kTc[:], kT[:, ds(4 * i, 4), :]).then_inc(C_dve.sem, 1)

                def four(ap):
                    return ap.unsqueeze(1).broadcast_to([P, HPG, P])

                def pairs(ap):
                    return ap.rearrange("p (q d) -> p q d", d=P).unsqueeze(2).broadcast_to([P, QPG, 2, P])

                for c in range(LANES):
                    e4 = Ec[c].rearrange("p (q r) d -> p q r d", r=2)
                    dve.wait_ge(C_act.sem, C_act.after(f"e.{c}", i))
                    V.tensor_tensor(e4, e4, pairs(ps[:, c, 0:2 * P]), ALU.mult).then_inc(C_dve.sem, 1)
                    dve.wait_ge(C_dve.sem, C_dve.after(f"L1.{c}", i))
                    dve.wait_ge(C_pool.sem, C_pool.after(f"MB.{c}", i))
                    V.tensor_tensor(Ec[c], Ec[c], Dc[c], ALU.mult).then_inc(C_dve.sem, 1)
                for c in range(LANES):
                    t4 = ETc[c].rearrange("p (q r) d -> p q r d", r=2)
                    dve.wait_ge(C_act.sem, C_act.after(f"eT.{c}", i))
                    V.tensor_tensor(t4, t4, pairs(ps[:, c, 2 * P:4 * P]), ALU.mult).then_inc(C_dve.sem, 1)
                for c in range(LANES):
                    dve.wait_ge(C_pool.sem, C_pool.after(f"C1.{c}", i))
                    V.tensor_tensor(Dc[c], four(IDENT), Cc[c], ALU.subtract).then_inc(C_dve.sem, 1)
                    dve.wait_ge(C_pe.sem, C_pe.after(f"T1.{c}", i))
                    V.tensor_tensor(DTc[c], four(IDENT), ps[:, 4 + c, :].rearrange("p (h d) -> p h d", d=P),
                                    ALU.subtract).then_inc(C_dve.sem, 1)
                for b in inv:
                    for c in range(LANES):
                        dve.wait_ge(C_pe.sem, C_pe.after(f"U{b}.{c}", i))
                        V.tensor_tensor(flat(DTc[c]), flat(DTc[c]), ps[:, 4 + c, :], ALU.subtract).then_inc(C_dve.sem, 1)
                    if b == 2:
                        for c in range(LANES):
                            dve.wait_ge(C_dve.sem, C_dve.after(f"A1.{c}", i))
                            V.tensor_tensor(ETc[c], ETc[c], four(LE), ALU.mult).then_inc(C_dve.sem, 1)

                def o(grp, t):
                    return tok[:, ds(16 + 8 * i + HPG * grp, HPG), t, :]

                def per_head(v, grp):
                    return v[:, ds(8 * i + HPG * grp, HPG)].unsqueeze(2).broadcast_to([P, HPG, P])

                def heads(bank):
                    return ps[:, bank, :].rearrange("p (h d) -> p h d", d=P)

                for grp in range(GROUPS):
                    dve.wait_ge(C_pe.sem, C_pe.after(f"O0.{grp}", i))
                    V.tensor_copy(o(grp, 0), heads(2 * grp)).then_inc(C_dve.sem, 1)
                for grp in range(GROUPS):
                    r = Cc[2 * grp + 1]
                    dve.wait_ge(C_pe.sem, C_pe.after(f"PK.{grp}", i))
                    V.tensor_tensor(r, heads(4 + 2 * grp), per_head(beg1, grp), ALU.mult).then_inc(C_dve.sem, 1)
                for grp in range(GROUPS):
                    r = Cc[2 * grp + 1]
                    dve.wait_ge(C_dve.sem, C_dve.after(f"r1.{grp}", i))
                    V.tensor_tensor(r, o(grp, 1), r, ALU.subtract).then_inc(C_dve.sem, 1)
                for grp in range(GROUPS):
                    dve.wait_ge(C_pe.sem, C_pe.after(f"v1.{grp}", i))
                    V.tensor_tensor(Cc[2 * grp + 1], heads(5 + 2 * grp), per_head(eg1, grp), ALU.mult)\
                     .then_inc(C_dve.sem, 1)
                for grp in range(GROUPS):
                    dve.wait_ge(C_pe.sem, C_pe.after(f"AV.{grp}", i))
                    dve.wait_ge(C_dve.sem, C_dve.after(f"o1a.{grp}", i))
                    V.tensor_tensor(o(grp, 1), Cc[2 * grp + 1], heads(2 * grp), ALU.add).then_inc(C_dve.sem, 1)

            dve.wait_ge(C_dve.sem, C_dve.after("o1.1", TURNS - 1))
            for h in range(VH):
                v = tok[:, 16 + h, 0, :]
                last = V.tensor_tensor_reduce((E_, ET)[h // 8][:, (h // 4) % 2, h % 4, :], v, v, 1.0, 0.0, ALU.mult, ALU.add,
                                              ssq[:, h, 0:1])
            last.then_inc(O_dve.sem, 1)
            dve.wait_ge(O_act.sem, O_act.after("sd"))
            V.reciprocal(rsn[:], rsn[:]).then_inc(O_dve.sem, 1)
            dve.wait_ge(O_dve.sem, O_dve.after("rs"))
            dve.wait_ge(C_pool.sem, C_pool.after("zn", TURNS - 1))
            o0 = tok[:, 16:32, 0, :]
            V.tensor_tensor(o0, o0, rsn[:, :, 0].unsqueeze(2).broadcast_to([P, VH, P]), ALU.mult).then_inc(O_dve.sem, 1)
            dve.wait_ge(O_dve.sem, O_dve.after("n"))
            V.tensor_tensor(o0, o0, zs[:, 0, :].rearrange("p (h d) -> p h d", d=P), ALU.mult).then_inc(O_dve.sem, 1)
            for c in range(8):
                dve.wait_ge(O_act.sem, O_act.after(f"h{c}"))
                v = slice(2 * c, 2 * c + 2)
                V.tensor_tensor(oTl[:, v, :].rearrange("p a b -> p (a b)"), ps[:, c, :],
                                oTh[:, v, :].rearrange("p a b -> p (a b)").bitcast(F32), ALU.subtract).then_inc(O_dve.sem, 1)
            for u in range(OUT_UNITS):
                lo(U_OUT + 2 + u)
            dve.wait_ge(unit_used, units(U_OUT + OUT_UNITS - 1))
            layer_norm(0, 0)

            def ffn(base, turn, S, done, tiles, u_bank, t_bank, hs, hTh, hTl):
                def hidden(n, up):
                    dve.wait_ge(unit_used, up)
                    dve.wait_ge(S["s"], n + 2)
                    V.tensor_tensor(hs[:], hs[:], ps[:, u_bank:u_bank + tiles, :], ALU.mult).then_inc(S["h"], 1)

                def hidden_lo(n):
                    dve.wait_ge(S["hh"], n + 2)
                    V.tensor_tensor(hTl[:].rearrange("p t m d -> p t (m d)"), ps[:, t_bank:t_bank + tiles, :],
                                    hTh[:].rearrange("p t m d -> p t (m d)").bitcast(F32), ALU.subtract).then_inc(S["hl"], 1)

                lo(base + 2, turn)
                lo(base + 3, turn)
                hidden(done, units(base + 3, turn))
                lo(base + 4, turn)
                lo(base + 5, turn)
                hidden_lo(done)
                with dve.Fori(0, FC - 1) as c:
                    for j in (6, 7, 8, 9):
                        lo(base + j, turn + c)
                    hidden(done + c + 1, units(base + 7, turn + c))
                    lo(base + 10, turn + c)
                    lo(base + 11, turn + c)
                    hidden_lo(done + c + 1)
                return turn + FC - 1

            transposed(1, xTh, xTl, 4)
            end = ffn(U_FFN, 0, dense, 0, NT, 2, 2, hs0, hTh0, hTl0)
            lo(U_FFN + 6, end)
            lo(U_FFN + 7, end)
            dve.wait_ge(unit_used, units(U_FFN + FFN_UNITS - 1))
            layer_norm(1, 4)

            transposed(2, xTh, xTl, 0)
            with dve.Fori(0, 2) as i:
                for j in range(2, 8):
                    lo(U_SBIN + j, i)
            for grp in range(2):
                for_diag = LT.unsqueeze(1).broadcast_to([P, 4, P])
                dve.wait_ge(T_pe.sem, T_pe.after("k", grp))
                V.tensor_copy(kTs[:], ps[:, 4:8, 0:SEQ]).then_inc(T_dve.sem, 1)
                dve.wait_ge(T_act.sem, T_act.after("l", grp))
                V.scalar_tensor_tensor(out=spl[:], in0=ps[:, 0:4, 0:384], scalar=0.0, in1=spl[:], op0=ALU.max, op1=ALU.add)\
                 .then_inc(T_dve.sem, 1)
                dve.wait_ge(T_dve.sem, T_dve.after("sp", grp))
                for w in (slice(0, P), slice(SEQ, 384)):
                    V.tensor_tensor(spl[:, :, w], spl[:, :, w], for_diag, ALU.mult).then_inc(T_dve.sem, 1)
                dve.wait_ge(T_pe.sem, T_pe.after("R", grp))
                V.tensor_scalar(att[:], ps[:, 0:4, 0:384], 0.0, None, ALU.min).then_inc(T_dve.sem, 1)
                dve.wait_ge(T_act.sem, T_act.after("p", grp))
                for w in (slice(0, P), slice(SEQ, 384)):
                    V.tensor_tensor(att[:, :, w], att[:, :, w], for_diag, ALU.mult).then_inc(T_dve.sem, 1)
                dve.wait_ge(T_act.sem, T_act.after("oh", grp))
                V.tensor_tensor(aTl[:, 4 * grp:4 * grp + 4, :], ps[:, 4:8, 0:SEQ],
                                aTh[:, 4 * grp:4 * grp + 4, :].bitcast(F32), ALU.subtract).then_inc(T_dve.sem, 1)
            for u in range(SBOUT_UNITS):
                lo(U_SBOUT + 2 + u)
            dve.wait_ge(unit_used, units(U_SBOUT + SBOUT_UNITS - 1))
            layer_norm(2, 0)

            transposed(3, xTh, xTl, 4)

            def step(name, ins):
                ins.then_inc(R_dve.sem, 1)
                dve.wait_ge(R_dve.sem, R_dve.after(name))

            def experts(v):
                return v.broadcast_to([P, NT, NE])

            idx = iota[:, 0:NE].unsqueeze(1).broadcast_to([P, NT, NE])
            dve.wait_ge(R_pe.sem, R_pe.after("lg"))
            step("lg", V.tensor_copy(rt["lg"][:].rearrange("p t e -> p (t e)"), ps[:, 0, 0:NT * NE]))
            for lg, m, eq, ca, i_, oh, rest in (("lg", "m1", "eq1", "ca", "i1", "oh1", "l2"),
                                                ("l2", "m2", "eq2", "c2", "i2", "oh2", None)):
                step(m, V.tensor_reduce(rs[m][:], rt[lg][:], AX_X, ALU.max))
                step(eq, V.tensor_tensor(rt[eq][:], rt[lg][:], experts(rs[m][:]), ALU.is_ge))
                step(ca, V.scalar_tensor_tensor(out=rt[ca][:], in0=rt[eq][:], scalar=-99.0, in1=idx, op0=ALU.mult,
                                                op1=ALU.add))
                step(i_, V.tensor_reduce(rs[i_][:], rt[ca][:], AX_X, ALU.min))
                step(oh, V.tensor_tensor(rt[oh][:], rt[ca][:], experts(rs[i_][:]), ALU.is_equal))
                if rest:
                    step(rest, V.scalar_tensor_tensor(out=rt[rest][:], in0=rt[oh][:], scalar=-3.0e38, in1=rt[lg][:],
                                                      op0=ALU.mult, op1=ALU.add))
            step("df", V.tensor_tensor(rs["df"][:], rs["m2"][:], rs["m1"][:], ALU.subtract))
            dve.wait_ge(R_act.sem, R_act.after("ex"))
            step("sm", V.tensor_scalar(rs["sm"][:], rs["ex"][:], 1.0, None, ALU.add))
            step("p1", V.reciprocal(rs["p1"][:], rs["sm"][:]))
            step("p2", V.tensor_tensor(rs["p2"][:], rs["ex"][:], rs["p1"][:], ALU.mult))
            step("mask", V.tensor_tensor(rt["mask"][:], rt["oh1"][:], rt["oh2"][:], ALU.add))
            step("cm1", V.tensor_tensor(rt["comb"][:], rt["oh1"][:], experts(rs["p1"][:]), ALU.mult))
            step("cm2", V.tensor_tensor(rt["tmp"][:], rt["oh2"][:], experts(rs["p2"][:]), ALU.mult))
            step("comb", V.tensor_tensor(rt["comb"][:], rt["comb"][:], rt["tmp"][:], ALU.add))
            dve.wait_ge(R_pe.sem, R_pe.after("rk"))
            step("rk1", V.scalar_tensor_tensor(out=rt["rank"][:].rearrange("p t e -> p (t e)"), in0=ps[:, 1, 0:NT * NE],
                                               scalar=1.0, in1=rt["mask"][:].rearrange("p t e -> p (t e)"), op0=ALU.add,
                                               op1=ALU.mult))
            step("rk2", V.tensor_scalar(rt["rank"][:], rt["rank"][:], -1.0, None, ALU.add))
            step("cnt", V.tensor_copy(cnt[:], ps[:, 1, NT * NE:(NT + 1) * NE]))
            step("ov", V.tensor_scalar(ov[:], cnt[:], float(P), None, ALU.is_gt))
            step("z0", V.memset(ranks[:], -1.0))
            step("z1", V.memset(gates[:], 0.0))
            step("z2", V.memset(ovp[:, 0:1], 0.0))
            for e in range(1, NE):
                step(f"pre{e}", V.tensor_tensor(ovp[:, e:e + 1], ovp[:, e - 1:e], ov[:, e - 1:e], ALU.add))
            for q in range(MAX_OVER):
                iq = ind[:, q, :]
                iq2 = iq.unsqueeze(1).broadcast_to([P, NT, NE])
                step(f"in{q}", V.tensor_scalar(iq, ovp[:], float(q), None, ALU.is_equal))
                step(f"im{q}", V.tensor_tensor(iq, iq, ov[:], ALU.mult))
                rq = ranks[:, :, NE + q:NE + q + 1]
                step(f"pr{q}", V.tensor_tensor(rt["tmp"][:], rt["rank"][:], iq2, ALU.mult))
                step(f"sr{q}", V.tensor_reduce(rq, rt["tmp"][:], AX_X, ALU.add))
                step(f"ad{q}", V.tensor_scalar(rq, rq, -float(P), None, ALU.add))
                step(f"pg{q}", V.tensor_tensor(rt["tmp"][:], rt["comb"][:], iq2, ALU.mult))
                step(f"sg{q}", V.tensor_reduce(gates[:, :, NE + q:NE + q + 1], rt["tmp"][:], AX_X, ALU.add))
                step(f"pi{q}", V.tensor_tensor(iq, iq, iota[:, 0:NE], ALU.mult))
                step(f"si{q}", V.tensor_reduce(ids[:, 1 + q:2 + q], iq, AX_X, ALU.add))
            step("rt", V.tensor_copy(ranks[:, :, 0:NE], rt["rank"][:]))
            step("gt", V.tensor_copy(gates[:, :, 0:NE], rt["comb"][:]))
            step("no", V.tensor_reduce(ids[:, 0:1], ov[:], AX_X, ALU.add))
            step("nc", V.tensor_scalar(ids[:, 0:1], ids[:, 0:1], float(NE), None, ALU.add))
            step("ni", V.tensor_copy(idi[:], ids[:]))
            dve.wait_ge(R_act.sem, R_act.after("xh"))
            step("xl", V.tensor_tensor(Xl[:], X[:], Xh[:].bitcast(F32), ALU.subtract))
            dve.wait_ge(xt_pe, 16)
            step("xa", V.tensor_scalar(X[:], X[:], ALPHA, None, ALU.mult))

            def select(r):
                for t in range(NT):
                    V.tensor_scalar(G[:, t, :], iota[:], ranks[:, t, ds(r, 1)], None, ALU.is_equal).then_inc(K_dve.sem, 1)

            def gathered(r):
                dve.wait_ge(K_pe.sem, K_pe.after("lo", r))
                for k, bank in ((0, 7), (4, 0)):
                    V.tensor_copy(xel[:, k:k + 4, :].rearrange("p k s -> p (k s)"), ps[:, bank, :]).then_inc(K_dve.sem, 1)

            n = dve.value_load(idi[0:1, 0:1], min_val=NE, max_val=NE + MAX_OVER)
            select(0)
            gathered(0)
            with dve.Fori(0, n) as r:
                dve.wait_ge(K_pe.sem, K_pe.after("tr", r))
                select(r + 1)
                end = ffn(U_MOE, FC * r, moe, FC * r, 1, 1, 4, hs1, hTh1, hTl1)
                gathered(r + 1)
                lo(U_MOE + 6, end)
                dve.wait_ge(yh_done, r + 1)
                V.tensor_tensor(Yl[:], ps[:, 2:4, :].rearrange("p b n -> p (b n)"), Yh[:].bitcast(F32), ALU.subtract)\
                 .then_inc(yl_done, 1)
                lo(U_MOE + 7, end)
                dve.wait_ge(scattered, r + 1)
                for t in range(NT):
                    V.scalar_tensor_tensor(out=X[:, t], in0=ps[:, 4 + 2 * t:6 + 2 * t, :].rearrange("p b n -> p (b n)"),
                                           scalar=gates[:, t, ds(r, 1)], in1=X[:, t], op0=ALU.mult, op1=ALU.add)\
                     .then_inc(added, 1)
            dve.wait_ge(added, NT * n + 1)
            layer_norm(3, None)


_INS = ["x", "gdn_w_in", "gdn_conv_w", "gdn_a_log", "gdn_dt_bias", "gdn_norm_w", "gdn_w_out", "sb_w_in", "sb_w_out",
        "ffn_w_gate", "ffn_w_up", "ffn_w_down", "moe_router", "moe_w_gate", "moe_w_up", "moe_w_down", "ln_g", "ln_b"]


def kernel(**inputs):
    import numpy as np
    import concourse.bacc as bacc
    from concourse.bass_utils import run_bass_kernel_spmd

    nc = bacc.Bacc("TRN2", target_bir_lowering=False, num_devices=1)
    arrays, args = {}, []
    for name in _INS:
        a = np.ascontiguousarray(inputs[name])
        arrays[f"in_{name}"] = a
        args.append(nc.dram_tensor(f"in_{name}", a.shape, mybir.dt.from_np(a.dtype), kind="ExternalInput").ap())
    args.append(nc.dram_tensor("out_0", (1, SEQ, D), F32, kind="ExternalOutput").ap())
    hybrid_trunk(nc, *args)
    r = run_bass_kernel_spmd(nc, [arrays], core_ids=[0])
    return r.results[0]["out_0"]
```

```python
from contextlib import ExitStack

import concourse.bass as bass
from concourse import mybir

ALU = mybir.AluOpType
ACT = mybir.ActivationFunctionType
AX_X = mybir.AxisListType.X
F32 = mybir.dt.float32
F32R = mybir.dt.float32r
I32 = mybir.dt.int32
ds = bass.ds

P = 128
SEQ = 256
NT = SEQ // P
D = 1024
KD = D // P
QK = 8
VH = 16
HPG = 4
QPG = HPG // 2
GROUPS = 2
LANES = GROUPS * NT
CONV_DIM = 4096
Z0 = CONV_DIM
BA0 = CONV_DIM + VH * P
FF = 3584
FC = FF // 512
NE = 8
TOPK = 2
SBH = 8
MAX_OVER = 3
ROUNDS = NE + MAX_OVER + 1
ALPHA = 4.0 ** 0.25
LN_EPS = 1e-5
RMS_EPS = 1e-6
SCALE = float(P) ** -0.5

RAW = 6
SPLIT = 3
CREDIT = 6
UNIT = 2048
EARLY = 3
A_UNITS = 24
OUT_UNITS = 8
FFN_UNITS = 6 * FC
SBIN_UNITS = 12
SBOUT_UNITS = 4
U_OUT = A_UNITS
U_FFN = U_OUT + OUT_UNITS
U_SBIN = U_FFN + FFN_UNITS
U_SBOUT = U_SBIN + SBIN_UNITS
U_MOE = U_SBOUT + SBOUT_UNITS

TURNS = VH // (GROUPS * HPG)
LEVELS = [1, 2, 4, 8, 16, 32, 64]
CST_IDENT = 2
CST = 9 + len(LEVELS) + 5 + 3 * len(LEVELS)
SMALL = 16 * 6


class Stages:

    def __init__(self, sem, names, lead=False):
        self.sem = sem
        self.names = list(names)
        self.lead = len(self.names) if lead else 0
        assert len(set(self.names)) == len(self.names)

    def after(self, name, turn=0):
        return turn * len(self.names) + self.names.index(name) + 1 + self.lead


def hybrid_trunk(nc, x, gdn_w_in, gdn_conv_w, gdn_a_log, gdn_dt_bias, gdn_norm_w, gdn_w_out,
                 sb_w_in, sb_w_out, ffn_w_gate, ffn_w_up, ffn_w_down,
                 moe_router, moe_w_gate, moe_w_up, moe_w_down, ln_g, ln_b, out):
    with ExitStack() as ctx:
        def sb(name, shape, dt=F32, where=ctx):
            return where.enter_context(nc.sbuf_tensor(name, shape, dt))

        def sem(name):
            return ctx.enter_context(nc.semaphore(name))

        raw = sb("raw", [P, RAW, UNIT])
        w_hi = sb("w_hi", [P, SPLIT, UNIT], F32R)
        w_lo = sb("w_lo", [P, SPLIT, UNIT], F32R)
        X = sb("X", [P, NT, D])
        cst = sb("cst", [P, 7 + len(LEVELS), P])
        IDENT, LE, GT, LT, NGE, ONES, NONES = (cst[:, i, :] for i in range(7))
        LEVEL = {b: cst[:, 7 + i, :] for i, b in enumerate(LEVELS)}
        iota = sb("iota", [P, P])
        zeros = sb("zeros", [P, 256], F32R)
        bah = sb("bah", [P, KD, 32], F32R)
        bal = sb("bal", [P, KD, 32], F32R)
        rw = sb("rw", [P, KD, NE])
        rwh = sb("rwh", [P, KD, NE], F32R)
        rwl = sb("rwl", [P, KD, NE], F32R)
        stats = sb("stats", [P, NT, 2, 6])
        mv = sb("mv", [P, NT, 2])
        sdev = sb("sdev", [P, NT, 1])
        rstd = sb("rstd", [P, NT, 1])
        warm = sb("warm", [P, 4, 1])
        ps = ctx.enter_context(nc.psum_tensor("ps", [P, 8, 512], F32))

        gdn = ExitStack()
        tok = sb("tok", [P, 32, NT, P], F32, gdn)
        zs = sb("zs", [P, NT, VH * P], F32, gdn)
        kT = sb("kT", [P, QK, SEQ], F32, gdn)
        ba = sb("ba", [P, NT, 32], F32, gdn)
        gsb = {n: sb(n, [P, NT, VH], F32, gdn) for n in ("beta", "xdt", "axdt", "lsp", "g")}
        beta, xdt, axdt, lsp, g = gsb.values()
        negA = sb("negA", [P, VH], F32, gdn)
        dtb = sb("dtb", [P, VH], F32, gdn)
        eg1 = sb("eg1", [P, VH], F32, gdn)
        beg1 = sb("beg1", [P, VH], F32, gdn)
        kdec = sb("kdec", [P, VH], F32, gdn)
        ssq = sb("ssq", [P, 2 * QK, NT], F32, gdn)
        rsn = sb("rsn", [P, 2 * QK, NT], F32, gdn)
        cw = sb("cw", [P, P], F32, gdn)
        nw = sb("nw", [P, P], F32, gdn)

        pa = ExitStack()
        xT0h = sb("xT0h", [P, KD, SEQ], F32R, pa)
        xT0l = sb("xT0l", [P, KD, SEQ], F32R, pa)
        pre = sb("pre", [P, 2, NT, 512], F32, pa)
        cacc = sb("cacc", [P, 2, 4, SEQ], F32, pa)
        pa.close()
        pc = ExitStack()
        E_ = sb("E_", [P, NT, HPG, P], F32, pc)
        ET = sb("ET", [P, NT, HPG, P], F32, pc)
        XB = sb("XB", [P, NT, HPG, P], F32, pc)
        DB = sb("DB", [P, NT, HPG, P], F32, pc)
        DTB = sb("DTB", [P, NT, HPG, P], F32, pc)
        CB = sb("CB", [P, NT, HPG, P], F32, pc)
        kTc = sb("kTc", [P, GROUPS * QPG, SEQ], F32, pc)
        pc.close()
        spare = raw[:, 2:RAW, :].rearrange("p s n -> p (s n)").rearrange("p (k t h d) -> p k t h d", t=NT, h=HPG, d=P)

        def lanes(first, k):
            return [first[:, 0], first[:, 1], spare[:, k, 0], spare[:, k, 1]]

        Ec, ETc, Xc, Dc, DTc, Cc = (lanes(b, k) for k, b in enumerate((E_, ET, XB, DB, DTB, CB)))
        qTc = spare[:, 6].rearrange("p t h d -> p (t h d)").rearrange("p (h s) -> p h s", s=SEQ)

        def flat(lane):
            return lane.rearrange("p h d -> p (h d)")

        po = ExitStack()
        oTh = sb("oTh", [P, VH, SEQ], F32R, po)
        oTl = sb("oTl", [P, VH, SEQ], F32R, po)
        po.close()
        baw = tok[:, 0:1].rearrange("p a b c -> p (a b c)").rearrange("p (k n) -> p k n", n=32)
        cwr = tok[:, 1, 0, :]
        baT = kT[0:32, 0, :]
        gdn.close()

        late = ctx
        lnrow = sb("lnrow", [P, 2, D], F32, late)
        xTh = sb("xTh", [P, KD, SEQ], F32R, late)
        xTl = sb("xTl", [P, KD, SEQ], F32R, late)
        fs = ExitStack()
        qkv = sb("qkv", [P, NT, 3 * D], F32, fs)
        qTs = sb("qTs", [P, 2, 4, SEQ], F32, fs)
        kTs = sb("kTs", [P, 2, 4, SEQ], F32, fs)
        spl = sb("spl", [P, 2, 4, 384], F32, fs)
        aTh = sb("aTh", [P, SBH, SEQ], F32R, fs)
        aTl = sb("aTl", [P, SBH, SEQ], F32R, fs)
        fs.close()
        fd = ExitStack()
        hs0 = sb("hs0", [P, NT, 512], F32, fd)
        hTh0 = sb("hTh0", [P, NT, 4, P], F32R, fd)
        hTl0 = sb("hTl0", [P, NT, 4, P], F32R, fd)
        fd.close()
        fm = ExitStack()
        Xh = sb("Xh", [P, NT, D], F32R, fm)
        Xl = sb("Xl", [P, NT, D], F32R, fm)
        xeh = sb("xeh", [P, KD, P], F32R, fm)
        xel = sb("xel", [P, KD, P], F32R, fm)
        Yh = sb("Yh", [P, D], F32R, fm)
        Yl = sb("Yl", [P, D], F32R, fm)
        hs1 = sb("hs1", [P, 1, 512], F32, fm)
        hTh1 = sb("hTh1", [P, 1, 4, P], F32R, fm)
        hTl1 = sb("hTl1", [P, 1, 4, P], F32R, fm)
        G = sb("G", [P, NT, P], F32R, fm)
        GTr = sb("GTr", [P, SEQ], F32R, fm)
        rt = {n: sb("rt_" + n, [P, NT, NE], F32, fm) for n in
              ("lg", "eq1", "ca", "oh1", "l2", "eq2", "oh2", "mask", "rank", "c2", "tmp")}
        rs = {n: sb("rs_" + n, [P, NT, 1], F32, fm) for n in
              ("m1", "i1", "m2", "i2", "df", "ex", "sm", "p1", "p2")}
        cnt = sb("cnt", [P, NE], F32, fm)
        ov = sb("ov", [P, NE], F32, fm)
        ovp = sb("ovp", [P, NE], F32, fm)
        ind = sb("ind", [P, MAX_OVER, NE], F32, fm)
        ranks = sb("ranks", [P, NT, ROUNDS], F32, fm)
        gates = sb("gates", [P, NT, ROUNDS], F32, fm)
        over = sb("over", [P, NT, MAX_OVER, NE], F32, fm)
        lgT = hs1[0:NE, 0, 0:SEQ]
        ids = sb("ids", [P, 4], F32, fm)
        idi = sb("idi", [P, 4], I32, fm)
        early = sb("early", [P, EARLY, UNIT], F32, fm)
        fm.close()

        raw_in = [sem(f"raw_in{i}") for i in range(RAW)]
        hi_done = sem("hi_done")
        lo_done = sem("lo_done")
        unit_used = sem("unit_used")
        early_in = sem("early_in")
        x_in = [sem(f"x_in{t}") for t in range(NT)]
        small_in = sem("small_in")
        cst_step = sem("cst_step")
        ln_in = sem("ln_in")
        out_done = sem("out_done")
        xt_pe, xt_hi, xt_lo = sem("xt_pe"), sem("xt_hi"), sem("xt_lo")
        A_pe = Stages(sem("A_pe"), ["t1A", "t1B", "t2A", "t2B"])
        A_act = Stages(sem("A_act"), ["preA", "c0A", "preB", "z", "siluA", "c0B", "tokA", "siluB", "tokB"], True)
        A_dve = Stages(sem("A_dve"), [f"{j}{m}{c}" for c in "AB" for j in (2, 1, 0) for m in range(4)])
        S_pe = Stages(sem("S_pe"), ["cw", "baT", "ba", "gc", "gl", "kT0", "kT1", "kT2", "kT3", "qT0", "qT1", "qT2", "qT3"])
        S_act = Stages(sem("S_act"), ["bah", "eb", "ax", "ex", "ea", "ln", "sq", "sd",
                                      "qT0", "qT1", "qT2", "qT3", "eg", "kd"])
        S_dve = Stages(sem("S_dve"), ["bal", "cw", "baT", "ba", "xdt", "b1", "b2", "sp", "g", "sq", "rs", "rq",
                                      "kT0", "kT1", "kT2", "kT3", "beg"])
        S_pool = Stages(sem("S_pool"), ["qn", "kn"])
        inv = LEVELS[1:]
        ln = range(LANES)
        C_pool = Stages(sem("C_pool"), ["G.0", "MB.0", "G.2", "MB.2", "MB.1", "MB.3", "G.1", "G.3"]
                        + [f"C{b}.{c}" for b in LEVELS for c in ln] + ["vb", "zn", "kd.0", "kd.1"])
        C_pe = Stages(sem("C_pe"), [f"{n}.{c}" for n in ("kk", "df", "dT", "T1") for c in ln]
                      + [f"{n}{b}.{c}" for b in inv for n in ("X", "U", "T") for c in ln if b < 64 or n != "T"]
                      + ["v0.0", "v0.1", "S.0", "O0.0", "S.1", "O0.1", "PK.0", "PQ.0", "PK.1", "PQ.1",
                         "v1.0", "v1.1", "AV.0", "AV.1"], True)
        C_act = Stages(sem("C_act"), ["cq"] + [f"{n}.{c}" for n in ("e", "eT") for c in ln]
                       + [f"{n}{b}.{c}" for b in inv for n in ("x", "d") for c in ln if b < 64 or n != "d"]
                       + [f"{n}.{g}" for n in ("v0s", "Ss", "v1s", "sq1") for g in range(GROUPS)], True)
        C_dve = Stages(sem("C_dve"), ["ck"] + [f"{n}.{c}" for c in ln for n in ("L1", "L")]
                       + [f"A1.{c}" for c in ln] + [f"{n}.{c}" for c in ln for n in ("d1", "dt1")]
                       + [f"u2.{c}" for c in ln] + [f"A.{c}" for c in ln]
                       + [f"u{b}.{c}" for b in inv[1:] for c in ln]
                       + [f"{n}.{g}" for n in ("o0", "r1", "r", "sq0", "ss0", "o1a", "o1") for g in range(GROUPS)], True)
        O_pe, O_act, O_dve, O_pool = (Stages(sem(n), s) for n, s in (
            ("O_pe", [f"t{c}" for c in range(8)]),
            ("O_act", ["sd"] + [f"h{c}" for c in range(8)]),
            ("O_dve", ["rs", "g0", "g1", "l0", "g2", "l1", "g3", "l2", "g4", "l3", "g5", "l4", "l5", "l6", "l7"]),
            ("O_pool", ["n", "z"])))
        ln_dve = [Stages(sem(f"ln_dve{k}"), [n for n in ("r0", "sa0", "sb0", "ag0", "r1", "rc0", "g0", "b0",
                                                         "sa1", "sb1", "ag1", "rc1", "g1", "b1") if n[0] != "r" or n[1] == "c" or k < 3])
                  for k in range(4)]
        ln_act = [Stages(sem(f"ln_act{k}"), ["sd0", "sd1"]) for k in range(4)]
        y_done = sem("y_done")
        names = ("t", "s", "hh", "h", "hl")
        dense = {n: sem("dense_" + n) for n in names}
        moe = {n: sem("moe_" + n) for n in names}
        B_act = Stages(sem("B_act"), ["c0", "c1", "c2"], True)
        T_pe = Stages(sem("T_pe"), ["qk0", "z0", "qk1", "z1", "R0", "R1", "o0", "o1"])
        T_act = Stages(sem("T_act"), ["q0", "a0", "e0", "l0", "q1", "a1", "e1", "l1", "p0", "p1", "oh0", "oh1"])
        T_dve = Stages(sem("T_dve"), ["k0", "k1", "sp0", "ma0", "mb0", "mn0", "sp1", "ma1", "mb1", "na0", "nb0", "mn1",
                                      "na1", "nb1", "ol0", "ol1"])
        R_pe = Stages(sem("R_pe"), ["lgT", "lg", "rk"])
        R_act = Stages(sem("R_act"), ["rwh", "xh", "ex"])
        R_dve = Stages(sem("R_dve"), ["rwl", "xl", "xa", "z0", "z1", "z2", "lgT", "lg", "m1", "eq1", "ca", "i1", "oh1", "l2",
                                      "m2", "eq2", "c2", "i2", "oh2", "mask", "df", "sm", "p1", "p2", "cm1", "cm2", "comb",
                                      "rk1", "rk2", "cnt", "ov"] + [f"pre{e}" for e in range(1, NE)]
                       + ["in", "im", "pr", "sr", "ad", "pg", "sg", "pi", "si", "no", "nc", "ni"])
        K_pe = Stages(sem("K_pe"), ["hi", "lo", "tr"])
        K_act = Stages(sem("K_act"), ["hi", "gt"])
        K_dve = Stages(sem("K_dve"), ["s0", "s1", "l7", "l0"])
        yh_done, yl_done, scattered, added = sem("yh_done"), sem("yl_done"), sem("scattered"), sem("added")

        def cols(w, half, c0):
            return w[half * 512:(half + 1) * 512, ds(c0, 512)].rearrange("(k p) n -> p k n", p=P)

        def rows(w, r0):
            return w[ds(r0, 256), :].rearrange("(k p) n -> p k n", p=P)

        early_sources = [None] * (6 - EARLY) + [early[:, e, :] for e in range(EARLY)]

        def unit_hi(j):
            return w_hi[:, j % SPLIT, :]

        def unit_lo(j):
            return w_lo[:, j % SPLIT, :]

        def units(j, turn=0):
            return j + 6 * turn + 1 + CREDIT

        block = ctx.enter_context(nc.Block())

        @block.sync
        def _(sp):
            def load(j, turn, src, k):
                sp.wait_ge(lo_done, units(j - RAW, turn))
                sp.dma_start(raw[:, j % RAW, :].rearrange("p (k n) -> p k n", k=k), src)\
                  .then_inc(raw_in[j % RAW], 16)

            for t in range(NT):
                sp.dma_start(X[:, t], x[0, t * P:(t + 1) * P, :]).then_inc(x_in[t], 16)
            with sp.Fori(0, 4) as i:
                for c, c0 in enumerate((i * 1024, i * 1024 + 512, i * 512 + Z0)):
                    for half in range(2):
                        load(2 * c + half, i, cols(gdn_w_in[0], half, c0), 4)
            for u in range(OUT_UNITS):
                if u == 2:
                    sp.wait_ge(C_dve.sem, C_dve.after("o1.1", TURNS - 1))
                load(U_OUT + u, 0, rows(gdn_w_out[0], u * 256), 2)

            def ffn(base, turn, wg, wu, wd, early_units=None):
                for k, w in enumerate((wg, wu)):
                    for half in range(2):
                        load(base + 2 * k + half, turn, cols(w, half, 0), 4)

                def chunk(c, present=()):
                    for j, src, k in ([(4 + 2 * i + half, cols(w, half, (c + 1) * 512), 4) for i, w in enumerate((wg, wu))
                                       for half in range(2)]
                                      + [(8 + half, rows(wd, c * 512 + half * 256), 2) for half in range(2)]):
                        if j in present:
                            there(base + j, turn + c)
                        else:
                            load(base + j, turn + c, src, k)

                def there(j, turn):
                    sp.wait_ge(lo_done, units(j - RAW, turn))
                    sp.sem_inc(raw_in[j % RAW], 16)

                last_down = [rows(wd, (FC - 1) * 512 + half * 256) for half in range(2)]
                if early_units:
                    sp.wait_ge(unit_used, units(U_SBOUT + SBOUT_UNITS - 1))
                    for e, src in enumerate([rows(wd, (FC - 2) * 512 + 256)] + last_down):
                        sp.dma_start(early[:, e, :].rearrange("p (k n) -> p k n", k=2), src).then_inc(early_in, 16)
                    with sp.Fori(0, FC - 2) as c:
                        chunk(c)
                    chunk(FC - 2, (9,))
                    sp.wait_ge(early_in, 16 * EARLY)
                    for half in range(2):
                        there(base + 4 + half, turn + FC - 1)
                else:
                    with sp.Fori(0, FC - 1) as c:
                        chunk(c)
                    for half in range(2):
                        load(base + 4 + half, turn + FC - 1, last_down[half], 2)

            ffn(U_FFN, 0, ffn_w_gate[0], ffn_w_up[0], ffn_w_down[0])
            with sp.Fori(0, 2) as i:
                for c in range(3):
                    for half in range(2):
                        load(U_SBIN + 2 * c + half, i, cols(sb_w_in[0], half, i * 1536 + c * 512), 4)
            for u in range(SBOUT_UNITS):
                load(U_SBOUT + u, 0, rows(sb_w_out[0], u * 256), 2)

            wg_all = moe_w_gate[0].rearrange("e k n -> (e k) n")
            wu_all = moe_w_up[0].rearrange("e k n -> (e k) n")
            wd_all = moe_w_down[0].rearrange("e k n -> (e k) n")

            def expert(turn, e, early_units=False):
                ffn(U_MOE, turn, wg_all[ds(e * D, D), :], wu_all[ds(e * D, D), :], wd_all[ds(e * FF, FF), :], early_units)

            expert(0, 0, True)
            with sp.Fori(1, NE) as e:
                expert(FC * e, e)
            sp.wait_ge(R_dve.sem, R_dve.after("ni"))
            n = sp.value_load(idi[0:1, 0:1], min_val=NE, max_val=NE + MAX_OVER)
            with sp.If(n > NE):
                with sp.Fori(NE, n) as r:
                    e = sp.value_load(idi[0:1, ds(r - (NE - 1), 1)], min_val=0, max_val=NE - 1)
                    expert(FC * r, e)
            for j in (U_MOE, U_MOE + 1):
                sp.wait_ge(lo_done, units(j - RAW, FC * n))
                sp.dma_start(raw[:, j % RAW, 0:NE], moe_router[0, 0:P, :]).then_inc(raw_in[j % RAW], 16)
            for t in range(NT):
                sp.wait_ge(ln_dve[3].sem, ln_dve[3].after(f"b{t}"))
                sp.dma_start(out[0, t * P:(t + 1) * P, :], X[:, t]).then_inc(out_done, 16)
            sp.wait_ge(out_done, 16 * NT)

        @block.gpsimd
        def _(pool):
            nc.gpsimd.memset(IDENT, 0.0).then_inc(cst_step, 1)
            pool.wait_ge(cst_step, 1)
            nc.gpsimd.affine_select(out=IDENT, in_=IDENT, compare_op=ALU.not_equal, fill=1.0, base=0, pattern=[[-1, P]],
                                    channel_multiplier=1).then_inc(cst_step, 1)
            for ap, v in ((LE, 1.0), (GT, 1.0), (LT, 1.0), (NGE, -1.0), (ONES, 1.0), (NONES, -1.0),
                          *((LEVEL[b], 1.0) for b in LEVELS)):
                nc.gpsimd.memset(ap, v).then_inc(cst_step, 1)
            nc.gpsimd.memset(zeros[:].bitcast(F32), 0.0).then_inc(cst_step, 1)
            n = CST_IDENT + 7 + len(LEVELS)
            nc.gpsimd.iota(iota[:], pattern=[[1, P]], base=0, channel_multiplier=0,
                           allow_small_or_imprecise_dtypes=True).then_inc(cst_step, 1)
            n += 1
            pool.wait_ge(cst_step, n)

            def cut(ap, pattern, base, cm, op):
                nc.gpsimd.affine_select(out=ap, in_=ap, compare_op=op, fill=0.0, base=base, pattern=pattern,
                                        channel_multiplier=cm).then_inc(cst_step, 1)

            cut(LE, [[1, P]], 0, -1, ALU.is_ge)
            cut(GT, [[-1, P]], 0, 1, ALU.is_gt)
            cut(LT, [[1, P]], 0, -1, ALU.is_gt)
            cut(NGE, [[-1, P]], 0, 1, ALU.is_ge)
            n += 4
            for b in LEVELS:
                v = LEVEL[b].rearrange("p (n h b) -> p n h b", h=2, b=b)
                nc.gpsimd.memset(v[:, :, 1, :], 0.0).then_inc(cst_step, 1)
                cut(v[:, :, 0, :], [[-2 * b, P // (2 * b)], [0, b]], -b, 1, ALU.is_ge)
                n += 2
            pool.wait_ge(cst_step, n)
            for b in LEVELS:
                v = LEVEL[b].rearrange("p (n h b) -> p n h b", h=2, b=b)
                cut(v[:, :, 0, :], [[2 * b, P // (2 * b)], [0, b]], 2 * b - 1, -1, ALU.is_ge)
                n += 1
            assert n == CST
            pool.wait_ge(cst_step, CST)

            for h0 in (0, QK):
                pool.wait_ge(S_dve.sem, S_dve.after("rq" if h0 == 0 else "rs"))
                v = tok[:, h0:h0 + QK]
                nc.gpsimd.tensor_tensor(v, v, rsn[:, h0:h0 + QK].unsqueeze(3).broadcast_to([P, QK, NT, P]), ALU.mult)\
                  .then_inc(S_pool.sem, 1)

            pool.wait_ge(S_dve.sem, S_dve.after("g"))
            pool.wait_ge(unit_used, units(A_UNITS - 1))
            with pool.Fori(0, TURNS) as i:
                def triangle(dst, mask, v, c):
                    nc.gpsimd.tensor_tensor(dst[c], mask.unsqueeze(1).broadcast_to([P, HPG, P]),
                                            v[:, c % 2, ds(8 * i + 4 * (c // 2), HPG)].unsqueeze(2)
                                            .broadcast_to([P, HPG, P]), ALU.mult).then_inc(C_pool.sem, 1)

                pool.wait_ge(C_pe.sem, C_pe.after("O0.1", i - 1))
                for c in (0, 2):
                    triangle(Xc, LE, g, c)
                    triangle(Dc, GT, beta, c)
                for c in (1, 3):
                    triangle(Dc, GT, beta, c)
                for c in (1, 3):
                    pool.wait_ge(C_pe.sem, C_pe.after(f"AV.{c // 2}", i - 1))
                    triangle(Xc, LE, g, c)
                for b in LEVELS:
                    for c in range(LANES):
                        if b == 1:
                            pool.wait_ge(C_dve.sem, C_dve.after(f"L.{c}", i))
                        elif b == 2:
                            pool.wait_ge(C_dve.sem, C_dve.after(f"d1.{c}", i))
                            pool.wait_ge(C_pe.sem, C_pe.after(f"T1.{c}", i))
                        else:
                            pool.wait_ge(C_pe.sem, C_pe.after(f"X{b // 2}.{c}", i))
                        nc.gpsimd.tensor_tensor(Cc[c], Ec[c], LEVEL[b].unsqueeze(1).broadcast_to([P, HPG, P]),
                                                ALU.mult).then_inc(C_pool.sem, 1)
                pool.wait_ge(A_act.sem, A_act.after("tokB", 3))
                v = tok[:, ds(16 + 8 * i, 8)]
                nc.gpsimd.tensor_tensor(v, v, beta[:, :, ds(8 * i, 8)].rearrange("p t h -> p h t").unsqueeze(3)
                                        .broadcast_to([P, 8, NT, P]), ALU.mult).then_inc(C_pool.sem, 1)
                zv = zs[:, ds(i, 1), :].rearrange("p t (h d) -> p (t h) d", d=P)
                nc.gpsimd.tensor_tensor(zv, zv, nw[:].unsqueeze(1).broadcast_to([P, VH, P]), ALU.mult)\
                  .then_inc(C_pool.sem, 1)
                for grp in range(GROUPS):
                    pool.wait_ge(C_pe.sem, C_pe.after(f"U64.{2 * grp}", i))
                    kq = tok[:, ds(QK + 4 * i + QPG * grp, QPG), 0, :]
                    nc.gpsimd.tensor_tensor(Dc[2 * grp].rearrange("p (q r) d -> p q r d", r=2),
                                            kq.unsqueeze(2).broadcast_to([P, QPG, 2, P]),
                                            kdec[:, ds(8 * i + 4 * grp, HPG)].rearrange("p (q r) -> p q r", r=2)
                                            .unsqueeze(3).broadcast_to([P, QPG, 2, P]), ALU.mult).then_inc(C_pool.sem, 1)

            pool.wait_ge(O_dve.sem, O_dve.after("rs"))
            pool.wait_ge(C_pool.sem, C_pool.after("zn", TURNS - 1))
            v = tok[:, 28:32]
            nc.gpsimd.tensor_tensor(v, v, rsn[:, 12:16].unsqueeze(3).broadcast_to([P, 4, NT, P]), ALU.mult)\
              .then_inc(O_pool.sem, 1)
            pool.wait_ge(O_pool.sem, O_pool.after("n"))
            nc.gpsimd.tensor_tensor(v, v, zs[:, :, 12 * P:].rearrange("p t (h d) -> p h t d", d=P), ALU.mult)\
              .then_inc(O_pool.sem, 1)

        @block.scalar
        def _(act):
            act.sem_inc(A_act.sem, A_act.lead)
            act.sem_inc(B_act.sem, B_act.lead)
            act.sem_inc(C_act.sem, C_act.lead)
            for S in (dense, moe):
                act.sem_inc(S["s"], 1)
                act.sem_inc(S["hh"], 1)
            act.dma_start(baw, gdn_w_in[0, :, BA0:BA0 + 32].rearrange("(k p) n -> p k n", p=P)).then_inc(small_in, 16)
            act.dma_start(cwr, gdn_conv_w[0].rearrange("j (c p) -> (j c) p", p=P)).then_inc(small_in, 16)
            act.dma_start(dtb[:], gdn_dt_bias[0].partition_broadcast(P)).then_inc(small_in, 16)
            act.dma_start(negA[:], gdn_a_log[0].partition_broadcast(P)).then_inc(small_in, 16)
            act.dma_start(nw[:], gdn_norm_w[0].partition_broadcast(P)).then_inc(small_in, 16)
            act.dma_start(rw[:], moe_router[0].rearrange("(k p) n -> p k n", p=P)).then_inc(small_in, 16)

            def hi(j, turn=0, src=None):
                act.wait_ge(raw_in[j % RAW], 16 * (turn + j // RAW + 1))
                act.wait_ge(unit_used, units(j - SPLIT, turn))
                nc.scalar.activation(unit_hi(j), raw[:, j % RAW, :] if src is None else src, ACT.Copy).then_inc(hi_done, 1)

            def transposed(k, t, th, bank):
                for half in range(2):
                    act.wait_ge(xt_pe, 4 * k + 2 * t + half + 1)
                    nc.scalar.activation(th[:, 4 * half:4 * half + 4, t * P:(t + 1) * P],
                                         ps[:, bank + 2 * t + half, :].rearrange("p (k s) -> p k s", s=P),
                                         ACT.Copy).then_inc(xt_hi, 1)

            def layer_norm(k, th=None, bank=None):
                nc.scalar.activation(warm[:, k], rw[:, 0, 0:1], ACT.Sqrt, scale=0.0)
                for t in range(NT):
                    act.wait_ge(ln_dve[k].sem, ln_dve[k].after(f"ag{t}"))
                    nc.scalar.activation(sdev[:, t], mv[:, t, 1:2], ACT.Sqrt, bias=LN_EPS).then_inc(ln_act[k].sem, 1)
                    if th is not None:
                        transposed(k + 1, t, th, bank)

            def load_ln(k):
                act.dma_start(lnrow[:, 0, :], ln_g[k // 2, k % 2].partition_broadcast(P)).then_inc(ln_in, 16)
                act.dma_start(lnrow[:, 1, :], ln_b[k // 2, k % 2].partition_broadcast(P)).then_inc(ln_in, 16)

            for t in range(NT):
                transposed(0, t, xT0h, 4)

            hi(0)
            hi(1)
            act.wait_ge(small_in, SMALL)
            nc.scalar.activation(bah[:], baw, ACT.Copy).then_inc(S_act.sem, 1)
            nc.scalar.activation(rwh[:], rw[:], ACT.Copy).then_inc(R_act.sem, 1)

            def first_tap(c, i):
                act.wait_ge(S_dve.sem, S_dve.after("cw"))
                act.wait_ge(A_pe.sem, A_pe.after("t1" + "AB"[c], i))
                for m in range(4):
                    last = nc.scalar.activation(cacc[:, c, m, :], ps[:, 4 + 2 * c + m // 2, (m % 2) * SEQ:(m % 2 + 1) * SEQ],
                                                ACT.Copy, scale=cw[:, ds(3 * 32 + i * 8 + 4 * c + m, 1)])
                last.then_inc(A_act.sem, 1)

            def silu(c, i):
                act.wait_ge(A_dve.sem, A_dve.after("03" + "AB"[c], i))
                nc.scalar.activation(cacc[:, c], cacc[:, c], ACT.Silu).then_inc(A_act.sem, 1)

            def by_token(c, i):
                act.wait_ge(A_pe.sem, A_pe.after("t2" + "AB"[c], i))
                nc.scalar.activation(tok[:, ds(i * 8 + 4 * c, 4), :, :],
                                     ps[:, 4 + 2 * c:6 + 2 * c, :].rearrange("p t (m d) -> p m t d", d=P),
                                     ACT.Copy).then_inc(A_act.sem, 1)

            def project(i, first=False):
                if not first:
                    silu(0, i - 1)
                hi(2, i)
                if not first:
                    first_tap(1, i - 1)
                    by_token(0, i - 1)
                hi(3, i)
                if not first:
                    silu(1, i - 1)
                hi(4, i)
                hi(5, i)
                if not first:
                    by_token(1, i - 1)
                act.wait_ge(unit_used, units(1, i))
                nc.scalar.activation(pre[:, 0], ps[:, 0:2, :], ACT.Copy).then_inc(A_act.sem, 1)
                hi(6, i)
                first_tap(0, i)
                act.wait_ge(unit_used, units(3, i))
                nc.scalar.activation(pre[:, 1], ps[:, 2:4, :], ACT.Copy).then_inc(A_act.sem, 1)
                hi(7, i)
                act.wait_ge(unit_used, units(5, i))
                nc.scalar.activation(zs[:, :, ds(i * 512, 512)], ps[:, 0:2, :], ACT.Silu).then_inc(A_act.sem, 1)

            project(0, True)
            act.wait_ge(S_dve.sem, S_dve.after("ba"))
            nc.scalar.activation(beta[:], ba[:, :, 0:VH], ACT.Exp, scale=-1.0).then_inc(S_act.sem, 1)
            act.wait_ge(S_dve.sem, S_dve.after("xdt"))
            nc.scalar.activation(axdt[:], xdt[:], ACT.Abs).then_inc(S_act.sem, 1)
            act.wait_ge(S_act.sem, S_act.after("ax"))
            nc.scalar.activation(axdt[:], axdt[:], ACT.Exp, scale=-1.0).then_inc(S_act.sem, 1)
            nc.scalar.activation(negA[:], negA[:], ACT.Exp).then_inc(S_act.sem, 1)
            act.wait_ge(S_act.sem, S_act.after("ex"))
            nc.scalar.activation(lsp[:], axdt[:], ACT.Ln, bias=1.0).then_inc(S_act.sem, 1)
            with act.Fori(1, 3) as i:
                project(i)
            act.wait_ge(A_act.sem, A_act.after("tokB", 1))
            for h in range(QK):
                for t in range(NT):
                    last = nc.scalar.activation(kT[:, h, t * P:(t + 1) * P], tok[:, h, t, :], ACT.Square,
                                                accum_out=ssq[:, h, t:t + 1])
            last.then_inc(S_act.sem, 1)
            act.wait_ge(S_act.sem, S_act.after("sq"))
            act.wait_ge(S_dve.sem, S_dve.after("sq"))
            nc.scalar.activation(rsn[:], ssq[:], ACT.Sqrt, bias=RMS_EPS).then_inc(S_act.sem, 1)
            project(3)
            silu(0, 3)
            first_tap(1, 3)
            by_token(0, 3)
            for q, bank in enumerate((3, 0, 1, 4)):
                act.wait_ge(S_pe.sem, S_pe.after(f"qT{q}"))
                nc.scalar.activation(tok[:, 2 * q:2 * q + 2].rearrange("p h t d -> p (h t d)"), ps[:, bank, :],
                                     ACT.Copy).then_inc(S_act.sem, 1)
            silu(1, 3)
            act.wait_ge(S_pe.sem, S_pe.after("gl"))
            nc.scalar.activation(eg1[:], ps[:, 2, 0:VH], ACT.Exp).then_inc(S_act.sem, 1)
            nc.scalar.activation(kdec[:], ps[:, 2, VH:2 * VH], ACT.Exp).then_inc(S_act.sem, 1)
            by_token(1, 3)

            act.wait_ge(lo_done, units(A_UNITS - 1))
            act.wait_ge(S_act.sem, S_act.after("qT3"))
            with act.Fori(0, TURNS) as i:
                act.wait_ge(C_pe.sem, C_pe.after("PQ.1", i - 1))
                nc.scalar.activation(qTc, tok[:, ds(4 * i, 4)].rearrange("p h t d -> p h (t d)"), ACT.Copy)\
                  .then_inc(C_act.sem, 1)
                for n, dst in (("df", Ec), ("dT", ETc)):
                    for c in range(LANES):
                        act.wait_ge(C_pe.sem, C_pe.after(f"{n}.{c}", i))
                        nc.scalar.activation(flat(dst[c]), ps[:, 4 + c, :], ACT.Exp).then_inc(C_act.sem, 1)
                for b in inv:
                    for c in range(LANES):
                        act.wait_ge(C_pe.sem, C_pe.after(f"X{b}.{c}", i))
                        nc.scalar.activation(flat(Xc[c]), ps[:, c, :], ACT.Copy).then_inc(C_act.sem, 1)
                    for c in range(LANES):
                        if b < 64:
                            act.wait_ge(C_pe.sem, C_pe.after(f"T{b}.{c}", i))
                            nc.scalar.activation(flat(Dc[c]), ps[:, 4 + c, :], ACT.Copy).then_inc(C_act.sem, 1)
                for n, dst, bank in (("v0", Xc, 0), ("S", Cc, 1)):
                    for grp in range(GROUPS):
                        act.wait_ge(C_pe.sem, C_pe.after(f"{n}.{grp}", i))
                        nc.scalar.activation(flat(dst[2 * grp]), ps[:, 2 * grp + bank, :], ACT.Copy).then_inc(C_act.sem, 1)
                for grp in range(GROUPS):
                    act.wait_ge(C_pe.sem, C_pe.after(f"v1.{grp}", i))
                    nc.scalar.activation(flat(Xc[2 * grp + 1]), ps[:, 2 * grp + 1, :], ACT.Copy).then_inc(C_act.sem, 1)
                for grp, scratch in enumerate((E_[:, 1], CB[:, 0])):
                    act.wait_ge(C_dve.sem, C_dve.after(f"o1.{grp}", i))
                    for h in range(HPG):
                        n = 8 * i + HPG * grp + h
                        last = nc.scalar.activation(scratch[:, h, :], tok[:, ds(16 + n, 1), 1, :]
                                                    .rearrange("p a d -> p (a d)"), ACT.Square,
                                                    accum_out=ssq[:, ds(n, 1), 1:2].rearrange("p a b -> p (a b)"))
                    last.then_inc(C_act.sem, 1)

            act.wait_ge(C_dve.sem, C_dve.after("ss0.1", TURNS - 1))
            act.wait_ge(C_act.sem, C_act.after("sq1.1", TURNS - 1))
            nc.scalar.activation(rsn[:], ssq[:], ACT.Sqrt, scale=1.0 / P, bias=RMS_EPS).then_inc(O_act.sem, 1)
            for c in range(8):
                if c > 3:
                    hi(U_OUT + c - 2)
                act.wait_ge(O_pe.sem, O_pe.after(f"t{c}"))
                nc.scalar.activation(oTh[:, 2 * c:2 * c + 2, :].rearrange("p a b -> p (a b)"), ps[:, 4 + c % 4, :], ACT.Copy)\
                  .then_inc(O_act.sem, 1)
            load_ln(0)
            for u in range(6, OUT_UNITS + 2):
                hi(U_OUT + u)
            layer_norm(0, xTh, 4)

            def ffn(base, turn, S, done, tiles, g_bank, t_bank, hs, hTh, first_gate=None, present=False):
                def silu(n, gate):
                    act.wait_ge(unit_used, gate)
                    act.wait_ge(S["t"], n + 1)
                    nc.scalar.activation(hs[:], ps[:, g_bank:g_bank + tiles, :], ACT.Silu).then_inc(S["s"], 1)

                def hidden(n):
                    act.wait_ge(S["t"], n + 2)
                    nc.scalar.activation(hTh[:].rearrange("p t m d -> p t (m d)"), ps[:, t_bank:t_bank + tiles, :],
                                         ACT.Copy).then_inc(S["hh"], 1)

                hi(base + 2, turn)
                hi(base + 3, turn)
                if first_gate:
                    first_gate()
                silu(done, units(base + 1, turn))
                hi(base + 4, turn)
                hi(base + 5, turn)
                hidden(done)

                def chunk(c, src):
                    for k in range(6):
                        hi(base + 6 + k, turn + c, src[k])
                        if k == 2:
                            silu(done + c + 1, units(base + 5, turn + c))
                    hidden(done + c + 1)

                with act.Fori(0, FC - 1 - present) as c:
                    chunk(c, [None] * 6)
                if present:
                    act.wait_ge(early_in, 16 * EARLY)
                    chunk(FC - 2, early_sources)
                return turn + FC - 1

            act.wait_ge(ln_dve[0].sem, ln_dve[0].after("b1"))
            load_ln(1)
            end = ffn(U_FFN, 0, dense, 0, NT, 0, 2, hs0, hTh0)
            hi(U_FFN + 6, end)
            hi(U_FFN + 7, end)
            layer_norm(1, xTh, 0)

            act.wait_ge(ln_dve[1].sem, ln_dve[1].after("b1"))
            load_ln(2)

            def chunk(c, bank, i):
                act.wait_ge(unit_used, units(U_SBIN + 2 * c + 1, i))
                nc.scalar.activation(qkv[:, :, i * 1536 + c * 512:i * 1536 + c * 512 + 512], ps[:, bank:bank + 2, :],
                                     ACT.Copy).then_inc(B_act.sem, 1)

            def queries(grp):
                act.wait_ge(T_pe.sem, T_pe.after(f"qk{grp}"))
                nc.scalar.activation(qTs[:, grp], ps[:, 4 * grp:4 * grp + 4, 0:SEQ], ACT.Copy, scale=SCALE)\
                  .then_inc(T_act.sem, 1)

            def exponential(grp):
                act.wait_ge(T_pe.sem, T_pe.after(f"z{grp}"))
                nc.scalar.activation(spl[:, grp], ps[:, 4 * grp:4 * grp + 4, 0:384], ACT.Abs).then_inc(T_act.sem, 1)
                act.wait_ge(T_act.sem, T_act.after(f"a{grp}"))
                nc.scalar.activation(spl[:, grp], spl[:, grp], ACT.Exp, scale=-1.0).then_inc(T_act.sem, 1)

            def logarithm(grp):
                act.wait_ge(T_act.sem, T_act.after(f"e{grp}"))
                nc.scalar.activation(spl[:, grp], spl[:, grp], ACT.Ln, bias=1.0).then_inc(T_act.sem, 1)

            for j in (2, 3):
                hi(U_SBIN + j)
            chunk(0, 4, 0)
            hi(U_SBIN + 4)
            chunk(1, 6, 0)
            for j in (5, 6):
                hi(U_SBIN + j)
            chunk(2, 0, 0)
            for j in (7, 8, 9):
                hi(U_SBIN + j)
            chunk(0, 4, 1)
            queries(0)
            hi(U_SBIN + 10)
            chunk(1, 6, 1)
            for j in (11, 12):
                hi(U_SBIN + j)
            exponential(0)
            chunk(2, 4, 1)
            hi(U_SBIN + 13)
            logarithm(0)
            queries(1)
            exponential(1)
            logarithm(1)
            for grp in range(2):
                act.wait_ge(T_dve.sem, T_dve.after(f"mn{grp}"))
                nc.scalar.activation(spl[:, grp], spl[:, grp], ACT.Exp).then_inc(T_act.sem, 1)
            for grp in range(2):
                act.wait_ge(T_pe.sem, T_pe.after(f"o{grp}"))
                nc.scalar.activation(aTh[:, 4 * grp:4 * grp + 4, :], ps[:, 4 * grp:4 * grp + 4, 0:SEQ], ACT.Copy)\
                  .then_inc(T_act.sem, 1)
            for u in range(SBOUT_UNITS):
                hi(U_SBOUT + 2 + u)
            layer_norm(2, xTh, 4)

            act.wait_ge(ln_dve[2].sem, ln_dve[2].after("b1"))
            load_ln(3)
            nc.scalar.activation(Xh[:], X[:], ACT.Copy).then_inc(R_act.sem, 1)
            act.wait_ge(R_dve.sem, R_dve.after("df"))
            nc.scalar.activation(rs["ex"][:], rs["df"][:], ACT.Exp).then_inc(R_act.sem, 1)

            def gathered(r):
                act.wait_ge(K_pe.sem, K_pe.after("hi", r))
                nc.scalar.activation(xeh[:].rearrange("p k s -> p (k s)"), ps[:, 5:7, :].rearrange("p b n -> p (b n)"),
                                     ACT.Copy).then_inc(K_act.sem, 1)

            def slots(r, first=False):
                act.wait_ge(K_pe.sem, K_pe.after("tr", r))
                if not first:
                    act.wait_ge(scattered, NT * r + NT)
                nc.scalar.activation(GTr[:], ps[:, 1, 0:SEQ], ACT.Copy).then_inc(K_act.sem, 1)

            def round_(r, first=False):
                end = ffn(U_MOE, FC * r, moe, FC * r, 1, 0, 4, hs1, hTh1, lambda: slots(r, first), first)
                gathered(r + 1)
                hi(U_MOE + 6, end)
                act.wait_ge(unit_used, units(U_MOE + 5, end))
                nc.scalar.activation(Yh[:], ps[:, 2:4, :].rearrange("p b n -> p (b n)"), ACT.Copy).then_inc(yh_done, 1)
                hi(U_MOE + 7, end)

            gathered(0)
            round_(0, True)
            act.wait_ge(R_dve.sem, R_dve.after("ni"))
            n = act.value_load(idi[0:1, 0:1], min_val=NE, max_val=NE + MAX_OVER)
            with act.Fori(1, n) as r:
                round_(r)
            layer_norm(3)

        @block.tensor
        def _(pe):
            pe.sem_inc(unit_used, CREDIT)
            pe.sem_inc(scattered, NT)
            pe.sem_inc(C_pe.sem, C_pe.lead)
            for S in (dense, moe):
                pe.sem_inc(S["t"], 1)

            def split3(o, lh, ll, rh, rl, start, stop):
                nc.tensor.matmul(o, lh, rh, start=start, stop=False, skip_group_check=True)
                nc.tensor.matmul(o, lh, rl, start=False, stop=False, skip_group_check=True)
                return nc.tensor.matmul(o, ll, rh, start=False, stop=stop, skip_group_check=True)

            def wide_tile(j, half, bank, t, xh, xl):
                for k in range(4):
                    kk, w = half * 4 + k, slice(k * 512, (k + 1) * 512)
                    last = split3(ps[:, bank, :], xh[:, kk, t * P:(t + 1) * P], xl[:, kk, t * P:(t + 1) * P],
                                  unit_hi(j)[:, w], unit_lo(j)[:, w], kk == 0, kk == KD - 1)
                return last

            def wide(j, turn, half, banks, xh, xl):
                pe.wait_ge(lo_done, units(j, turn))
                for t, bank in enumerate(banks):
                    last = wide_tile(j, half, bank, t, xh, xl)
                return last.then_inc(unit_used, 1)

            def wide_first(j, k, banks, xh, xl, before=None):
                for t, bank in enumerate(banks):
                    if before:
                        before(t)
                    for half in range(2):
                        pe.wait_ge(xt_lo, 4 * k + 2 * t + half + 1)
                        if t == 0:
                            pe.wait_ge(lo_done, units(j + half))
                        last = wide_tile(j + half, half, bank, t, xh, xl)
                        if t == NT - 1:
                            last.then_inc(unit_used, 1)

            def deep(j, turn, banks, lhs, start, stop, final=False):
                pe.wait_ge(lo_done, units(j, turn))
                for t, bank in enumerate(banks):
                    for half in range(2):
                        for k in range(2):
                            w = slice(k * D + half * 512, k * D + half * 512 + 512)
                            lh, ll = lhs(t, k)
                            last = split3(ps[:, bank + half, :], lh, ll, unit_hi(j)[:, w], unit_lo(j)[:, w],
                                          start and k == 0, stop and k == 1)
                    if final and t == 0:
                        last.then_inc(y_done, 1)
                return last.then_inc(unit_used, 1)

            def transpose_x(bank, t, sem, value):
                pe.wait_ge(sem, value)
                for half in range(2):
                    for k in range(4):
                        c = (4 * half + k) * P
                        last = nc.tensor.transpose(ps[:, bank + 2 * t + half, k * P:(k + 1) * P], X[:, t, c:c + P], IDENT)
                    last.then_inc(xt_pe, 1)

            def transpose_normalized(k, bank):
                return lambda t: transpose_x(bank, t, ln_dve[k].sem, ln_dve[k].after(f"b{t}"))

            pe.wait_ge(cst_step, CST_IDENT)
            for t in range(NT):
                transpose_x(4, t, x_in[t], 16)

            def to_channels(c, i):
                pe.wait_ge(A_act.sem, A_act.after("pre" + "AB"[c], i))
                pe.wait_ge(A_act.sem, A_act.after("tok" + "AB"[c], i - 1))
                for m in range(4):
                    for t in range(NT):
                        o = (m % 2) * SEQ + t * P
                        last = nc.tensor.transpose(ps[:, 4 + 2 * c + m // 2, o:o + P], pre[:, c, t, m * P:(m + 1) * P],
                                                   IDENT)
                last.then_inc(A_pe.sem, 1)

            def to_tokens(c, i):
                pe.wait_ge(A_act.sem, A_act.after("silu" + "AB"[c], i))
                for t in range(NT):
                    for m in range(4):
                        last = nc.tensor.transpose(ps[:, 4 + 2 * c + t, m * P:(m + 1) * P], cacc[:, c, m, t * P:(t + 1) * P],
                                                   IDENT)
                last.then_inc(A_pe.sem, 1)

            def project(i, first=False):
                pe.wait_ge(A_act.sem, A_act.after("z", i - 1))
                if first:
                    wide_first(0, 0, (0, 1), xT0h, xT0l)
                else:
                    wide(0, i, 0, (0, 1), xT0h, xT0l)
                    to_tokens(0, i - 1)
                    wide(1, i, 1, (0, 1), xT0h, xT0l)
                if first:
                    pe.wait_ge(small_in, SMALL)
                    nc.tensor.transpose(ps[:, 5, 0:P], cwr, IDENT).then_inc(S_pe.sem, 1)
                    pe.wait_ge(S_dve.sem, S_dve.after("bal"))
                    for k in range(KD):
                        last = split3(ps[0:32, 6, 0:SEQ], bah[:, k, :], bal[:, k, :], xT0h[:, k, :], xT0l[:, k, :],
                                      k == 0, k == KD - 1)
                    last.then_inc(S_pe.sem, 1)
                pe.wait_ge(A_act.sem, A_act.after("preB", i - 1))
                wide(2, i, 0, (2, 3), xT0h, xT0l)
                if not first:
                    to_tokens(1, i - 1)
                wide(3, i, 1, (2, 3), xT0h, xT0l)
                if first:
                    pe.wait_ge(S_dve.sem, S_dve.after("baT"))
                    for t in range(NT):
                        last = nc.tensor.transpose(ps[:, 7, t * 32:t * 32 + 32], baT[:, t * P:(t + 1) * P],
                                                   IDENT[0:32, 0:32])
                    last.then_inc(S_pe.sem, 1)
                to_channels(0, i)
                wide(4, i, 0, (0, 1), xT0h, xT0l)
                wide(5, i, 1, (0, 1), xT0h, xT0l)
                if first:
                    pe.wait_ge(S_dve.sem, S_dve.after("ba"))
                to_channels(1, i)

            project(0, True)
            pe.wait_ge(cst_step, CST)
            with pe.Fori(1, 4) as i:
                project(i)

            def turned(name, h0, bank):
                for h in range(2):
                    for t in range(NT):
                        o = h * SEQ + t * P
                        last = nc.tensor.transpose(ps[:, bank, o:o + P], tok[:, h0 + h, t, :], IDENT)
                last.then_inc(S_pe.sem, 1)

            pe.wait_ge(S_dve.sem, S_dve.after("g"))
            nc.tensor.matmul(ps[:, 2, 0:VH], LE, g[:, 1, :], start=True, stop=True).then_inc(S_pe.sem, 1)
            nc.tensor.matmul(ps[:, 2, VH:2 * VH], GT, g[:, 0, :], start=True, stop=True).then_inc(S_pe.sem, 1)
            pe.wait_ge(S_pool.sem, S_pool.after("kn"))
            turned("kT0", 8, 3)
            pe.wait_ge(A_act.sem, A_act.after("z", 3))
            turned("kT1", 10, 0)
            turned("kT2", 12, 1)
            to_tokens(0, 3)
            pe.wait_ge(A_act.sem, A_act.after("tokA", 3))
            turned("kT3", 14, 5)
            for q, bank in enumerate((3, 0, 1, 4)):
                if q < 3:
                    pe.wait_ge(S_dve.sem, S_dve.after(f"kT{q}"))
                turned(f"qT{q}", 2 * q, bank)
            to_tokens(1, 3)
            pe.wait_ge(A_act.sem, A_act.after("tokB", 3))
            pe.wait_ge(S_act.sem, S_act.after("kd"))
            pe.wait_ge(S_dve.sem, S_dve.after("kT3"))

            with pe.Fori(0, TURNS) as i:
                def heads(bank, lhs, rhs):
                    for h in range(HPG):
                        last = nc.tensor.matmul(ps[:, bank, h * P:(h + 1) * P], lhs(h), rhs(h), start=True, stop=True)
                    return last.then_inc(C_pe.sem, 1)

                def turned(bank, src):
                    for h in range(HPG):
                        last = nc.tensor.transpose(ps[:, bank, h * P:(h + 1) * P], src[:, h, :], IDENT)
                    last.then_inc(C_pe.sem, 1)

                pe.wait_ge(C_act.sem, C_act.after("cq", i))
                pe.wait_ge(C_dve.sem, C_dve.after("ck", i))
                pe.wait_ge(C_dve.sem, C_dve.after("o1.1", i - 1))
                pe.wait_ge(C_act.sem, C_act.after("v1s.1", i - 1))
                for c in range(LANES):
                    tt = slice(c % 2 * P, c % 2 * P + P)
                    for h in range(QPG):
                        kh = kTc[:, QPG * (c // 2) + h, tt]
                        nc.tensor.matmul(ps[:, c, h * P:(h + 1) * P], kh, kh, start=True, stop=True)
                        last = nc.tensor.matmul(ps[:, c, (2 + h) * P:(3 + h) * P], kh, qTc[:, QPG * (c // 2) + h, tt],
                                                start=True, stop=True)
                    last.then_inc(C_pe.sem, 1)
                for c in range(LANES):
                    pe.wait_ge(C_pool.sem, C_pool.after(f"G.{c}", i))
                    heads(4 + c, lambda h: Xc[c][:, h, :], lambda h: GT)
                for c in range(LANES):
                    pe.wait_ge(C_act.sem, C_act.after(f"e.{c}", i))
                    nc.tensor.matmul(ps[:, 4 + c, :], GT, flat(Xc[c]), start=True, stop=True).then_inc(C_pe.sem, 1)
                for c in range(LANES):
                    pe.wait_ge(C_pool.sem, C_pool.after(f"C1.{c}", i))
                    pe.wait_ge(C_act.sem, C_act.after(f"eT.{c}", i))
                    turned(4 + c, Cc[c])
                for b in inv:
                    for c in range(LANES):
                        pe.wait_ge(C_pool.sem, C_pool.after(f"C{b}.{c}", i))
                        if b == 2:
                            pe.wait_ge(C_dve.sem, C_dve.after(f"A1.{c}", i))
                            pe.wait_ge(C_dve.sem, C_dve.after(f"dt1.{c}", i))
                        else:
                            pe.wait_ge(C_dve.sem, C_dve.after(f"u{b // 2}.{c}", i))
                        heads(c, lambda h: Cc[c][:, h, :], lambda h: DTc[c][:, h, :])
                    for c in range(LANES):
                        pe.wait_ge(C_act.sem, C_act.after(f"x{b}.{c}", i))
                        if b == 2:
                            pe.wait_ge(C_dve.sem, C_dve.after(f"dt1.{c}", i))
                        else:
                            pe.wait_ge(C_act.sem, C_act.after(f"d{b // 2}.{c}", i))
                        heads(4 + c, lambda h: Dc[c][:, h, :], lambda h: Xc[c][:, h, :])
                    for c in range(LANES):
                        if b < 64:
                            pe.wait_ge(C_dve.sem, C_dve.after(f"u{b}.{c}", i))
                            turned(4 + c, DTc[c])
                pe.wait_ge(C_pool.sem, C_pool.after("vb", i))
                for grp in range(GROUPS):
                    c0 = 2 * grp
                    pe.wait_ge(C_dve.sem, C_dve.after(f"u64.{c0}", i))
                    heads(c0, lambda h: DTc[c0][:, h, :], lambda h: tok[:, ds(16 + 8 * i + HPG * grp + h, 1), 0, :]
                          .rearrange("p a d -> p (a d)"))
                for grp in range(GROUPS):
                    c0 = 2 * grp
                    pe.wait_ge(C_act.sem, C_act.after(f"v0s.{grp}", i))
                    pe.wait_ge(C_pool.sem, C_pool.after(f"kd.{grp}", i))
                    pe.wait_ge(C_dve.sem, C_dve.after("A.3", i))
                    heads(c0 + 1, lambda h: Dc[c0][:, h, :], lambda h: Xc[c0][:, h, :])
                    heads(c0, lambda h: ETc[c0][:, h, :], lambda h: Xc[c0][:, h, :])
                for grp in range(GROUPS):
                    c0 = 2 * grp
                    pe.wait_ge(C_dve.sem, C_dve.after(f"u64.{c0 + 1}", i))
                    pe.wait_ge(C_act.sem, C_act.after(f"Ss.{grp}", i))
                    heads(4 + c0, lambda h: kTc[:, QPG * grp + h // 2, P:SEQ], lambda h: Cc[c0][:, h, :])
                    heads(5 + c0, lambda h: qTc[:, QPG * grp + h // 2, P:SEQ], lambda h: Cc[c0][:, h, :])
                for grp in range(GROUPS):
                    c0 = 2 * grp
                    pe.wait_ge(C_dve.sem, C_dve.after(f"r.{grp}", i))
                    heads(c0 + 1, lambda h: DTc[c0 + 1][:, h, :], lambda h: Cc[c0 + 1][:, h, :])
                for grp in range(GROUPS):
                    c0 = 2 * grp
                    pe.wait_ge(C_act.sem, C_act.after(f"v1s.{grp}", i))
                    heads(c0, lambda h: ETc[c0 + 1][:, h, :], lambda h: Xc[c0 + 1][:, h, :])

            pe.wait_ge(C_dve.sem, C_dve.after("o1.1", TURNS - 1))
            for c in range(8 + 3):
                if c < 8:
                    if c < 6:
                        pe.wait_ge(O_dve.sem, O_dve.after(f"g{c}"))
                    else:
                        pe.wait_ge(O_pool.sem, O_pool.after("z"))
                    if c > 3:
                        pe.wait_ge(O_dve.sem, O_dve.after(f"l{c - 4}"))
                    for h in range(2):
                        for t in range(NT):
                            o = h * SEQ + t * P
                            last = nc.tensor.transpose(ps[:, 4 + c % 4, o:o + P], tok[:, 16 + 2 * c + h, t, :], IDENT)
                    last.then_inc(O_pe.sem, 1)
                u = c - 3
                if u >= 0:
                    pe.wait_ge(O_dve.sem, O_dve.after(f"l{u}"))
                    deep(U_OUT + u, 0, (0, 2), lambda t, k: (oTh[:, 2 * u + k, t * P:(t + 1) * P],
                                                             oTl[:, 2 * u + k, t * P:(t + 1) * P]),
                         u == 0, u == OUT_UNITS - 1, u == OUT_UNITS - 1)

            def ffn(base, turn, S, done, xh, xl, hs, hTh, hTl, g_banks, u_banks, t_banks, y_banks,
                    first_gate=None, t_free=None, before_last=None):
                tiles = range(len(g_banks))

                def chunk(j, turn, n, down):
                    pe.wait_ge(S["s"], n + 1)
                    if len(tiles) == NT and not down:
                        wide_first(j, 1, g_banks, xh, xl, transpose_normalized(0, 4))
                    else:
                        wide(j, turn, 0, g_banks, xh, xl)
                        wide(j + 1, turn, 1, g_banks, xh, xl)
                    if first_gate and not down:
                        first_gate()
                    pe.wait_ge(S["h"], n + 1)
                    if u_banks == t_banks:
                        pe.wait_ge(S["hl"], n + 1)
                    wide(j + 2, turn, 0, u_banks, xh, xl)
                    wide(j + 3, turn, 1, u_banks, xh, xl)
                    if down:
                        down_units(j + 4, turn, n)
                    pe.wait_ge(S["h"], n + 2)
                    pe.wait_ge(S["hl"], n + 1)
                    if t_free and not down:
                        t_free()
                    for t in tiles:
                        for m in range(4):
                            last = nc.tensor.transpose(ps[:, t_banks[t], m * P:(m + 1) * P], hs[:, t, m * P:(m + 1) * P],
                                                       IDENT)
                    last.then_inc(S["t"], 1)

                def down_units(j, turn, n, final=False):
                    pe.wait_ge(S["hl"], n + 1)
                    for half in range(2):
                        deep(j + half, turn, y_banks,
                             lambda t, k: (hTh[:, t, 2 * half + k, :], hTl[:, t, 2 * half + k, :]), False, False,
                             final and half == 1)

                chunk(base, turn, done, False)
                for bank in y_banks:
                    for quarter in range(4):
                        nc.tensor.matmul(ps[:, bank + quarter // 2, quarter % 2 * 256:quarter % 2 * 256 + 256],
                                         zeros[:, 0:P], zeros[:], start=True, stop=True)
                with pe.Fori(0, FC - 1) as c:
                    chunk(base + 4, turn + c, done + c + 1, True)
                if before_last:
                    before_last()
                down_units(base + 4, turn + FC - 1, done + FC, len(tiles) == NT)

            ffn(U_FFN, 0, dense, 0, xTh, xTl, hs0, hTh0, hTl0, (0, 1), (2, 3), (2, 3), (4, 6))

            wide_first(U_SBIN, 2, (4, 5), xTh, xTl, transpose_normalized(1, 0))

            def chunk(c, bank, i):
                wide(U_SBIN + 2 * c, i, 0, (bank, bank + 1), xTh, xTl)
                wide(U_SBIN + 2 * c + 1, i, 1, (bank, bank + 1), xTh, xTl)

            def to_channels(grp):
                for h in range(4):
                    for part in range(2):
                        for t in range(NT):
                            c = part * D + (4 * grp + h) * P
                            o = part * SEQ + t * P
                            last = nc.tensor.transpose(ps[:, 4 * grp + h, o:o + P], qkv[:, t, c:c + P], IDENT)
                last.then_inc(T_pe.sem, 1)

            def scores(grp):
                pe.wait_ge(T_act.sem, T_act.after(f"q{grp}"))
                pe.wait_ge(T_dve.sem, T_dve.after(f"k{grp}"))
                for h in range(4):
                    bank = 4 * grp + h
                    nc.tensor.matmul(ps[:, bank, 0:SEQ], kTs[:, grp, h, 0:P], qTs[:, grp, h, :], start=True, stop=False,
                                     skip_group_check=True)
                    last = nc.tensor.matmul(ps[:, bank, SEQ:384], kTs[:, grp, h, P:SEQ], qTs[:, grp, h, P:SEQ],
                                            start=False, stop=False, skip_group_check=True)
                last.then_inc(T_pe.sem, 1)

            chunk(1, 6, 0)
            chunk(2, 0, 0)
            pe.wait_ge(B_act.sem, B_act.after("c0", 0))
            chunk(0, 4, 1)
            pe.wait_ge(B_act.sem, B_act.after("c2", 0))
            to_channels(0)
            chunk(1, 6, 1)
            scores(0)
            pe.wait_ge(B_act.sem, B_act.after("c0", 1))
            chunk(2, 4, 1)
            pe.wait_ge(B_act.sem, B_act.after("c2", 1))
            to_channels(1)
            scores(1)
            for grp in range(2):
                pe.wait_ge(T_dve.sem, T_dve.after(f"mb{grp}"))
                for h in range(4):
                    bank = 4 * grp + h
                    nc.tensor.matmul(ps[:, bank, 0:SEQ], NGE, spl[:, grp, h, 0:SEQ], start=False, stop=False,
                                     skip_group_check=True)
                    nc.tensor.matmul(ps[:, bank, P:SEQ], NONES, spl[:, grp, h, SEQ:384], start=False, stop=False,
                                     skip_group_check=True)
                    last = nc.tensor.matmul(ps[:, bank, SEQ:384], NGE, spl[:, grp, h, SEQ:384], start=False, stop=True,
                                            skip_group_check=True)
                last.then_inc(T_pe.sem, 1)
            for grp in range(2):
                pe.wait_ge(T_dve.sem, T_dve.after(f"nb{grp}"))
                for h in range(4):
                    c = 2 * D + (4 * grp + h) * P
                    bank = 4 * grp + h
                    nc.tensor.matmul(ps[:, bank, 0:SEQ], qkv[:, 0, c:c + P], spl[:, grp, h, 0:SEQ], start=True, stop=False,
                                     skip_group_check=True)
                    last = nc.tensor.matmul(ps[:, bank, P:SEQ], qkv[:, 1, c:c + P], spl[:, grp, h, SEQ:384], start=False,
                                            stop=True, skip_group_check=True)
                last.then_inc(T_pe.sem, 1)
            for u in range(SBOUT_UNITS):
                pe.wait_ge(T_dve.sem, T_dve.after(f"ol{u // 2}"))
                deep(U_SBOUT + u, 0, (0, 2), lambda t, k: (aTh[:, 2 * u + k, t * P:(t + 1) * P],
                                                           aTl[:, 2 * u + k, t * P:(t + 1) * P]),
                     u == 0, u == SBOUT_UNITS - 1, u == SBOUT_UNITS - 1)

            for t in range(NT):
                transpose_normalized(2, 4)(t)
            pe.wait_ge(R_dve.sem, R_dve.after("rwl"))
            pe.wait_ge(xt_lo, 16)
            for k in range(KD):
                last = split3(ps[0:NE, 0, 0:SEQ], rwh[:, k, :], rwl[:, k, :], xTh[:, k, :], xTl[:, k, :], k == 0, k == KD - 1)
            last.then_inc(R_pe.sem, 1)
            pe.wait_ge(R_dve.sem, R_dve.after("lgT"))
            for t in range(NT):
                last = nc.tensor.transpose(ps[:, 1, t * NE:(t + 1) * NE], lgT[:, t * P:(t + 1) * P], IDENT[0:NE, 0:NE])
            last.then_inc(R_pe.sem, 1)
            pe.wait_ge(R_dve.sem, R_dve.after("mask"))
            mask = rt["mask"]
            nc.tensor.matmul(ps[:, 1, 0:NE], LT, mask[:, 0, :], start=True, stop=True)
            nc.tensor.matmul(ps[:, 1, NE:2 * NE], LT, mask[:, 1, :], start=True, stop=False)
            nc.tensor.matmul(ps[:, 1, NE:2 * NE], ONES, mask[:, 0, :], start=False, stop=True)
            nc.tensor.matmul(ps[:, 1, 2 * NE:3 * NE], ONES, mask[:, 0, :], start=True, stop=False)
            nc.tensor.matmul(ps[:, 1, 2 * NE:3 * NE], ONES, mask[:, 1, :], start=False, stop=True).then_inc(R_pe.sem, 1)

            def gather(r):
                pe.wait_ge(K_dve.sem, K_dve.after("s1", r))
                for part, (src, banks) in enumerate(((Xh, (5, 6)), (Xl, (7, 0)))):
                    for k in range(KD):
                        o = ps[:, banks[k // 4], (k % 4) * P:(k % 4 + 1) * P]
                        for t in range(NT):
                            last = nc.tensor.matmul(o, src[:, t, k * P:(k + 1) * P], G[:, t, :], start=t == 0,
                                                    stop=t == NT - 1)
                    last.then_inc(K_pe.sem, 1)
                for t in range(NT):
                    last = nc.tensor.transpose(ps[:, 1, t * P:(t + 1) * P], G[:, t, :].bitcast(F32), IDENT)
                last.then_inc(K_pe.sem, 1)

            pe.wait_ge(R_act.sem, R_act.after("xh"))
            pe.wait_ge(R_dve.sem, R_dve.after("cnt"))
            gather(0)

            def scatter(done):
                pe.wait_ge(yl_done, done)
                for t in range(NT):
                    for half in range(2):
                        w = slice(half * 512, half * 512 + 512)
                        o = ps[:, 4 + 2 * t + half, :]
                        nc.tensor.matmul(o, GTr[:, t * P:(t + 1) * P], Yh[:, w], start=True, stop=False)
                        last = nc.tensor.matmul(o, GTr[:, t * P:(t + 1) * P], Yl[:, w], start=False, stop=True)
                    last.then_inc(scattered, 1)

            def round_(r, first=False):
                pe.wait_ge(K_act.sem, K_act.after("hi", r))
                pe.wait_ge(K_dve.sem, K_dve.after("l0", r))

                def first_gate():
                    if not first:
                        scatter(r)
                    pe.wait_ge(K_act.sem, K_act.after("gt", r))

                def t_free():
                    pe.wait_ge(added, NT * r + 1)

                def next_rows():
                    pe.wait_ge(moe["s"], FC * (r + 1) + 1)
                    gather(r + 1)

                ffn(U_MOE, FC * r, moe, FC * r, xeh, xel, hs1, hTh1, hTl1, (0,), (1,), (4,), (2,),
                    first_gate, t_free, next_rows)

            round_(0, True)
            pe.wait_ge(R_dve.sem, R_dve.after("ni"))
            n = pe.value_load(idi[0:1, 0:1], min_val=NE, max_val=NE + MAX_OVER)
            with pe.Fori(1, n) as r:
                round_(r)
            pe.wait_ge(K_act.sem, K_act.after("hi", n))
            pe.wait_ge(K_dve.sem, K_dve.after("l7", n))
            scatter(n)

        @block.vector
        def _(dve):
            V = nc.vector
            dve.sem_inc(lo_done, CREDIT)
            dve.sem_inc(C_dve.sem, C_dve.lead)
            dve.sem_inc(added, 1)
            for S in (dense, moe):
                dve.sem_inc(S["h"], 1)
                dve.sem_inc(S["hl"], 1)

            def lo(j, turn=0, src=None):
                dve.wait_ge(hi_done, j + 6 * turn + 1)
                V.tensor_tensor(unit_lo(j), raw[:, j % RAW, :] if src is None else src, unit_hi(j).bitcast(F32),
                                ALU.subtract).then_inc(lo_done, 1)

            def transposed(k, t, th, tl, bank):
                for half in range(2):
                    dve.wait_ge(xt_hi, 4 * k + 2 * t + half + 1)
                    v = (slice(None), slice(4 * half, 4 * half + 4), slice(t * P, (t + 1) * P))
                    V.tensor_tensor(tl[v], ps[:, bank + 2 * t + half, :].rearrange("p (k s) -> p k s", s=P),
                                    th[v].bitcast(F32), ALU.subtract).then_inc(xt_lo, 1)

            def layer_norm(k, y_bank, y_unit, th=None, tl=None, bank=None):
                L, A = ln_dve[k], ln_act[k]

                def residual(t):
                    if y_bank is not None:
                        if t == 0:
                            dve.wait_ge(y_done, k + 1)
                        else:
                            dve.wait_ge(unit_used, units(y_unit))
                        V.scalar_tensor_tensor(out=X[:, t], in0=X[:, t], scalar=ALPHA,
                                               in1=ps[:, y_bank + 2 * t:y_bank + 2 * t + 2, :].rearrange("p b n -> p (b n)"),
                                               op0=ALU.mult, op1=ALU.add).then_inc(L.sem, 1)

                def statistics(t):
                    if y_bank is not None:
                        dve.wait_ge(L.sem, L.after(f"r{t}"))
                    else:
                        dve.wait_ge(added, NT * n + t)
                    for h in range(2):
                        V.bn_stats(stats[:, t, h, :], X[:, t, h * 512:(h + 1) * 512]).then_inc(L.sem, 1)
                    dve.wait_ge(L.sem, L.after(f"sb{t}"))
                    V.bn_aggr(mv[:, t, :], stats[:, t]).then_inc(L.sem, 1)

                def scaled(t):
                    dve.wait_ge(A.sem, A.after(f"sd{t}"))
                    V.reciprocal(rstd[:, t], sdev[:, t]).then_inc(L.sem, 1)
                    V.scalar_tensor_tensor(out=X[:, t], in0=X[:, t], scalar=mv[:, t, 0:1], in1=lnrow[:, 0, :],
                                           op0=ALU.subtract, op1=ALU.mult).then_inc(L.sem, 1)
                    dve.wait_ge(L.sem, L.after(f"g{t}"))
                    V.scalar_tensor_tensor(out=X[:, t], in0=X[:, t], scalar=rstd[:, t], in1=lnrow[:, 1, :],
                                           op0=ALU.mult, op1=ALU.add).then_inc(L.sem, 1)

                residual(0)
                statistics(0)
                residual(1)
                dve.wait_ge(ln_in, 32 * (k + 1))
                scaled(0)
                statistics(1)
                if th is not None:
                    transposed(k + 1, 0, th, tl, bank)
                scaled(1)
                if th is not None:
                    transposed(k + 1, 1, th, tl, bank)

            for t in range(NT):
                transposed(0, t, xT0h, xT0l, 4)

            lo(0)
            lo(1)
            dve.wait_ge(S_act.sem, S_act.after("bah"))
            V.tensor_tensor(bal[:], baw, bah[:].bitcast(F32), ALU.subtract).then_inc(S_dve.sem, 1)
            dve.wait_ge(R_act.sem, R_act.after("rwh"))
            V.tensor_tensor(rwl[:], rw[:], rwh[:].bitcast(F32), ALU.subtract).then_inc(R_dve.sem, 1)

            def convolve(c, i):
                for j in (2, 1, 0):
                    for m in range(4):
                        src = ps[:, 4 + 2 * c + m // 2, (m % 2) * SEQ:(m % 2 + 1) * SEQ]
                        w = cw[:, ds(j * 32 + i * 8 + 4 * c + m, 1)]
                        s = 3 - j
                        if s == 1:
                            dve.wait_ge(A_act.sem, A_act.after("c0" + "AB"[c], i))
                        else:
                            dve.wait_ge(A_dve.sem, A_dve.after(f"{j + 1}{m}" + "AB"[c], i))
                        V.scalar_tensor_tensor(out=cacc[:, c, m, s:], in0=src[:, 0:SEQ - s], scalar=w,
                                               in1=cacc[:, c, m, s:], op0=ALU.mult, op1=ALU.add)\
                         .then_inc(A_dve.sem, 1)

            def project(i, first=False):
                lo(2, i)
                if first:
                    dve.wait_ge(S_pe.sem, S_pe.after("cw"))
                    V.tensor_copy(cw[:], ps[:, 5, 0:P]).then_inc(S_dve.sem, 1)
                    dve.wait_ge(S_pe.sem, S_pe.after("baT"))
                    V.tensor_copy(baT, ps[0:32, 6, 0:SEQ]).then_inc(S_dve.sem, 1)
                else:
                    convolve(1, i - 1)
                for j in (3, 4, 5, 6):
                    lo(j, i)
                if first:
                    dve.wait_ge(S_pe.sem, S_pe.after("ba"))
                    V.tensor_copy(ba[:].rearrange("p t n -> p (t n)"), ps[:, 7, 0:64]).then_inc(S_dve.sem, 1)
                convolve(0, i)
                lo(7, i)

            project(0, True)
            V.tensor_tensor(xdt[:], ba[:, :, VH:2 * VH], dtb[:].unsqueeze(1).broadcast_to([P, NT, VH]), ALU.add)\
             .then_inc(S_dve.sem, 1)
            dve.wait_ge(S_act.sem, S_act.after("eb"))
            V.tensor_scalar(beta[:], beta[:], 1.0, None, ALU.add).then_inc(S_dve.sem, 1)
            dve.wait_ge(S_dve.sem, S_dve.after("b1"))
            V.reciprocal(beta[:], beta[:]).then_inc(S_dve.sem, 1)
            with dve.Fori(1, 3) as i:
                project(i)
            dve.wait_ge(S_act.sem, S_act.after("ln"))
            V.scalar_tensor_tensor(out=xdt[:], in0=xdt[:], scalar=0.0, in1=lsp[:], op0=ALU.max, op1=ALU.add)\
             .then_inc(S_dve.sem, 1)
            dve.wait_ge(S_dve.sem, S_dve.after("sp"))
            V.scalar_tensor_tensor(out=g[:], in0=xdt[:], scalar=-1.0, in1=negA[:].unsqueeze(1).broadcast_to([P, NT, VH]),
                                   op0=ALU.mult, op1=ALU.mult).then_inc(S_dve.sem, 1)
            dve.wait_ge(A_act.sem, A_act.after("tokB", 1))
            dve.wait_ge(A_pe.sem, A_pe.after("t1B", 2))
            for h in range(QK):
                for t in range(NT):
                    k = tok[:, QK + h, t, :]
                    last = V.tensor_tensor_reduce(pre[:, h // 4, t, h % 4 * P:h % 4 * P + P], k, k, 1.0, 0.0, ALU.mult,
                                                  ALU.add, ssq[:, QK + h, t:t + 1])
            last.then_inc(S_dve.sem, 1)
            dve.wait_ge(S_act.sem, S_act.after("sd"))
            V.reciprocal(rsn[:], rsn[:]).then_inc(S_dve.sem, 1)
            dve.wait_ge(S_dve.sem, S_dve.after("rs"))
            V.tensor_scalar(rsn[:, 0:QK], rsn[:, 0:QK], SCALE, None, ALU.mult).then_inc(S_dve.sem, 1)
            project(3)

            for c, bank in enumerate((3, 0, 1, 5)):
                if c == 3:
                    convolve(1, 3)
                dve.wait_ge(S_pe.sem, S_pe.after(f"kT{c}"))
                V.tensor_copy(kT[:, 2 * c:2 * c + 2, :].rearrange("p a b -> p (a b)"), ps[:, bank, :])\
                 .then_inc(S_dve.sem, 1)
            dve.wait_ge(S_act.sem, S_act.after("eg"))
            V.tensor_tensor(beg1[:], beta[:, 1, :], eg1[:], ALU.mult).then_inc(S_dve.sem, 1)

            dve.wait_ge(S_dve.sem, S_dve.after("kT3"))
            dve.wait_ge(A_act.sem, A_act.after("tokA", 3))
            with dve.Fori(0, TURNS) as i:
                dve.wait_ge(C_pe.sem, C_pe.after("PK.1", i - 1))
                V.tensor_copy(kTc[:], kT[:, ds(4 * i, 4), :]).then_inc(C_dve.sem, 1)

                def four(ap):
                    return ap.unsqueeze(1).broadcast_to([P, HPG, P])

                def pairs(ap):
                    return ap.rearrange("p (q d) -> p q d", d=P).unsqueeze(2).broadcast_to([P, QPG, 2, P])

                for c in range(LANES):
                    e4 = Ec[c].rearrange("p (q r) d -> p q r d", r=2)
                    dve.wait_ge(C_act.sem, C_act.after(f"e.{c}", i))
                    V.tensor_tensor(e4, e4, pairs(ps[:, c, 0:2 * P]), ALU.mult).then_inc(C_dve.sem, 1)
                    dve.wait_ge(C_dve.sem, C_dve.after(f"L1.{c}", i))
                    dve.wait_ge(C_pool.sem, C_pool.after(f"MB.{c}", i))
                    V.tensor_tensor(Ec[c], Ec[c], Dc[c], ALU.mult).then_inc(C_dve.sem, 1)
                for c in range(LANES):
                    t4 = ETc[c].rearrange("p (q r) d -> p q r d", r=2)
                    dve.wait_ge(C_act.sem, C_act.after(f"eT.{c}", i))
                    V.tensor_tensor(t4, t4, pairs(ps[:, c, 2 * P:4 * P]), ALU.mult).then_inc(C_dve.sem, 1)
                for c in range(LANES):
                    dve.wait_ge(C_pool.sem, C_pool.after(f"C1.{c}", i))
                    V.tensor_tensor(Dc[c], four(IDENT), Cc[c], ALU.subtract).then_inc(C_dve.sem, 1)
                    dve.wait_ge(C_pe.sem, C_pe.after(f"T1.{c}", i))
                    V.tensor_tensor(DTc[c], four(IDENT), ps[:, 4 + c, :].rearrange("p (h d) -> p h d", d=P),
                                    ALU.subtract).then_inc(C_dve.sem, 1)
                for b in inv:
                    for c in range(LANES):
                        dve.wait_ge(C_pe.sem, C_pe.after(f"U{b}.{c}", i))
                        V.tensor_tensor(flat(DTc[c]), flat(DTc[c]), ps[:, 4 + c, :], ALU.subtract).then_inc(C_dve.sem, 1)
                    if b == 2:
                        for c in range(LANES):
                            dve.wait_ge(C_dve.sem, C_dve.after(f"A1.{c}", i))
                            V.tensor_tensor(ETc[c], ETc[c], four(LE), ALU.mult).then_inc(C_dve.sem, 1)

                def o(grp, t):
                    return tok[:, ds(16 + 8 * i + HPG * grp, HPG), t, :]

                def per_head(v, grp):
                    return v[:, ds(8 * i + HPG * grp, HPG)].unsqueeze(2).broadcast_to([P, HPG, P])

                def heads(bank):
                    return ps[:, bank, :].rearrange("p (h d) -> p h d", d=P)

                for grp in range(GROUPS):
                    dve.wait_ge(C_pe.sem, C_pe.after(f"O0.{grp}", i))
                    V.tensor_copy(o(grp, 0), heads(2 * grp)).then_inc(C_dve.sem, 1)
                for grp in range(GROUPS):
                    r = Cc[2 * grp + 1]
                    dve.wait_ge(C_pe.sem, C_pe.after(f"PK.{grp}", i))
                    V.tensor_tensor(r, heads(4 + 2 * grp), per_head(beg1, grp), ALU.mult).then_inc(C_dve.sem, 1)
                for grp in range(GROUPS):
                    r = Cc[2 * grp + 1]
                    dve.wait_ge(C_dve.sem, C_dve.after(f"r1.{grp}", i))
                    V.tensor_tensor(r, o(grp, 1), r, ALU.subtract).then_inc(C_dve.sem, 1)
                for grp, scratch in enumerate((E_[:, 0], DTB[:, 0])):
                    dve.wait_ge(C_dve.sem, C_dve.after(f"o0.{grp}", i))
                    V.tensor_tensor(scratch, o(grp, 0), o(grp, 0), ALU.mult).then_inc(C_dve.sem, 1)
                for grp, scratch in enumerate((E_[:, 0], DTB[:, 0])):
                    dve.wait_ge(C_dve.sem, C_dve.after(f"sq0.{grp}", i))
                    V.tensor_reduce(ssq[:, ds(8 * i + HPG * grp, HPG), 0], scratch, AX_X, ALU.add).then_inc(C_dve.sem, 1)
                for grp in range(GROUPS):
                    dve.wait_ge(C_pe.sem, C_pe.after(f"v1.{grp}", i))
                    V.tensor_tensor(Cc[2 * grp + 1], heads(5 + 2 * grp), per_head(eg1, grp), ALU.mult)\
                     .then_inc(C_dve.sem, 1)
                for grp in range(GROUPS):
                    dve.wait_ge(C_pe.sem, C_pe.after(f"AV.{grp}", i))
                    dve.wait_ge(C_dve.sem, C_dve.after(f"o1a.{grp}", i))
                    V.tensor_tensor(o(grp, 1), Cc[2 * grp + 1], heads(2 * grp), ALU.add).then_inc(C_dve.sem, 1)

            dve.wait_ge(O_act.sem, O_act.after("sd"))
            V.reciprocal(rsn[:], rsn[:]).then_inc(O_dve.sem, 1)
            dve.wait_ge(O_dve.sem, O_dve.after("rs"))
            dve.wait_ge(C_pool.sem, C_pool.after("zn", TURNS - 1))

            def gated(c):
                for h in (2 * c, 2 * c + 1):
                    for t in range(NT):
                        v = tok[:, 16 + h, t, :]
                        last = V.scalar_tensor_tensor(out=v, in0=v, scalar=rsn[:, h, t:t + 1], in1=zs[:, t, h * P:(h + 1) * P],
                                                      op0=ALU.mult, op1=ALU.mult)
                last.then_inc(O_dve.sem, 1)

            gated(0)
            for c in range(8):
                if c + 1 < 6:
                    gated(c + 1)
                if c > 3:
                    lo(U_OUT + c - 2)
                dve.wait_ge(O_act.sem, O_act.after(f"h{c}"))
                v = slice(2 * c, 2 * c + 2)
                V.tensor_tensor(oTl[:, v, :].rearrange("p a b -> p (a b)"), ps[:, 4 + c % 4, :],
                                oTh[:, v, :].rearrange("p a b -> p (a b)").bitcast(F32), ALU.subtract).then_inc(O_dve.sem, 1)
            for u in range(6, OUT_UNITS + 2):
                lo(U_OUT + u)
            layer_norm(0, 0, U_OUT + OUT_UNITS - 1, xTh, xTl, 4)

            def ffn(base, turn, S, done, tiles, u_bank, t_bank, hs, hTh, hTl, first_gate=None, present=False):
                def hidden(n, up):
                    dve.wait_ge(unit_used, up)
                    dve.wait_ge(S["s"], n + 2)
                    V.tensor_tensor(hs[:], hs[:], ps[:, u_bank:u_bank + tiles, :], ALU.mult).then_inc(S["h"], 1)

                def hidden_lo(n):
                    dve.wait_ge(S["hh"], n + 2)
                    V.tensor_tensor(hTl[:].rearrange("p t m d -> p t (m d)"), ps[:, t_bank:t_bank + tiles, :],
                                    hTh[:].rearrange("p t m d -> p t (m d)").bitcast(F32), ALU.subtract).then_inc(S["hl"], 1)

                lo(base + 2, turn)
                lo(base + 3, turn)
                if first_gate:
                    first_gate()
                hidden(done, units(base + 3, turn))
                lo(base + 4, turn)
                lo(base + 5, turn)
                hidden_lo(done)

                def chunk(c, src):
                    for k in range(6):
                        lo(base + 6 + k, turn + c, src[k])
                        if k == 3:
                            hidden(done + c + 1, units(base + 7, turn + c))
                    hidden_lo(done + c + 1)

                with dve.Fori(0, FC - 1 - present) as c:
                    chunk(c, [None] * 6)
                if present:
                    chunk(FC - 2, early_sources)
                return turn + FC - 1

            end = ffn(U_FFN, 0, dense, 0, NT, 2, 2, hs0, hTh0, hTl0)
            lo(U_FFN + 6, end)
            lo(U_FFN + 7, end)
            layer_norm(1, 4, U_FFN + FFN_UNITS - 1, xTh, xTl, 0)

            for_diag = LT.unsqueeze(1).broadcast_to([P, 4, P])

            def keys(grp):
                dve.wait_ge(T_pe.sem, T_pe.after(f"qk{grp}"))
                dve.wait_ge(T_act.sem, T_act.after(f"q{grp}"))
                V.tensor_copy(kTs[:, grp], ps[:, 4 * grp:4 * grp + 4, SEQ:2 * SEQ]).then_inc(T_dve.sem, 1)

            def masked(grp):
                for w in (slice(0, P), slice(SEQ, 384)):
                    V.tensor_tensor(spl[:, grp, :, w], spl[:, grp, :, w], for_diag, ALU.mult).then_inc(T_dve.sem, 1)

            def softplus(grp):
                dve.wait_ge(T_act.sem, T_act.after(f"l{grp}"))
                V.scalar_tensor_tensor(out=spl[:, grp], in0=ps[:, 4 * grp:4 * grp + 4, 0:384], scalar=0.0, in1=spl[:, grp],
                                       op0=ALU.max, op1=ALU.add).then_inc(T_dve.sem, 1)
                dve.wait_ge(T_dve.sem, T_dve.after(f"sp{grp}"))
                masked(grp)

            def exponent(grp):
                dve.wait_ge(T_pe.sem, T_pe.after(f"R{grp}"))
                V.tensor_scalar(spl[:, grp], ps[:, 4 * grp:4 * grp + 4, 0:384], 0.0, None, ALU.min).then_inc(T_dve.sem, 1)

            def weights(grp):
                dve.wait_ge(T_act.sem, T_act.after(f"p{grp}"))
                masked(grp)

            for j in range(2, 10):
                lo(U_SBIN + j)
            keys(0)
            for j in range(10, 14):
                lo(U_SBIN + j)
            keys(1)
            softplus(0)
            exponent(0)
            softplus(1)
            weights(0)
            exponent(1)
            weights(1)
            for grp in range(2):
                dve.wait_ge(T_act.sem, T_act.after(f"oh{grp}"))
                V.tensor_tensor(aTl[:, 4 * grp:4 * grp + 4, :], ps[:, 4 * grp:4 * grp + 4, 0:SEQ],
                                aTh[:, 4 * grp:4 * grp + 4, :].bitcast(F32), ALU.subtract).then_inc(T_dve.sem, 1)
            for u in range(SBOUT_UNITS):
                lo(U_SBOUT + 2 + u)
            layer_norm(2, 0, U_SBOUT + SBOUT_UNITS - 1, xTh, xTl, 4)

            def step(name, ins):
                ins.then_inc(R_dve.sem, 1)
                dve.wait_ge(R_dve.sem, R_dve.after(name))

            def experts(v):
                return v.broadcast_to([P, NT, NE])

            def select(r):
                for t in range(NT):
                    V.tensor_scalar(G[:, t, :], iota[:], ranks[:, t, ds(r, 1)], None, ALU.is_equal).then_inc(K_dve.sem, 1)

            def gathered(r):
                dve.wait_ge(K_pe.sem, K_pe.after("lo", r))
                for k, bank in ((0, 7), (4, 0)):
                    V.tensor_copy(xel[:, k:k + 4, :].rearrange("p k s -> p (k s)"), ps[:, bank, :]).then_inc(K_dve.sem, 1)

            dve.wait_ge(R_act.sem, R_act.after("xh"))
            step("xl", V.tensor_tensor(Xl[:], X[:], Xh[:].bitcast(F32), ALU.subtract))
            dve.wait_ge(xt_pe, 16)
            step("xa", V.tensor_scalar(X[:], X[:], ALPHA, None, ALU.mult))
            step("z0", V.memset(ranks[:], -1.0))
            step("z1", V.memset(gates[:], 0.0))
            step("z2", V.memset(ovp[:, 0:1], 0.0))
            dve.wait_ge(R_pe.sem, R_pe.after("lgT"))
            step("lgT", V.tensor_copy(lgT, ps[0:NE, 0, 0:SEQ]))

            idx = iota[:, 0:NE].unsqueeze(1).broadcast_to([P, NT, NE])
            dve.wait_ge(R_pe.sem, R_pe.after("lg"))
            step("lg", V.tensor_copy(rt["lg"][:].rearrange("p t e -> p (t e)"), ps[:, 1, 0:NT * NE]))
            for lg, m, eq, ca, i_, oh, rest in (("lg", "m1", "eq1", "ca", "i1", "oh1", "l2"),
                                                ("l2", "m2", "eq2", "c2", "i2", "oh2", None)):
                step(m, V.tensor_reduce(rs[m][:], rt[lg][:], AX_X, ALU.max))
                step(eq, V.tensor_tensor(rt[eq][:], rt[lg][:], experts(rs[m][:]), ALU.is_ge))
                step(ca, V.scalar_tensor_tensor(out=rt[ca][:], in0=rt[eq][:], scalar=-99.0, in1=idx, op0=ALU.mult,
                                                op1=ALU.add))
                step(i_, V.tensor_reduce(rs[i_][:], rt[ca][:], AX_X, ALU.min))
                step(oh, V.tensor_tensor(rt[oh][:], rt[ca][:], experts(rs[i_][:]), ALU.is_equal))
                if rest:
                    step(rest, V.scalar_tensor_tensor(out=rt[rest][:], in0=rt[oh][:], scalar=-3.0e38, in1=rt[lg][:],
                                                      op0=ALU.mult, op1=ALU.add))
            step("mask", V.tensor_tensor(rt["mask"][:], rt["oh1"][:], rt["oh2"][:], ALU.add))
            step("df", V.tensor_tensor(rs["df"][:], rs["m2"][:], rs["m1"][:], ALU.subtract))
            dve.wait_ge(R_act.sem, R_act.after("ex"))
            step("sm", V.tensor_scalar(rs["sm"][:], rs["ex"][:], 1.0, None, ALU.add))
            step("p1", V.reciprocal(rs["p1"][:], rs["sm"][:]))
            step("p2", V.tensor_tensor(rs["p2"][:], rs["ex"][:], rs["p1"][:], ALU.mult))
            comb = gates[:, :, 0:NE]
            step("cm1", V.tensor_tensor(comb, rt["oh1"][:], experts(rs["p1"][:]), ALU.mult))
            step("cm2", V.tensor_tensor(rt["tmp"][:], rt["oh2"][:], experts(rs["p2"][:]), ALU.mult))
            step("comb", V.tensor_tensor(comb, comb, rt["tmp"][:], ALU.add))
            dve.wait_ge(R_pe.sem, R_pe.after("rk"))
            step("rk1", V.scalar_tensor_tensor(out=rt["rank"][:].rearrange("p t e -> p (t e)"), in0=ps[:, 1, 0:NT * NE],
                                               scalar=1.0, in1=rt["mask"][:].rearrange("p t e -> p (t e)"), op0=ALU.add,
                                               op1=ALU.mult))
            rank = ranks[:, :, 0:NE]
            step("rk2", V.tensor_scalar(rank, rt["rank"][:], -1.0, None, ALU.add))
            step("cnt", V.tensor_copy(cnt[:], ps[:, 1, NT * NE:(NT + 1) * NE]))
            select(0)
            step("ov", V.tensor_scalar(ov[:], cnt[:], float(P), None, ALU.is_gt))
            for e in range(1, NE):
                step(f"pre{e}", V.tensor_tensor(ovp[:, e:e + 1], ovp[:, e - 1:e], ov[:, e - 1:e], ALU.add))

            def by_extra(v):
                return v.unsqueeze(1).broadcast_to([P, MAX_OVER, NE])

            step("in", V.tensor_tensor(ind[:], by_extra(ovp[:]), iota[:, 0:MAX_OVER].unsqueeze(2)
                                       .broadcast_to([P, MAX_OVER, NE]), ALU.is_equal))
            step("im", V.tensor_tensor(ind[:], ind[:], by_extra(ov[:]), ALU.mult))
            every = (P, NT, MAX_OVER, NE)
            ind4 = ind[:].unsqueeze(1).broadcast_to(every)
            rq = ranks[:, :, NE:NE + MAX_OVER]
            step("pr", V.tensor_tensor(over[:], rank.unsqueeze(2).broadcast_to(every), ind4, ALU.mult))
            step("sr", V.tensor_reduce(rq, over[:], AX_X, ALU.add))
            step("ad", V.tensor_scalar(rq, rq, -float(P), None, ALU.add))
            step("pg", V.tensor_tensor(over[:], comb.unsqueeze(2).broadcast_to(every), ind4, ALU.mult))
            step("sg", V.tensor_reduce(gates[:, :, NE:NE + MAX_OVER], over[:], AX_X, ALU.add))
            step("pi", V.tensor_tensor(ind[:], ind[:], by_extra(iota[:, 0:NE]), ALU.mult))
            step("si", V.tensor_reduce(ids[:, 1:1 + MAX_OVER], ind[:], AX_X, ALU.add))
            step("no", V.tensor_reduce(ids[:, 0:1], ov[:], AX_X, ALU.add))
            step("nc", V.tensor_scalar(ids[:, 0:1], ids[:, 0:1], float(NE), None, ALU.add))
            step("ni", V.tensor_copy(idi[:], ids[:]))

            def add(r, done):
                for t in range(NT):
                    dve.wait_ge(scattered, NT * done + t + 1)
                    V.scalar_tensor_tensor(out=X[:, t], in0=ps[:, 4 + 2 * t:6 + 2 * t, :].rearrange("p b n -> p (b n)"),
                                           scalar=gates[:, t, ds(r, 1)], in1=X[:, t], op0=ALU.mult, op1=ALU.add)\
                     .then_inc(added, 1)

            def round_(r, first=False):
                dve.wait_ge(K_pe.sem, K_pe.after("tr", r))
                select(r + 1)
                end = ffn(U_MOE, FC * r, moe, FC * r, 1, 1, 4, hs1, hTh1, hTl1, None if first else lambda: add(r - 1, r),
                          first)
                gathered(r + 1)
                lo(U_MOE + 6, end)
                dve.wait_ge(yh_done, r + 1)
                V.tensor_tensor(Yl[:], ps[:, 2:4, :].rearrange("p b n -> p (b n)"), Yh[:].bitcast(F32), ALU.subtract)\
                 .then_inc(yl_done, 1)
                lo(U_MOE + 7, end)

            gathered(0)
            round_(0, True)
            n = dve.value_load(idi[0:1, 0:1], min_val=NE, max_val=NE + MAX_OVER)
            with dve.Fori(1, n) as r:
                round_(r)
            add(n - 1, n)
            layer_norm(3, None, None)


_INS = ["x", "gdn_w_in", "gdn_conv_w", "gdn_a_log", "gdn_dt_bias", "gdn_norm_w", "gdn_w_out", "sb_w_in", "sb_w_out",
        "ffn_w_gate", "ffn_w_up", "ffn_w_down", "moe_router", "moe_w_gate", "moe_w_up", "moe_w_down", "ln_g", "ln_b"]


def kernel(**inputs):
    import numpy as np
    import concourse.bacc as bacc
    from concourse.bass_utils import run_bass_kernel_spmd

    nc = bacc.Bacc("TRN2", target_bir_lowering=False, num_devices=1)
    arrays, args = {}, []
    for name in _INS:
        a = np.ascontiguousarray(inputs[name])
        arrays[f"in_{name}"] = a
        args.append(nc.dram_tensor(f"in_{name}", a.shape, mybir.dt.from_np(a.dtype), kind="ExternalInput").ap())
    args.append(nc.dram_tensor("out_0", (1, SEQ, D), F32, kind="ExternalOutput").ap())
    hybrid_trunk(nc, *args)
    r = run_bass_kernel_spmd(nc, [arrays], core_ids=[0])
    return r.results[0]["out_0"]
```
